# Optimizing a Trainium2 kernel written in Bass

```python
import math
import jax, jax.numpy as jnp
from jax import lax
import numpy as np

D_MODEL = 2048
BATCH = 1
SEQ = 512
DEPTH = 1

A_HEADS = 8
A_HEAD_DIM = 64
A_V_DIM = 2 * A_HEAD_DIM
A_WIDTH = A_HEADS * A_V_DIM
B_HEADS = 8
B_Q_LORA = 512
B_KV_LORA = 512
B_NOPE = 128
B_ROPE = 64
B_V_DIM = 128
B_WIDTH = B_HEADS * B_V_DIM
N_BRANCH = 2

ROPE_THETA = 10000.0
NORM_EPS = 1e-6
SUBLN_EPS = 1e-5
Q_BLOCK = 128

A_Q_COLS = A_HEADS * 2 * A_HEAD_DIM
A_K_COLS = A_HEADS * 2 * A_HEAD_DIM
A_V_COLS = A_WIDTH
A_G_COLS = A_WIDTH
B_CQ_COLS = B_Q_LORA
B_CKV_COLS = B_KV_LORA
B_KR_COLS = B_ROPE
B_G_COLS = B_WIDTH
MERGE_COLS = N_BRANCH * D_MODEL
_SIZES = [A_Q_COLS, A_K_COLS, A_V_COLS, A_G_COLS, B_CQ_COLS, B_CKV_COLS, B_KR_COLS, B_G_COLS, MERGE_COLS]
IN_COLS = sum(_SIZES)
SPLIT_POINTS = [int(v) for v in np.cumsum(_SIZES)[:-1]]

kernel_name = "hybrid_diffattn_mla_gated_encoder"

def _rmsnorm(x, g, eps=NORM_EPS):
    xf = x.astype(jnp.float32)
    y = xf * lax.rsqrt(jnp.mean(xf * xf, axis=-1, keepdims=True) + eps)
    return y.astype(x.dtype) * g

def _lambda_init(layer_idx):
    return 0.8 - 0.6 * math.exp(-0.3 * layer_idx)

def _alibi_slopes(n_heads):
    return jnp.asarray([2.0 ** (-8.0 * (h + 1) / n_heads) for h in range(n_heads)], dtype=jnp.float32)

def _rope_cos_sin(pos):
    half = B_ROPE // 2
    inv = ROPE_THETA ** (-jnp.arange(half, dtype=jnp.float32) / half)
    ang = pos.astype(jnp.float32)[..., None] * inv
    return jnp.cos(ang), jnp.sin(ang)

def _apply_rope(t, cos, sin):
    half = t.shape[-1] // 2
    t1 = t[..., :half].astype(jnp.float32)
    t2 = t[..., half:].astype(jnp.float32)
    out = jnp.concatenate([t1 * cos - t2 * sin, t1 * sin + t2 * cos], axis=-1)
    return out.astype(t.dtype)

def _to_blocks(t):
    b, s = t.shape[0], t.shape[1]
    nb = s // Q_BLOCK
    return t.reshape(b, nb, Q_BLOCK, *t.shape[2:]).swapaxes(0, 1)

def _from_blocks(t):
    nb, b = t.shape[0], t.shape[1]
    return t.swapaxes(0, 1).reshape(b, nb * Q_BLOCK, *t.shape[3:])

def _diff_attention(q1, q2, k1, k2, v, pos_f, lam, slopes):
    scale = A_HEAD_DIM ** -0.5

    def one_block(args):
        qb1, qb2, pb = args
        dist = jnp.abs(pb[:, :, None] - pos_f[:, None, :])
        bias = -slopes[None, :, None, None] * dist[:, None]
        s1 = jnp.einsum('bqhd,bkhd->bhqk', qb1, k1).astype(jnp.float32) * scale + bias
        s2 = jnp.einsum('bqhd,bkhd->bhqk', qb2, k2).astype(jnp.float32) * scale + bias
        p = jax.nn.softmax(s1, axis=-1) - lam * jax.nn.softmax(s2, axis=-1)
        return jnp.einsum('bhqk,bkhe->bqhe', p.astype(v.dtype), v)

    out = lax.map(one_block, (_to_blocks(q1), _to_blocks(q2), _to_blocks(pos_f)))
    return _from_blocks(out)

def _mla_attention(q_nope, q_rope, k_nope, k_rope, v):
    scale = (B_NOPE + B_ROPE) ** -0.5

    def one_block(args):
        qn, qr = args
        s = (jnp.einsum('bqhd,bkhd->bhqk', qn, k_nope)
             + jnp.einsum('bqhr,bkr->bhqk', qr, k_rope)).astype(jnp.float32) * scale
        p = jax.nn.softmax(s, axis=-1)
        return jnp.einsum('bhqk,bkhe->bqhe', p.astype(v.dtype), v)

    out = lax.map(one_block, (_to_blocks(q_nope), _to_blocks(q_rope)))
    return _from_blocks(out)

def setup_inputs(seed: int = 0) -> dict:
    key = jax.random.key(seed)
    ks = jax.random.split(key, 20)
    f32 = jnp.float32
    nrm = lambda k, shape, fan_in: jax.random.normal(k, shape, f32) * (fan_in ** -0.5)
    gain = lambda k, shape: 1.0 + 0.02 * jax.random.normal(k, shape, f32)
    x = jax.random.normal(ks[0], (BATCH, SEQ, D_MODEL), f32)
    offsets = jax.random.randint(ks[1], (BATCH, 1), 0, 1024, dtype=jnp.int32)
    positions = (jnp.arange(SEQ, dtype=jnp.int32)[None, :] + offsets).astype(jnp.int32)
    return {
        "x": x,
        "positions": positions,
        "norm_g": gain(ks[2], (DEPTH, D_MODEL)),
        "w_in": nrm(ks[3], (DEPTH, D_MODEL, IN_COLS), D_MODEL),
        "lam_q1": 0.1 * jax.random.normal(ks[4], (DEPTH, A_HEAD_DIM), f32),
        "lam_k1": 0.1 * jax.random.normal(ks[5], (DEPTH, A_HEAD_DIM), f32),
        "lam_q2": 0.1 * jax.random.normal(ks[6], (DEPTH, A_HEAD_DIM), f32),
        "lam_k2": 0.1 * jax.random.normal(ks[7], (DEPTH, A_HEAD_DIM), f32),
        "a_subln_g": gain(ks[8], (DEPTH, A_V_DIM)),
        "w_oa": nrm(ks[9], (DEPTH, A_WIDTH, D_MODEL), A_WIDTH),
        "q_norm_g": gain(ks[10], (DEPTH, B_Q_LORA)),
        "w_uq": nrm(ks[11], (DEPTH, B_Q_LORA, B_HEADS * (B_NOPE + B_ROPE)), B_Q_LORA),
        "kv_norm_g": gain(ks[12], (DEPTH, B_KV_LORA)),
        "w_ukv": nrm(ks[13], (DEPTH, B_KV_LORA, B_HEADS * (B_NOPE + B_V_DIM)), B_KV_LORA),
        "w_ob": nrm(ks[14], (DEPTH, B_WIDTH, D_MODEL), B_WIDTH),
        "w_out": nrm(ks[15], (DEPTH, D_MODEL, D_MODEL), D_MODEL),
        "final_g": gain(ks[16], (D_MODEL,)),
    }

def reference(x, positions, norm_g, w_in, lam_q1, lam_k1, lam_q2, lam_k2, a_subln_g, w_oa,
              q_norm_g, w_uq, kv_norm_g, w_ukv, w_ob, w_out, final_g):
    b, s, _ = x.shape
    pos_f = positions.astype(jnp.float32)
    slopes = _alibi_slopes(A_HEADS)
    cos, sin = _rope_cos_sin(positions)
    for layer in range(DEPTH):
        lam_init = _lambda_init(layer)
        h = _rmsnorm(x, norm_g[layer])
        proj = h @ w_in[layer]
        aq, ak, av, ag, cq, ckv, kr, bg, mg = jnp.split(proj, SPLIT_POINTS, axis=-1)

        aq = aq.reshape(b, s, A_HEADS, 2, A_HEAD_DIM)
        ak = ak.reshape(b, s, A_HEADS, 2, A_HEAD_DIM)
        av = av.reshape(b, s, A_HEADS, A_V_DIM)
        lam = (jnp.exp(jnp.sum(lam_q1[layer].astype(jnp.float32) * lam_k1[layer].astype(jnp.float32)))
               - jnp.exp(jnp.sum(lam_q2[layer].astype(jnp.float32) * lam_k2[layer].astype(jnp.float32)))
               + lam_init)
        oa = _diff_attention(aq[..., 0, :], aq[..., 1, :], ak[..., 0, :], ak[..., 1, :], av,
                             pos_f, lam, slopes)
        oa = _rmsnorm(oa, a_subln_g[layer], SUBLN_EPS) * (1.0 - lam_init)
        ya = (oa.reshape(b, s, A_WIDTH) * jax.nn.silu(ag)) @ w_oa[layer]

        q = (_rmsnorm(cq, q_norm_g[layer]) @ w_uq[layer]).reshape(b, s, B_HEADS, B_NOPE + B_ROPE)
        kv = (_rmsnorm(ckv, kv_norm_g[layer]) @ w_ukv[layer]).reshape(b, s, B_HEADS, B_NOPE + B_V_DIM)
        q_nope, q_rope = q[..., :B_NOPE], q[..., B_NOPE:]
        k_nope, vb = kv[..., :B_NOPE], kv[..., B_NOPE:]
        q_rope = _apply_rope(q_rope, cos[:, :, None, :], sin[:, :, None, :])
        k_rope = _apply_rope(kr, cos, sin)
        ob = _mla_attention(q_nope, q_rope, k_nope, k_rope, vb)
        yb = (ob.reshape(b, s, B_WIDTH) * jax.nn.silu(bg)) @ w_ob[layer]

        ga, gb = jnp.split(mg, 2, axis=-1)
        merged = jax.nn.sigmoid(ga) * ya + jax.nn.sigmoid(gb) * yb
        x = x + merged @ w_out[layer]
    return _rmsnorm(x, final_g)


_drawn_inputs = setup_inputs


def setup_inputs(seed=0):
    import zlib

    import numpy as np

    out = dict(_drawn_inputs(seed))
    spreads = {}
    factors = {'norm_g': 5.261,
     'lam_k1': 6.959,
     'lam_q2': 7.335,
     'lam_k2': 2.81,
     'a_subln_g': 8.0,
     'q_norm_g': 8.0,
     'kv_norm_g': 8.0,
     'final_g': 2.904}
    for name, (base, spread) in spreads.items():
        noise = np.random.default_rng([zlib.crc32(name.encode()), seed]).standard_normal(out[name].shape)
        drawn = base * np.exp(spread * noise) if base else spread * noise
        out[name] = __import__('jax').numpy.asarray(drawn.astype(out[name].dtype))
    for name, factor in factors.items():
        out[name] = (out[name] * factor).astype(out[name].dtype)
    return out
```

```python
import math
from contextlib import ExitStack

import concourse.bass as bass
from concourse import mybir

F32 = mybir.dt.float32
F32R = mybir.dt.float32r
I32 = mybir.dt.int32
ALU = mybir.AluOpType
ACT = mybir.ActivationFunctionType
AX_X = mybir.AxisListType.X

P = 128
SEQ, D_MODEL = 512, 2048
TOK = SEQ // P
KT = D_MODEL // P
HEADS = 8
A_DIM, B_NOPE, B_ROPE = 64, 128, 64
LORA = 512
LT = LORA // P
AQ, AK, AV, AG = 0, 1024, 2048, 3072
CQ, CKV, KR, BG, MG = 4096, 4608, 5120, 5184, 6208
A_SCALE = A_DIM ** -0.5
B_SCALE = (B_NOPE + B_ROPE) ** -0.5
LAM_INIT = 0.8 - 0.6 * math.exp(-0.3 * 0)
SLOPE0, SLOPE_RATIO = 2.0 ** (-8.0 / HEADS), 2.0 ** (-8.0 / HEADS)
NORM_EPS, SUBLN_EPS = 1e-6, 1e-5

SLOTS = 4
AHEAD = 2
A_STEPS, C_STEPS, B_STEPS, M_STEPS, F_STEPS = 8, 20, 4, 12, 8
C0 = HEADS * A_STEPS
B0 = C0 + C_STEPS
M0 = B0 + B_STEPS * HEADS - 2
FIN0 = M0 + M_STEPS * (KT // 2)
N_CHUNK = D_MODEL // SEQ
PIECES = FIN0 + F_STEPS * N_CHUNK

GATED_AT = [(0, 1, 2), (3, 4, 5), (6, 7, 8, 9), (12,), (10, 11, 13, 14, 15), ()] + [()] * (M_STEPS - 6)

TWO_PI_1 = 6.28125
TWO_PI_2 = 1.93500518798828125e-3
TWO_PI_3 = 2 * math.pi - TWO_PI_1 - TWO_PI_2
GATED_ORDER = [head for step in GATED_AT for head in step]
ROUND_1 = 1.5 * 2.0 ** 23
ROUND_2048 = 1.5 * 2.0 ** 34
PI_DOWN = 3.1415925


class Piece:

    def __init__(self, first, loop=0, stride=0):
        self.first = first
        self.slot = first % SLOTS
        self.n = loop * stride + first
        self.turn = loop * (stride // SLOTS) + first // SLOTS

    def after(self, k):
        return self.n + (k + 1)


def hybrid_encoder(nc, x, positions, norm_g, w_in, lam_q1, lam_k1, lam_q2, lam_k2, a_subln_g, w_oa,
                   q_norm_g, w_uq, kv_norm_g, w_ukv, w_ob, w_out, final_g, consts, out):
    ctx = ExitStack()
    with ctx:
        base = (nc.sbuf_base + 63) // 64 * 64
        KB = 1024

        def at(name, kb, shape, dt=F32):
            return nc.alloc_sbuf_tensor_at(name, shape, dt, offset=base + int(kb * KB))

        def sem(name):
            return ctx.enter_context(nc.semaphore(name))

        h_hi = at("h_hi", 0, [P, KT, SEQ], F32R)
        h_lo = at("h_lo", 32, [P, KT, SEQ], F32R)
        mg_hi = at("mg_hi", 0, [P, KT, SEQ], F32R)
        mg_lo = at("mg_lo", 32, [P, KT, SEQ], F32R)
        w_raw = at("w_raw", 64, [P, SLOTS, 1024])
        w_lo = at("w_lo", 64, [P, SLOTS, 1024], F32R)
        w_hi = at("w_hi", 80, [P, SLOTS, 1024], F32R)
        gated = at("gated", 96, [P, 2 * HEADS * SEQ])
        merged = at("merged", 96, [P, KT * SEQ])
        c_raw = at("c_raw", 112, [P, 2 * LT, SEQ])
        dist = at("dist", 120, [P, TOK, SEQ])
        x_tok = at("x_tok", 128, [P, TOK, D_MODEL])
        c_hi = at("c_hi", 128, [P, 2 * LT, SEQ], F32R)
        c_lo = at("c_lo", 144, [P, 2 * LT, SEQ], F32R)
        ga_hi = at("ga_hi", 128, [P, HEADS, SEQ], F32R)
        ga_lo = at("ga_lo", 144, [P, HEADS, SEQ], F32R)
        gb_hl = at("gb_hl", 160, [P, HEADS, 2, SEQ], F32R)
        square_junk = at("square_junk", 160, [P, D_MODEL])
        fg = at("fg", 160, [P, D_MODEL])
        q_hl = at("q_hl", 160, [P, 2, SEQ], F32R)
        c_sq = at("c_sq", 160, [P, SEQ])
        k_hl = at("k_hl", 164, [P, 2, SEQ], F32R)
        vT = at("vT", 168, [P, SEQ])
        v_hl = at("v_hl", 170, [P, 2, TOK, P], F32R)
        e = at("e", 174, [P, 2, 2, SEQ])
        e_b = at("e_b", 174, [P, 2, SEQ])
        rope_in = at("rope_in", 178, [P, SEQ])
        rope_sw = at("rope_sw", 180, [P, SEQ])
        pt = at("pt", 182, [P, 2, TOK, 2 * P], F32R)
        oT = at("oT", 190, [P, SEQ])
        eg = at("eg", 192, [P, SEQ])
        cos_t = at("cos_t", 194, [P, SEQ])
        sin_t = at("sin_t", 196, [P, SEQ])
        kr_hi = at("kr_hi", 198, [P, SEQ], F32R)
        kr_lo = at("kr_lo", 200, [P, SEQ], F32R)
        qr_hl = at("qr_hl", 202, [P, SEQ], F32R)
        sig = at("sig", 192, [P, 2, 2, SEQ])
        part = at("part", 200, [P, 2, SEQ])
        cst = at("cst", 204, [P, 2 * P + 1])
        small = at("small", 205.25, [P, 160])
        pos_i = at("pos_i", 182, [P, SEQ], I32)
        pos_f = at("pos_f", 184, [P, SEQ])
        lam_in = at("lam_in", 186, [P, 6, A_DIM])
        assert base + 207 * KB <= nc.sbuf_usable_end

        ident, swap = cst[:, 0:P], cst[:, P:2 * P]
        inv_freq = cst[:, 2 * P:2 * P + 1]
        g_in = small[:, 0:KT]
        g_q, g_kv = small[:, 16:20], small[:, 20:24]
        g_sub = small[:, 24:25]
        lam = small[:, 25:26]
        ones = small[:, 26:27]
        mhalf = small[:, 27:31]
        pos_q = small[:, 31:35]
        x_ss, x_var, x_rstd = small[:, 35:39], small[:, 39:43], small[:, 43:47]
        mx, nm = small[:, 47:55], small[:, 55:63]
        sums, rs = small[:, 63:71], small[:, 71:79]
        o_var, o_rstd = small[:, 79:83], small[:, 83:87]
        c_ss, c_var, c_rstd = small[:, 87:91], small[:, 91:95], small[:, 95:99]
        f_ss = small[:, 99:115]
        f_sum, f_var, f_rstd = small[:, 115:119], small[:, 119:123], small[:, 123:127]
        lam_s, lam_e = small[:, 127:129], small[:, 129:131]
        half_pi = small[:, 131:132]
        g_sub_raw = small[:, 132:133]
        rs_lam = small[:, 133:135]
        pos_qi = at("pos_qi", 187.75, [P, TOK], I32)

        bank = [ctx.enter_context(nc.psum_tensor(f"bank{i}", [P, SEQ], F32)) for i in range(8)]
        ACC = bank[0:2]
        SC = bank[2:6]
        TR = bank[6]
        OB = bank[7]

        landed = [sem(f"landed{i}") for i in range(SLOTS)]
        hi_ready = sem("hi_ready")
        lo_ready = sem("lo_ready")
        used = sem("used")
        small_in, x_in = sem("small_in"), [sem(f"x_in{t}") for t in range(TOK)]
        pos_in, cst_in = sem("pos_in"), sem("cst_in")
        ones_set = sem("ones_set")
        v_chain = sem("v_chain")
        a_chain = sem("a_chain")
        lam_sum, lam_exp = sem("lam_sum"), sem("lam_exp")
        angle_ready, trig_ready = sem("angle_ready"), sem("trig_ready")
        x_ss_ready, x_var_ready, x_rstd_ready, x_normed = (
            sem("x_ss_ready"), sem("x_var_ready"), sem("x_rstd_ready"), sem("x_normed"))
        x_turned, h_hi_ready, h_lo_ready = sem("x_turned"), sem("h_hi_ready"), sem("h_lo_ready")
        dist_ready, dist_halved = sem("dist_ready"), sem("dist_halved")
        proj_hi = sem("proj_hi")
        acc_read = sem("acc_read")
        gate_exp, silu_add, silu_inv, silu_done = sem("gate_exp"), sem("silu_add"), sem("silu_inv"), sem("silu_done")
        v_turned, v_hi_ready, v_lo_ready = sem("v_turned"), sem("v_hi_ready"), sem("v_lo_ready")
        scored = sem("scored")
        max_taken = sem("max_taken")
        bias_ready = sem("bias_ready")
        exp_done = sem("exp_done")
        inv_ready, inv_lam_ready, e2_scaled, p_ready = (
            sem("inv_ready"), sem("inv_lam_ready"), sem("e2_scaled"), sem("p_ready"))
        p_turned, pt_hi_ready, pt_lo_ready = sem("p_turned"), sem("pt_hi_ready"), sem("pt_lo_ready")
        pv_done = sem("pv_done")
        o_squared, o_copied, o_summed, o_var_ready, o_rstd_ready, o_spread, o_normed, head_gated = (
            sem("o_squared"), sem("o_copied"), sem("o_summed"), sem("o_var_ready"), sem("o_rstd_ready"),
            sem("o_spread"), sem("o_normed"), sem("head_gated"))
        c_squared, c_summed, c_ss_ready, c_var_ready, c_rstd_ready, c_spread, c_scaled, c_hi_ready, c_lo_ready = (
            sem("c_squared"), sem("c_summed"), sem("c_ss_ready"), sem("c_var_ready"), sem("c_rstd_ready"),
            sem("c_spread"), sem("c_scaled"), sem("c_hi_ready"), sem("c_lo_ready"))
        rope_copied, rope_swapped, rope_cos, rope_sin, rope_done, rope_hi, rope_lo = (
            sem("rope_copied"), sem("rope_swapped"), sem("rope_cos"), sem("rope_sin"), sem("rope_done"),
            sem("rope_hi"), sem("rope_lo"))
        g_hi_ready, g_lo_ready = sem("g_hi_ready"), sem("g_lo_ready")
        sig_ready, part_a, part_b, merged_ready = sem("sig_ready"), sem("part_a"), sem("part_b"), sem("merged_ready")
        mg_hi_ready, mg_lo_ready = sem("mg_hi_ready"), sem("mg_lo_ready")
        x_again, fg_in = sem("x_again"), sem("fg_in")
        chunk_done, x_added, f_squared, f_sum_ready, f_var_ready, f_rstd_ready, scaled, stored = (
            sem("chunk_done"), sem("x_added"), sem("f_squared"), sem("f_sum_ready"), sem("f_var_ready"),
            sem("f_rstd_ready"), sem("scaled"), sem("stored"))

        BH = HEADS
        ROPES = HEADS + 1

        def tile_no(head, t):
            return head * TOK + (t + 1)

        block = ctx.enter_context(nc.Block())

        @block.sync
        def _(sp):
            def load(piece, parts):
                if not isinstance(piece.n, int) or piece.n >= SLOTS:
                    sp.wait_ge(used, piece.n - (SLOTS - 1))
                    sp.nop(nofuse=True)
                for dst, src in parts:
                    sp.dma_start(dst, src).then_inc(landed[piece.slot], 16)

            def rows(w, r0, n, col, width):
                return w[0, r0 * P:(r0 + n) * P, bass.ds(col, width)].rearrange("(k p) c -> p k c", p=P)

            def block_piece(piece, w, r0, col):
                raw = w_raw[:, piece.slot, :].rearrange("p (k c) -> p k c", k=8)
                load(piece, [(raw[:, 4 * j:4 * j + 4, :], rows(w, r0 + 4 * j, 4, col, P)) for j in range(2)])

            def a_head(h):
                for s in range(A_STEPS):
                    block_piece(Piece(s, h, A_STEPS), w_in, 8 * (s % 2), h * P + (AQ, AK, AV, AG)[s // 2])

            def up_pieces(h):
                piece = Piece(B0, h, B_STEPS)
                raw = w_raw[:, piece.slot, :].rearrange("p (k c) -> p k c", k=LT)
                width = B_NOPE + B_ROPE
                load(piece, [(raw[:, :, 0:width], rows(w_uq, 0, LT, h * width, width)),
                             (raw[:, :, width:2 * P], rows(w_uq, 0, LT, h * width + B_NOPE, B_ROPE))])
                piece = Piece(B0 + 1, h, B_STEPS)
                raw = w_raw[:, piece.slot, :].rearrange("p (k c) -> p k c", k=LT)
                load(piece, [(raw[:, 2 * j:2 * j + 2, :], rows(w_ukv, 2 * j, 2, h * (2 * P), 2 * P))
                             for j in range(2)])

            def merge_blocks(i):
                for b in range(2):
                    col = i * (2 * P) + b * P
                    for s in range(4):
                        block_piece(Piece(M0 + 6 * b + s, i, M_STEPS), w_in, 8 * (s % 2),
                                    col + (MG if s < 2 else MG + D_MODEL))
                    block_piece(Piece(M0 + 6 * b + 4, i, M_STEPS), w_oa, 0, col)
                    block_piece(Piece(M0 + 6 * b + 5, i, M_STEPS), w_ob, 0, col)

            def out_chunk(c):
                for s in range(F_STEPS):
                    piece = Piece(FIN0 + s, c, F_STEPS)
                    raw = w_raw[:, piece.slot, :].rearrange("p (k c) -> p k c", k=2)
                    load(piece, [(raw[:, j:j + 1, :], rows(w_out, 2 * s + j, 1, c * SEQ, SEQ)) for j in range(2)])
                    if s == 4:
                        sp.dma_start(x_tok[:, :, bass.ds(c * SEQ, SEQ)],
                                     x[0, :, bass.ds(c * SEQ, SEQ)].rearrange("(t p) c -> p t c", p=P)
                                     ).then_inc(x_again, 16)

            for t in range(TOK):
                sp.dma_start(x_tok[:, t, :], x[0, t * P:(t + 1) * P, :]).then_inc(x_in[t], 16)
            a_head(0)
            with sp.Fori(1, HEADS) as h:
                a_head(h)
            for b in range(2 * LT):
                for s in range(2):
                    block_piece(Piece(C0 + 2 * b + s), w_in, 8 * s, CQ + b * P)
            for s in range(2):
                piece = Piece(C0 + 4 * LT + s)
                raw = w_raw[:, piece.slot, :].rearrange("p (k c) -> p k c", k=8)
                load(piece, [(raw[:, :, j * B_ROPE:(j + 1) * B_ROPE], rows(w_in, 8 * s, 8, KR, B_ROPE))
                             for j in range(2)])
            for s in range(2):
                block_piece(Piece(C0 + 4 * LT + 2 + s), w_in, 8 * s, BG)
            up_pieces(0)
            with sp.Fori(1, HEADS) as h:
                for s in range(2):
                    block_piece(Piece(B0 - 2 + s, h, B_STEPS), w_in, 8 * s, h * P + BG)
                up_pieces(h)
            with sp.Fori(0, KT // 2) as i:
                merge_blocks(i)
            out_chunk(0)
            sp.dma_start(fg[:, :], final_g.rearrange("(a d) -> a d", a=1).broadcast_to([P, D_MODEL])
                         ).then_inc(fg_in, 16)
            with sp.Fori(1, N_CHUNK) as c:
                out_chunk(c)
            for t in range(TOK):
                sp.wait_ge(scaled, t + 1)
                sp.dma_start(out[0, t * P:(t + 1) * P, :], x_tok[:, t, :]).then_inc(stored, 16)
            sp.wait_ge(stored, 16 * TOK)

        @block.gpsimd
        def _(pool):
            pool.memset(ones, 1.0).then_inc(ones_set, 1)
            pool.memset(mhalf, -0.5).then_inc(ones_set, 1)
            pool.memset(half_pi, math.pi / 2).then_inc(ones_set, 1)
            pool.wait_ge(ones_set, 3)

            def rsqrt(dst, src, ready, n, done):
                pool.wait_ge(ready, n)
                pool.tensor_tensor(dst, src, mhalf[:, 0:src.shape[1]], ALU.pow).then_inc(done, 1)

            for t in range(TOK):
                rsqrt(x_rstd[:, t:t + 1], x_var[:, t:t + 1], x_var_ready, t + 1, x_rstd_ready)

            def halve(h, t):
                pool.wait_ge(max_taken, tile_no(h, t))
                pool.nop(nofuse=True)
                pool.tensor_scalar(dist[:, t, :], dist[:, t, :], SLOPE_RATIO, 1.0, ALU.mult, ALU.mult
                                   ).then_inc(dist_halved, 1)

            for t in range(3):
                halve(0, t)
            with pool.Fori(1, HEADS) as h:
                halve(h - 1, 3)
                rsqrt(o_rstd, o_var, o_var_ready, h, o_rstd_ready)
                for t in range(3):
                    halve(h, t)
            rsqrt(o_rstd, o_var, o_var_ready, HEADS, o_rstd_ready)
            for i in range(2):
                rsqrt(c_rstd, c_var, c_var_ready, i + 1, c_rstd_ready)
            for t in range(TOK):
                rsqrt(f_rstd[:, t:t + 1], f_var[:, t:t + 1], f_var_ready, t + 1, f_rstd_ready)

        @block.scalar
        def _(act):
            def split_hi(piece):
                act.wait_ge(landed[piece.slot], (piece.turn + 1) * 32)
                act.activation(w_hi[:, piece.slot, :], w_raw[:, piece.slot, :], ACT.Copy).then_inc(hi_ready, 1)

            def proj_split_hi(dst, src, piece_end, n_use, use_sem):
                act.wait_ge(used, piece_end)
                if use_sem is not None:
                    act.wait_ge(use_sem, n_use)
                act.activation(dst, src, ACT.Copy).then_inc(proj_hi, 1)

            def pt_hi(head, t, src):
                act.wait_ge(p_turned, tile_no(head, t))
                if t >= 2:
                    act.wait_ge(pv_done, head * 2 + 1)
                act.activation(pt[:, 0, :, (t % 2) * P:(t % 2 + 1) * P],
                               src[:, :].rearrange("p (k c) -> p k c", k=TOK), ACT.Copy).then_inc(pt_hi_ready, 1)

            def exp_a(head, t):
                act.wait_ge(bias_ready, tile_no(head, t))
                for m in range(2):
                    b = 2 * (t % 2) + m
                    last = act.activation(e[:, t % 2, m, :], e[:, t % 2, m, :], ACT.Exp, bias=nm[:, b:b + 1],
                                          scale=A_SCALE, accum_out=sums[:, b:b + 1])
                last.then_inc(exp_done, 1)

            def exp_b(head, t, first):
                act.wait_ge(bias_ready, tile_no(head, t))
                if not first or t >= 2:
                    act.wait_ge(p_turned, tile_no(head, t) - 2)
                act.activation(e_b[:, t % 2, :], SC[t][:, :], ACT.Exp, bias=nm[:, t:t + 1], scale=B_SCALE,
                               accum_out=sums[:, t:t + 1]).then_inc(exp_done, 1)

            def gate(head, piece_end, bank_, first):
                act.wait_ge(used, piece_end)
                if not first:
                    act.wait_ge(silu_done, head)
                act.activation(eg[:, :], bank_[:, :], ACT.Exp, scale=-1.0).then_inc(gate_exp, 1)

            def v_hi(head, src):
                act.wait_ge(v_turned, head + 1)
                act.activation(v_hl[:, 0, :, :], src[:, :].rearrange("p (t c) -> p t c", t=TOK), ACT.Copy
                               ).then_inc(v_hi_ready, 1)

            act.dma_start(cst[:, :], consts[:, :]).then_inc(cst_in, 16)
            act.dma_start(pos_i[:, :], positions.broadcast_to([P, SEQ])).then_inc(pos_in, 16)
            with nc.allow_non_contiguous_dma("gains and positions by partition"):
                act.dma_start(pos_qi[:, :], positions[0, :].rearrange("(t p) -> p t", p=P)).then_inc(pos_in, 16)
                for dst, src in ((g_in, norm_g), (g_q, q_norm_g), (g_kv, kv_norm_g), (g_sub_raw, a_subln_g)):
                    act.dma_start(dst, src[0, :].rearrange("(t p) -> p t", p=P)).then_inc(small_in, 16)
            for i, src in enumerate((lam_q1, lam_k1, lam_q2, lam_k2)):
                act.dma_start(lam_in[:, i, :], src.broadcast_to([P, A_DIM])).then_inc(small_in, 16)
            act.wait_ge(ones_set, 3)
            act.wait_ge(angle_ready, 1)
            act.activation(sin_t[:, :], cos_t[:, :], ACT.Sin).then_inc(trig_ready, 1)
            act.activation(eg[:, :], cos_t[:, :], ACT.Abs).then_inc(a_chain, 1)
            act.wait_ge(a_chain, 1)
            act.activation(cos_t[:, :], eg[:, :], ACT.Sin, scale=-1.0, bias=half_pi).then_inc(trig_ready, 1)
            for t in range(TOK):
                act.wait_ge(x_in[t], 16)
                if t:
                    act.wait_ge(x_ss_ready, t)
                act.activation(square_junk[:, :], x_tok[:, t, :], ACT.Square, accum_out=x_ss[:, t:t + 1]
                               ).then_inc(x_ss_ready, 1)
            for n in range(AHEAD):
                split_hi(Piece(n))
            act.wait_ge(small_in, 16 * 8)
            for k in range(KT):
                act.wait_ge(x_turned, k + 1)
                act.activation(h_hi[:, k, :], bank[2 + k % 6][:, :], ACT.Copy, scale=g_in[:, k:k + 1]
                               ).then_inc(h_hi_ready, 1)
            act.wait_ge(lam_sum, 2)
            act.activation(lam_e, lam_s, ACT.Exp).then_inc(lam_exp, 1)

            def a_step(s, h, cur, prev, first=False):
                if s == 0 and prev:
                    pt_hi(h - 1, 1, TR)
                    exp_a(h - 1, 3)
                    gate(h - 1, (h - 1) * A_STEPS + 8, ACC[1], first)
                if s == 1 and prev:
                    pt_hi(h - 1, 2, TR)
                if s == 2 and prev:
                    pt_hi(h - 1, 3, TR)
                if s == 2 and cur:
                    proj_split_hi(q_hl[:, 0, :], ACC[0][:, :], h * A_STEPS + 2,
                                  tile_no(h, 0) - 1, scored if prev else None)
                if s == 3 and prev:
                    act.wait_ge(pv_done, h * 2)
                    act.activation(vT[:, :], OB[:, :], ACT.Square).then_inc(o_squared, 1)
                if s == 4 and cur:
                    proj_split_hi(k_hl[:, 0, :], ACC[1][:, :], h * A_STEPS + 4,
                                  tile_no(h, 0) - 1, scored if prev else None)
                if s == 5 and cur:
                    exp_a(h, 0)
                if s == 6 and cur:
                    exp_a(h, 1)
                if s == 7 and cur:
                    pt_hi(h, 0, TR)
                    v_hi(h, OB)
                    exp_a(h, 2)

            for s in range(A_STEPS):
                split_hi(Piece(s + AHEAD))
                a_step(s, 0, True, False)
            for s in range(A_STEPS):
                split_hi(Piece(A_STEPS + s + AHEAD))
                a_step(s, 1, True, True, True)
            with act.Fori(2, HEADS) as h:
                for s in range(A_STEPS):
                    split_hi(Piece(s + AHEAD, h, A_STEPS))
                    a_step(s, h, True, True)

            def c_hi_of(i):
                act.wait_ge(c_scaled, i + 1)
                act.activation(c_hi[:, i, :], c_raw[:, i, :], ACT.Copy).then_inc(c_hi_ready, 1)

            def rope_his(i):
                act.wait_ge(rope_done, i + 1)
                if i == 0:
                    act.activation(kr_hi[:, :], rope_in[:, :], ACT.Copy).then_inc(rope_hi, 1)

            for s in range(C_STEPS):
                split_hi(Piece(C0 + s + AHEAD))
                if s < 6:
                    a_step(s, HEADS, False, True)
                b = s // 2 - 1
                if s % 2 == 0 and 0 <= b < 2 * LT:
                    act.wait_ge(acc_read, HEADS * 4 + b + 1)
                    if b:
                        act.wait_ge(c_summed, b)
                    act.activation(c_sq[:, :], c_raw[:, b, :], ACT.Square).then_inc(c_squared, 1)
                if s in (10, 11):
                    for i in range(2):
                        c_hi_of(2 * (s - 10) + i)
                if s in (18, 19):
                    for i in range(2):
                        c_hi_of(LT + 2 * (s - 18) + i)
                if s == 19:
                    rope_his(0)

            def b_step(s, h, cur, prev):
                H = h + BH
                if s == 0 and cur:
                    gate(H, h * B_STEPS + B0, ACC[1], False)
                if s == 0 and prev:
                    exp_b(H - 1, 2, False)
                    exp_b(H - 1, 3, False)
                    pt_hi(H - 1, 0, SC[0])
                    pt_hi(H - 1, 1, SC[1])
                if s == 1 and cur:
                    proj_split_hi(q_hl[:, 0, :], ACC[0][:, :], h * B_STEPS + (B0 + 1),
                                  tile_no(H, 0) - 1 if prev else 2 * LT, scored if prev else c_summed)
                if s == 1 and prev:
                    pt_hi(H - 1, 2, SC[2])
                    pt_hi(H - 1, 3, SC[3])
                if s == 2 and cur:
                    act.wait_ge(rope_done, h + 2)
                    if prev:
                        act.wait_ge(scored, tile_no(H, 0) - 1)
                    act.activation(kr_lo[64:P, :], rope_in[64:P, :], ACT.Copy).then_inc(rope_hi, 1)
                    act.activation(qr_hl[0:64, :], rope_in[0:64, :], ACT.Copy).then_inc(rope_hi, 1)
                    proj_split_hi(k_hl[:, 0, :], ACC[1][:, :], h * B_STEPS + (B0 + 2),
                                  tile_no(H, 0) - 1, scored)
                if s == 3 and cur:
                    exp_b(H, 0, False)
                    exp_b(H, 1, False)
                    v_hi(H, TR)

            for s in range(B_STEPS):
                split_hi(Piece(B0 + s + AHEAD))
                b_step(s, 0, True, False)
            with act.Fori(1, HEADS - 1) as h:
                for s in range(B_STEPS):
                    split_hi(Piece(B0 + s + AHEAD, h, B_STEPS))
                    b_step(s, h, True, True)
            last = HEADS - 1
            for s in range(2):
                split_hi(Piece(B0 + B_STEPS * last + s + AHEAD))
                b_step(s, last, True, True)

            def sigmoid(i, b, branch):
                first = M0 + 6 * b + 2 * branch + 2
                act.wait_ge(used, i * M_STEPS + first)
                act.activation(sig[:, b, branch, :], bank[(0, 4)[b] + branch][:, :], ACT.Sigmoid
                               ).then_inc(sig_ready, 1)

            def merge_step(s, i):
                if s in (2, 4, 8, 10):
                    b = s // 6
                    if s % 6 == 2 and not isinstance(i, int):
                        act.wait_ge(merged_ready, i * 2 + (b - 1))
                    sigmoid(i, b, (s % 6) // 4)

            def gated_hi(head):
                act.wait_ge(head_gated, head + 1)
                dst = ga_hi[:, head, :] if head < HEADS else gb_hl[:, head - HEADS, 0, :]
                act.activation(dst, gated[:, head * SEQ:(head + 1) * SEQ], ACT.Copy).then_inc(g_hi_ready, 1)

            for s in range(M_STEPS):
                split_hi(Piece(M0 + s + AHEAD))
                if s < 2:
                    b_step(s + 2, last, True, True)
                elif s < 5:
                    b_step(s - 2, HEADS, False, True)
                if s == 0:
                    act.wait_ge(used, M0)
                if s == 2:
                    act.wait_ge(scored, tile_no(2 * HEADS - 1, 3))
                    act.wait_ge(silu_done, 2 * HEADS)
                if s == 3:
                    act.wait_ge(p_turned, tile_no(2 * HEADS - 1, 3))
                if s == 4:
                    act.wait_ge(pv_done, 4 * HEADS)
                for head in GATED_AT[s]:
                    gated_hi(head)
                merge_step(s, 0)
            with act.Fori(1, KT // 2) as i:
                for s in range(M_STEPS):
                    split_hi(Piece(M0 + s + AHEAD, i, M_STEPS))
                    merge_step(s, i)

            def merged_hi(j):
                act.wait_ge(merged_ready, j + 1)
                if j == 0:
                    act.wait_ge(used, FIN0 - 2)
                act.activation(mg_hi[:, j, :], merged[:, j * SEQ:(j + 1) * SEQ], ACT.Copy).then_inc(mg_hi_ready, 1)

            def chunk_squares(c):
                for t in range(TOK):
                    act.wait_ge(x_added, c * TOK + (t + 1))
                    if isinstance(c, int) and c == 0 and t == 0:
                        act.wait_ge(fg_in, 16)
                    else:
                        act.wait_ge(f_squared, c * TOK + t)
                    act.activation(eg[:, :], x_tok[:, t, bass.ds(c * SEQ, SEQ)], ACT.Square,
                                   accum_out=f_ss[:, bass.ds(c * TOK + t, 1)]).then_inc(f_squared, 1)

            for j in range(4):
                merged_hi(j)
            for s in range(F_STEPS):
                split_hi(Piece(FIN0 + s + AHEAD))
                for j in (4 + 2 * s, 5 + 2 * s):
                    if j < KT:
                        merged_hi(j)
            chunk_squares(0)
            with act.Fori(1, N_CHUNK - 1) as c:
                for s in range(F_STEPS):
                    split_hi(Piece(FIN0 + s + AHEAD, c, F_STEPS))
                chunk_squares(c)
            for s in range(F_STEPS - AHEAD):
                split_hi(Piece(FIN0 + F_STEPS * (N_CHUNK - 1) + s + AHEAD))
            chunk_squares(N_CHUNK - 1)

        @block.vector
        def _(dve):
            chain = [0]

            def link(ins):
                chain[0] += 1
                ins.then_inc(v_chain, 1)
                dve.wait_ge(v_chain, chain[0])

            def split_lo(piece):
                dve.wait_ge(hi_ready, piece.after(0))
                dve.tensor_tensor(w_lo[:, piece.slot, :], w_raw[:, piece.slot, :],
                                  w_hi[:, piece.slot, :].bitcast(F32), ALU.subtract).then_inc(lo_ready, 1)

            def proj_split_lo(dst, src, n):
                dve.wait_ge(proj_hi, n)
                dve.tensor_tensor(dst[:, 1, :], src[:, :], dst[:, 0, :].bitcast(F32), ALU.subtract
                                  ).then_inc(acc_read, 1)

            def pt_lo(head, t, src):
                dve.wait_ge(pt_hi_ready, tile_no(head, t))
                c = slice((t % 2) * P, (t % 2 + 1) * P)
                dve.tensor_tensor(pt[:, 1, :, c], src[:, :].rearrange("p (k c) -> p k c", k=TOK),
                                  pt[:, 0, :, c].bitcast(F32), ALU.subtract).then_inc(pt_lo_ready, 1)

            def max_a(head, t, first):
                n = tile_no(head, t)
                dve.wait_ge(scored, n)
                if not first:
                    dve.wait_ge(dist_halved, n - TOK)
                if not first or t >= 2:
                    dve.wait_ge(p_turned, n - 2)
                dve.nop(nofuse=True)
                for m in range(2):
                    b = 2 * (t % 2) + m
                    last = dve.tensor_tensor_reduce(out=e[:, t % 2, m, :], in0=SC[b][:, :], in1=dist[:, t, :],
                                                    scale=1.0, scalar=-3.0e38, op0=ALU.add, op1=ALU.max,
                                                    accum_out=mx[:, b:b + 1])
                last.then_inc(max_taken, 1)
                dve.wait_ge(max_taken, n)
                b = 2 * (t % 2)
                dve.tensor_scalar(nm[:, b:b + 2], mx[:, b:b + 2], -A_SCALE, None, ALU.mult).then_inc(bias_ready, 1)

            def norm_a(head, t):
                n = tile_no(head, t)
                b = 2 * (t % 2)
                dve.wait_ge(exp_done, n)
                dve.reciprocal(rs[:, b:b + 2], sums[:, b:b + 2]).then_inc(inv_ready, 1)
                dve.wait_ge(inv_ready, n)
                dve.tensor_scalar(rs_lam[:, t % 2:t % 2 + 1], rs[:, b + 1:b + 2], lam, None, ALU.mult
                                  ).then_inc(inv_lam_ready, 1)
                dve.wait_ge(inv_lam_ready, n)
                dve.tensor_scalar(e[:, t % 2, 1, :], e[:, t % 2, 1, :], rs_lam[:, t % 2:t % 2 + 1], None, ALU.mult
                                  ).then_inc(e2_scaled, 1)
                dve.wait_ge(e2_scaled, n)
                dve.scalar_tensor_tensor(e[:, t % 2, 0, :], e[:, t % 2, 0, :], rs[:, b:b + 1], e[:, t % 2, 1, :],
                                         ALU.mult, ALU.subtract).then_inc(p_ready, 1)

            def max_b(head, t):
                n = tile_no(head, t)
                dve.wait_ge(scored, n)
                dve.reduce_max(mx[:, t:t + 1], SC[t][:, :], AX_X).then_inc(max_taken, 1)
                dve.wait_ge(max_taken, n)
                dve.tensor_scalar(nm[:, t:t + 1], mx[:, t:t + 1], -B_SCALE, None, ALU.mult).then_inc(bias_ready, 1)

            def norm_b(head, t):
                n = tile_no(head, t)
                dve.wait_ge(exp_done, n)
                dve.reciprocal(rs[:, t:t + 1], sums[:, t:t + 1]).then_inc(inv_ready, 1)
                dve.wait_ge(inv_ready, n)
                dve.tensor_scalar(e_b[:, t % 2, :], e_b[:, t % 2, :], rs[:, t:t + 1], None, ALU.mult
                                  ).then_inc(p_ready, 1)

            def gate_of(head):
                return gated[:, bass.ds(head * SEQ, SEQ)]

            def gate_copy(head, src):
                dve.wait_ge(gate_exp, head + 1)
                dve.tensor_copy(gate_of(head), src[:, :]).then_inc(acc_read, 1)

            def silu_half(head, half):
                if half == 0:
                    dve.wait_ge(gate_exp, head + 1)
                    dve.tensor_scalar(eg[:, :], eg[:, :], 1.0, None, ALU.add).then_inc(silu_add, 1)
                    dve.wait_ge(silu_add, head + 1)
                c = slice(half * (SEQ // 2), (half + 1) * (SEQ // 2))
                dve.reciprocal(eg[:, c], eg[:, c]).then_inc(silu_inv, 1)

            def silu_mult(head, n_copy):
                dve.wait_ge(silu_inv, head * 2 + 2)
                dve.wait_ge(acc_read, n_copy)
                dve.tensor_tensor(gate_of(head), gate_of(head), eg[:, :], ALU.mult).then_inc(silu_done, 1)

            def v_lo(head, src):
                dve.wait_ge(v_hi_ready, head + 1)
                dve.tensor_tensor(v_hl[:, 1, :, :], src[:, :].rearrange("p (t c) -> p t c", t=TOK),
                                  v_hl[:, 0, :, :].bitcast(F32), ALU.subtract).then_inc(v_lo_ready, 1)

            dve.wait_ge(pos_in, 32)
            dve.wait_ge(cst_in, 16)
            link(dve.tensor_copy(pos_f[:, :], pos_i[:, :]))
            link(dve.tensor_copy(pos_q, pos_qi[:, :]))
            r, n1, n0 = cos_t, sin_t, eg
            link(dve.tensor_scalar(r[:, :], pos_f[:, :], inv_freq, None, ALU.mult))
            link(dve.tensor_scalar(n0[:, :], r[:, :], 1.0 / (2.0 * math.pi), ROUND_1, ALU.mult, ALU.add))
            link(dve.tensor_scalar(n0[:, :], n0[:, :], -ROUND_1, None, ALU.add))
            link(dve.tensor_scalar(n1[:, :], n0[:, :], ROUND_2048, -ROUND_2048, ALU.add, ALU.add))
            link(dve.tensor_tensor(n0[:, :], n0[:, :], n1[:, :], ALU.subtract))
            for part_2pi in (TWO_PI_1, TWO_PI_2, TWO_PI_3):
                for n in (n1, n0):
                    link(dve.scalar_tensor_tensor(r[:, :], n[:, :], -part_2pi, r[:, :], ALU.mult, ALU.add))
            dve.tensor_scalar(r[:, :], r[:, :], PI_DOWN, -PI_DOWN, ALU.min, ALU.max).then_inc(angle_ready, 1)
            for t in range(TOK):
                dve.wait_ge(x_ss_ready, t + 1)
                dve.tensor_scalar(x_var[:, t:t + 1], x_ss[:, t:t + 1], 1.0 / D_MODEL, NORM_EPS, ALU.mult, ALU.add
                                  ).then_inc(x_var_ready, 1)
                dve.wait_ge(x_rstd_ready, t + 1)
                dve.tensor_scalar(x_tok[:, t, :], x_tok[:, t, :], x_rstd[:, t:t + 1], None, ALU.mult
                                  ).then_inc(x_normed, 1)
            for n in range(AHEAD):
                split_lo(Piece(n))
            dve.wait_ge(small_in, 16 * 8)
            for k in range(KT):
                dve.wait_ge(h_hi_ready, k + 1)
                dve.scalar_tensor_tensor(h_lo[:, k, :], bank[2 + k % 6][:, :], g_in[:, k:k + 1],
                                         h_hi[:, k, :].bitcast(F32), ALU.mult, ALU.subtract
                                         ).then_inc(h_lo_ready, 1)
            for i in range(2):
                dve.tensor_tensor_reduce(out=lam_in[:, 4 + i, :], in0=lam_in[:, 2 * i, :],
                                              in1=lam_in[:, 2 * i + 1, :], scale=1.0, scalar=0.0,
                                              op0=ALU.mult, op1=ALU.add, accum_out=lam_s[:, i:i + 1]).then_inc(lam_sum, 1)
            link(dve.tensor_scalar(g_sub, g_sub_raw, 1.0 - LAM_INIT, None, ALU.mult))
            for t in range(TOK):
                link(dve.tensor_scalar(dist[:, t, :], pos_f[:, :], pos_q[:, t:t + 1], SLOPE0 / A_SCALE,
                                       ALU.subtract, ALU.mult))
                link(dve.scalar_tensor_tensor(dist[:, t, :], dist[:, t, :], -1.0, dist[:, t, :], ALU.mult, ALU.min))
            dve.wait_ge(lam_exp, 1)
            link(dve.tensor_scalar(lam, lam_e[:, 0:1], lam_e[:, 1:2], LAM_INIT, ALU.subtract, ALU.add))

            def a_step(s, h, cur, prev, first=False):
                if s == 0 and prev:
                    pt_lo(h - 1, 1, TR)
                    norm_a(h - 1, 2)
                    max_a(h - 1, 3, first)
                    gate_copy(h - 1, ACC[1])
                if s == 1 and prev:
                    pt_lo(h - 1, 2, TR)
                    norm_a(h - 1, 3)
                    silu_half(h - 1, 0)
                if s == 2 and prev:
                    pt_lo(h - 1, 3, TR)
                if s == 2 and cur:
                    proj_split_lo(q_hl, ACC[0], h * 2 + 1)
                if s == 2 and prev:
                    silu_half(h - 1, 1)
                if s == 3 and prev:
                    dve.wait_ge(o_squared, h)
                    if not first:
                        dve.wait_ge(head_gated, h - 1)
                    dve.tensor_copy(oT[:, :], OB[:, :]).then_inc(o_copied, 1)
                    silu_mult(h - 1, h * 4)
                if s == 4 and cur:
                    proj_split_lo(k_hl, ACC[1], h * 2 + 2)
                if s == 4 and prev:
                    dve.wait_ge(o_summed, h)
                    dve.tensor_scalar(o_var, TR[:, 0:TOK], 1.0 / P, SUBLN_EPS, ALU.mult, ALU.add
                                      ).then_inc(o_var_ready, 1)
                if s == 5 and cur:
                    max_a(h, 0, not prev)
                if s == 5 and prev:
                    dve.wait_ge(o_spread, h)
                    dve.wait_ge(o_copied, h)
                    dve.scalar_tensor_tensor(oT[:, :], TR[:, :], g_sub, oT[:, :], ALU.mult, ALU.mult
                                             ).then_inc(o_normed, 1)
                    dve.wait_ge(o_normed, h)
                    dve.wait_ge(silu_done, h)
                    dve.tensor_tensor(gate_of(h - 1), gate_of(h - 1), oT[:, :], ALU.mult).then_inc(head_gated, 1)
                if s == 6 and cur:
                    dve.wait_ge(used, h * A_STEPS + 6)
                    if prev:
                        dve.wait_ge(o_summed, h)
                    dve.tensor_copy(vT[:, :], ACC[0][:, :]).then_inc(acc_read, 1)
                    norm_a(h, 0)
                    max_a(h, 1, not prev)
                if s == 7 and cur:
                    pt_lo(h, 0, TR)
                    norm_a(h, 1)
                    max_a(h, 2, not prev)
                    v_lo(h, OB)

            for s in range(A_STEPS):
                split_lo(Piece(s + AHEAD))
                a_step(s, 0, True, False)
            for s in range(A_STEPS):
                split_lo(Piece(A_STEPS + s + AHEAD))
                a_step(s, 1, True, True, True)
            with dve.Fori(2, HEADS) as h:
                for s in range(A_STEPS):
                    split_lo(Piece(s + AHEAD, h, A_STEPS))
                    a_step(s, h, True, True)

            def c_norm(i):
                j = i // LT
                dve.wait_ge(c_spread, j + 1)
                dve.wait_ge(acc_read, HEADS * 4 + i + 1)
                g = (g_q, g_kv)[j][:, i % LT:i % LT + 1]
                dve.scalar_tensor_tensor(c_raw[:, i, :], c_raw[:, i, :], g, SC[2 * j + 1][:, :],
                                         ALU.mult, ALU.mult).then_inc(c_scaled, 1)

            def c_lo_of(i):
                dve.wait_ge(c_hi_ready, i + 1)
                dve.tensor_tensor(c_lo[:, i, :], c_raw[:, i, :], c_hi[:, i, :].bitcast(F32), ALU.subtract
                                  ).then_inc(c_lo_ready, 1)

            def rope_copy(i, piece_end, src):
                dve.wait_ge(used, piece_end)
                if not isinstance(i, int) or i > 0:
                    dve.wait_ge(rope_lo, i)
                dve.tensor_copy(rope_in[:, :], src[:, :]).then_inc(rope_copied, 1)

            def rotate(i):
                dve.wait_ge(rope_swapped, i + 1)
                dve.tensor_tensor(rope_sw[:, :], TR[:, :], sin_t[:, :], ALU.mult).then_inc(rope_sin, 1)
                dve.tensor_tensor(rope_in[:, :], rope_in[:, :], cos_t[:, :], ALU.mult).then_inc(rope_cos, 1)
                dve.wait_ge(rope_sin, i + 1)
                dve.wait_ge(rope_cos, i + 1)
                dve.tensor_tensor(rope_in[:, :], rope_in[:, :], rope_sw[:, :], ALU.add).then_inc(rope_done, 1)

            for s in range(C_STEPS):
                split_lo(Piece(C0 + s + AHEAD))
                if s < 6:
                    a_step(s, HEADS, False, True)
                b = s // 2 - 1
                if s % 2 == 0 and 0 <= b < 2 * LT:
                    dve.wait_ge(used, C0 + s)
                    if b == LT:
                        dve.wait_ge(dist_halved, HEADS * TOK - 1)
                    dve.tensor_copy(c_raw[:, b, :], ACC[b % 2][:, :]).then_inc(acc_read, 1)
                if s in (9, 17):
                    j = s // 16
                    dve.wait_ge(c_summed, LT * (j + 1))
                    dve.tensor_reduce(c_ss, SC[2 * j][:, 0:LT * TOK].rearrange("p (b t) -> p t b", b=LT),
                                      axis=AX_X, op=ALU.add).then_inc(c_ss_ready, 1)
                    dve.wait_ge(c_ss_ready, j + 1)
                    dve.tensor_scalar(c_var, c_ss, 1.0 / LORA, NORM_EPS, ALU.mult, ALU.add).then_inc(c_var_ready, 1)
                if s in (10, 11, 18, 19):
                    i = (LT * (s // 16)) + 2 * (s % 2)
                    c_norm(i)
                    c_norm(i + 1)
                    c_lo_of(i)
                    c_lo_of(i + 1)
                if s == 18:
                    dve.wait_ge(used, C0 + 18)
                    dve.tensor_copy(rope_in[:, :], ACC[0][:, :]).then_inc(acc_read, 1)
                    dve.wait_ge(acc_read, HEADS * 4 + 9)
                if s == 19:
                    rotate(0)
                    dve.wait_ge(rope_hi, 1)
                    dve.tensor_tensor(kr_lo[0:64, :], rope_in[0:64, :], kr_hi[0:64, :].bitcast(F32), ALU.subtract
                                      ).then_inc(rope_lo, 1)

            G0 = HEADS * 4 + 10

            def b_step(s, h, cur, prev):
                H = h + BH
                if s == 0 and cur:
                    gate_copy(H, ACC[1])
                if s == 0 and prev:
                    max_b(H - 1, 2)
                    max_b(H - 1, 3)
                    pt_lo(H - 1, 0, SC[0])
                    pt_lo(H - 1, 1, SC[1])
                    norm_b(H - 1, 2)
                    norm_b(H - 1, 3)
                if s == 1 and cur:
                    proj_split_lo(q_hl, ACC[0], H * 2 + 1)
                    rope_copy(h + 1, h * B_STEPS + (B0 + 1), TR)
                if s == 1 and prev:
                    pt_lo(H - 1, 2, SC[2])
                    pt_lo(H - 1, 3, SC[3])
                if s == 1 and cur:
                    silu_half(H, 0)
                if s == 2 and cur:
                    rotate(h + 1)
                    proj_split_lo(k_hl, ACC[1], H * 2 + 2)
                    dve.wait_ge(rope_hi, h * 2 + 3)
                    dve.tensor_tensor(qr_hl[64:P, :], rope_in[64:P, :], kr_lo[64:P, :].bitcast(F32), ALU.subtract
                                      ).then_inc(rope_lo, 1)
                    dve.wait_ge(used, h * B_STEPS + (B0 + 2))
                    if prev:
                        dve.wait_ge(v_turned, H)
                    dve.tensor_copy(vT[:, :], ACC[0][:, :]).then_inc(acc_read, 1)
                if s == 2 and prev:
                    dve.wait_ge(pv_done, H * 2)
                    dve.wait_ge(silu_done, H)
                    dve.tensor_tensor(gate_of(H - 1), OB[:, :], gate_of(H - 1), ALU.mult).then_inc(head_gated, 1)
                if s == 3 and cur:
                    max_b(H, 0)
                    max_b(H, 1)
                    v_lo(H, TR)
                    norm_b(H, 0)
                    norm_b(H, 1)
                    silu_half(H, 1)
                    silu_mult(H, h * 4 + G0)

            for s in range(B_STEPS):
                split_lo(Piece(B0 + s + AHEAD))
                b_step(s, 0, True, False)
            with dve.Fori(1, HEADS - 1) as h:
                for s in range(B_STEPS):
                    split_lo(Piece(B0 + s + AHEAD, h, B_STEPS))
                    b_step(s, h, True, True)
            last = HEADS - 1
            for s in range(2):
                split_lo(Piece(B0 + B_STEPS * last + s + AHEAD))
                b_step(s, last, True, True)

            def gated_lo(head):
                dve.wait_ge(g_hi_ready, GATED_ORDER.index(head) + 1)
                hi, lo = ((ga_hi[:, head, :], ga_lo[:, head, :]) if head < HEADS else
                          (gb_hl[:, head - HEADS, 0, :], gb_hl[:, head - HEADS, 1, :]))
                dve.tensor_tensor(lo, gated[:, head * SEQ:(head + 1) * SEQ], hi.bitcast(F32), ALU.subtract
                                  ).then_inc(g_lo_ready, 1)

            def branch_a(i, b):
                dve.wait_ge(used, i * M_STEPS + (M0 + 6 * b + 5))
                dve.wait_ge(sig_ready, i * 4 + (2 * b + 1))
                dve.tensor_tensor(part[:, 0, :], bank[4 * b + 2][:, :], sig[:, b, 0, :], ALU.mult).then_inc(part_a, 1)

            def branch_b(i, b):
                n = i * 2 + (b + 1)
                dve.wait_ge(used, i * M_STEPS + (M0 + 6 * b + 6))
                dve.wait_ge(sig_ready, i * 4 + (2 * b + 2))
                dve.tensor_tensor(part[:, 1, :], bank[4 * b + 3][:, :], sig[:, b, 1, :], ALU.mult).then_inc(part_b, 1)
                dve.wait_ge(part_a, n)
                dve.wait_ge(part_b, n)
                dve.tensor_tensor(merged[:, bass.ds(i * (2 * SEQ) + b * SEQ, SEQ)], part[:, 0, :], part[:, 1, :],
                                  ALU.add).then_inc(merged_ready, 1)

            def merge_step(s, i, prev):
                if s == 0 and prev:
                    branch_b(i - 1, 1)
                if s == 5:
                    if prev:
                        dve.wait_ge(merged_ready, i * 2)
                    branch_a(i, 0)
                if s == 6:
                    branch_b(i, 0)
                if s == 11:
                    dve.wait_ge(merged_ready, i * 2 + 1)
                    branch_a(i, 1)

            for s in range(M_STEPS):
                split_lo(Piece(M0 + s + AHEAD))
                if s < 2:
                    b_step(s + 2, last, True, True)
                elif s < 5:
                    b_step(s - 2, HEADS, False, True)
                for head in GATED_AT[s]:
                    gated_lo(head)
                merge_step(s, 0, False)
            with dve.Fori(1, KT // 2) as i:
                for s in range(M_STEPS):
                    split_lo(Piece(M0 + s + AHEAD, i, M_STEPS))
                    merge_step(s, i, True)

            def merged_lo(j):
                dve.wait_ge(mg_hi_ready, j + 1)
                dve.tensor_tensor(mg_lo[:, j, :], merged[:, j * SEQ:(j + 1) * SEQ], mg_hi[:, j, :].bitcast(F32),
                                  ALU.subtract).then_inc(mg_lo_ready, 1)

            def add_x(c, t):
                if t < TOK - 1:
                    dve.wait_ge(chunk_done, c * (TOK - 1) + (t + 1))
                else:
                    dve.wait_ge(used, c * F_STEPS + (FIN0 + F_STEPS))
                dve.wait_ge(x_again, c * 16 + 16)
                xt = x_tok[:, t, bass.ds(c * SEQ, SEQ)]
                dve.tensor_tensor(xt, bank[t][:, :], xt, ALU.add).then_inc(x_added, 1)

            for j in range(4):
                merged_lo(j)
            branch_b(KT // 2 - 1, 1)
            for s in range(F_STEPS):
                split_lo(Piece(FIN0 + s + AHEAD))
                for j in (4 + 2 * s, 5 + 2 * s):
                    if j < KT:
                        merged_lo(j)
            for t in range(TOK):
                add_x(0, t)
            with dve.Fori(1, N_CHUNK - 1) as c:
                for s in range(F_STEPS):
                    split_lo(Piece(FIN0 + s + AHEAD, c, F_STEPS))
                for t in range(TOK):
                    add_x(c, t)
            for s in range(F_STEPS - AHEAD):
                split_lo(Piece(FIN0 + F_STEPS * (N_CHUNK - 1) + s + AHEAD))
            dve.wait_ge(fg_in, 16)
            for t in range(TOK):
                add_x(N_CHUNK - 1, t)
                dve.wait_ge(f_squared, (N_CHUNK - 1) * TOK + t + 1)
                dve.tensor_reduce(f_sum[:, t:t + 1], f_ss.rearrange("p (c t) -> p t c", t=TOK)[:, t:t + 1, :],
                                  axis=AX_X, op=ALU.add).then_inc(f_sum_ready, 1)
                dve.wait_ge(f_sum_ready, t + 1)
                dve.tensor_scalar(f_var[:, t:t + 1], f_sum[:, t:t + 1], 1.0 / D_MODEL, NORM_EPS, ALU.mult, ALU.add
                                  ).then_inc(f_var_ready, 1)
                dve.wait_ge(f_rstd_ready, t + 1)
                dve.scalar_tensor_tensor(x_tok[:, t, :], x_tok[:, t, :], f_rstd[:, t:t + 1], fg[:, :],
                                         ALU.mult, ALU.mult).then_inc(scaled, 1)

        @block.tensor
        def _(pe):
            def three(dst, lhs_hi, lhs_lo, rhs_hi, rhs_lo, start, stop):
                pe.matmul(dst, lhs_hi, rhs_hi, start=start, stop=False)
                pe.matmul(dst, lhs_hi, rhs_lo, start=False, stop=False)
                return pe.matmul(dst, lhs_lo, rhs_hi, start=False, stop=stop)

            def tile(piece, c0, width=P):
                return w_hi[:, piece.slot, c0:c0 + width], w_lo[:, piece.slot, c0:c0 + width]

            def project(piece, dst, half, halves, rhs_hi, rhs_lo, k0, h_waits=False):
                pe.wait_ge(lo_ready, piece.after(0))
                for k in range(8):
                    if h_waits:
                        pe.wait_ge(h_lo_ready, k0 + k + 1)
                    hi, lo = tile(piece, k * P)
                    last = three(dst[:, :], hi, lo, rhs_hi[:, k0 + k, :], rhs_lo[:, k0 + k, :],
                                 half == 0 and k == 0, half == halves - 1 and k == 7)
                last.then_inc(used, 1)

            def scores_a(head, t, first):
                if t == 0:
                    pe.wait_ge(acc_read, head * 4 + 2)
                if not first or t >= 2:
                    pe.wait_ge(max_taken, tile_no(head, t) - 2)
                a, b = SC[2 * (t % 2)], SC[2 * (t % 2) + 1]
                q = slice(t * P, (t + 1) * P)
                for i, (l, r) in enumerate(((0, 0), (0, 1), (1, 0))):
                    for dst, rows in ((a, slice(0, 64)), (b, slice(64, P))):
                        last = pe.matmul(dst[:, :], q_hl[rows, l, q], k_hl[rows, r, :], start=(i == 0), stop=(i == 2))
                last.then_inc(scored, 1)

            def scores_b(h, t, prev):
                H = h + BH
                if t == 0:
                    pe.wait_ge(acc_read, h * 4 + (HEADS * 4 + 12))
                    pe.wait_ge(rope_lo, h + 2)
                if prev:
                    pe.wait_ge(pt_lo_ready, tile_no(H, t) - TOK)
                elif t == 0:
                    pe.wait_ge(c_lo_ready, 2 * LT)
                q = slice(t * P, (t + 1) * P)
                dst = SC[t][:, :]
                pe.matmul(dst, q_hl[:, 0, q], k_hl[:, 0, :], start=True, stop=False)
                pe.matmul(dst, q_hl[:, 0, q], k_hl[:, 1, :], start=False, stop=False)
                pe.matmul(dst, q_hl[:, 1, q], k_hl[:, 0, :], start=False, stop=False)
                pe.matmul(dst, qr_hl[:, q], kr_hi[:, :], start=False, stop=False)
                pe.matmul(dst, qr_hl[0:64, q], kr_lo[0:64, :], start=False, stop=True).then_inc(scored, 1)

            def turn(src, dst, done):
                for k in range(TOK):
                    last = pe.transpose(dst[:, k * P:(k + 1) * P], src[:, k * P:(k + 1) * P], ident)
                last.then_inc(done, 1)

            def turn_p_a(head, t, first):
                pe.wait_ge(p_ready, tile_no(head, t))
                if t:
                    pe.wait_ge(pt_lo_ready, tile_no(head, t) - 1)
                elif not first:
                    pe.wait_ge(o_normed, head)
                turn(e[:, t % 2, 0, :], TR, p_turned)

            def turn_p_b(head, t):
                pe.wait_ge(p_ready, tile_no(head, t))
                turn(e_b[:, t % 2, :], SC[t], p_turned)

            def pv(head, pair):
                pe.wait_ge(pt_lo_ready, tile_no(head, 2 * pair + 1))
                pe.wait_ge(v_lo_ready, head + 1)
                for k in range(TOK):
                    last = three(OB[:, pair * 2 * P:(pair + 1) * 2 * P], v_hl[:, 0, k, :], v_hl[:, 1, k, :],
                                 pt[:, 0, k, :], pt[:, 1, k, :], k == 0, k == TOK - 1)
                last.then_inc(pv_done, 1)

            def column_sums(sq, dst, c0, done):
                for t in range(TOK):
                    last = pe.matmul(dst[:, c0 + t:c0 + t + 1], sq[:, t * P:(t + 1) * P], ones, start=True, stop=True)
                last.then_inc(done, 1)

            def spread(col, dst, done):
                for t in range(TOK):
                    last = pe.matmul(dst[:, t * P:(t + 1) * P], col[:, t:t + 1].broadcast_to([P, P]), ident,
                                     start=True, stop=True)
                last.then_inc(done, 1)

            pe.wait_ge(cst_in, 16)
            pe.wait_ge(ones_set, 3)
            pe.wait_ge(x_normed, TOK)
            for k in range(KT):
                if k >= 6:
                    pe.wait_ge(h_lo_ready, k - 5)
                for t in range(TOK):
                    last = pe.transpose(bank[2 + k % 6][:, t * P:(t + 1) * P], x_tok[:, t, k * P:(k + 1) * P], ident)
                last.then_inc(x_turned, 1)

            def a_extras(s, h, cur, prev, first=False):
                if s == 0 and prev:
                    turn_p_a(h - 1, 2, first)
                    pv(h - 1, 0)
                if s == 1 and prev:
                    turn_p_a(h - 1, 3, first)
                if s == 2 and prev:
                    pv(h - 1, 1)
                if s == 3 and prev:
                    pe.wait_ge(o_squared, h)
                    pe.wait_ge(pt_lo_ready, h * TOK)
                    column_sums(vT, TR, 0, o_summed)
                if s == 4 and cur:
                    scores_a(h, 0, not prev)
                if s == 4 and prev:
                    pe.wait_ge(o_rstd_ready, h)
                    spread(o_rstd, TR, o_spread)
                if s == 5 and cur:
                    scores_a(h, 1, not prev)
                if s == 6 and cur:
                    pe.wait_ge(acc_read, h * 4 + 3)
                    if prev:
                        pe.wait_ge(o_copied, h)
                    turn(vT, OB, v_turned)
                    turn_p_a(h, 0, not prev)
                    scores_a(h, 2, not prev)
                if s == 7 and cur:
                    turn_p_a(h, 1, not prev)
                    scores_a(h, 3, not prev)

            def a_head(h, prev, first=False):
                for s in range(A_STEPS):
                    g = s // 2
                    if s % 2 == 0 and (prev or g >= 2):
                        pe.wait_ge(acc_read, h * 4 + (g - 1))
                    project(Piece(s, h, A_STEPS), ACC[g % 2], s % 2, 2, h_hi, h_lo, 8 * (s % 2),
                            h_waits=not prev and s < 2)
                    a_extras(s, h, True, prev, first)

            a_head(0, False)
            with pe.Fori(1, HEADS) as h:
                a_head(h, True)

            for s in range(C_STEPS):
                b = s // 2
                if s % 2 == 0:
                    pe.wait_ge(acc_read, HEADS * 4 + b - 1)
                project(Piece(C0 + s), ACC[b % 2], s % 2, 2, h_hi, h_lo, 8 * (s % 2))
                if s < 6:
                    a_extras(s, HEADS, False, True)
                b -= 1
                if s % 2 == 0 and 0 <= b < 2 * LT:
                    if b == 0:
                        pe.wait_ge(max_taken, HEADS * TOK)
                    pe.wait_ge(c_squared, b + 1)
                    column_sums(c_sq, SC[2 * (b // LT)], TOK * (b % LT), c_summed)
                if s in (9, 17):
                    j = s // 16
                    pe.wait_ge(c_rstd_ready, j + 1)
                    spread(c_rstd, SC[2 * j + 1], c_spread)
                if s == 18:
                    pe.wait_ge(acc_read, HEADS * 4 + 9)
                    pe.wait_ge(o_normed, HEADS)
                    pe.matmul(TR[:, :], swap, rope_in[:, :], start=True, stop=True).then_inc(rope_swapped, 1)

            def up(piece, c0, dst, which):
                for k in range(LT):
                    hi, lo = tile(piece, k * 2 * P + c0)
                    last = three(dst[:, :], hi, lo, c_hi[:, which * LT + k, :], c_lo[:, which * LT + k, :],
                                 k == 0, k == LT - 1)
                return last

            def b_extras(s, h, cur, prev):
                H = h + BH
                if s == 0 and prev:
                    pe.wait_ge(head_gated, H - 1)
                    pv(H - 1, 0)
                    turn_p_b(H - 1, 2)
                    turn_p_b(H - 1, 3)
                if s == 1 and cur:
                    pe.wait_ge(rope_copied, h + 1)
                    pe.matmul(TR[:, :], swap, rope_in[:, :], start=True, stop=True).then_inc(rope_swapped, 1)
                if s == 1 and prev:
                    pv(H - 1, 1)
                if s == 2 and cur:
                    scores_b(h, 0, prev)
                    scores_b(h, 1, prev)
                    pe.wait_ge(acc_read, h * 4 + (HEADS * 4 + 13))
                    pe.wait_ge(rope_sin, h + 2)
                    turn(vT, TR, v_turned)
                if s == 3 and cur:
                    scores_b(h, 2, prev)
                    scores_b(h, 3, prev)
                    turn_p_b(H, 0)
                    turn_p_b(H, 1)

            def b_up(h, prev):
                g = h * 4 + (HEADS * 4 + 10)
                H = h + BH
                piece = Piece(B0, h, B_STEPS)
                pe.wait_ge(lo_ready, piece.after(0))
                if prev:
                    pe.wait_ge(v_lo_ready, H)
                else:
                    pe.wait_ge(rope_lo, 1)
                    pe.wait_ge(c_lo_ready, LT)
                up(piece, P, TR, 0)
                pe.wait_ge(acc_read, g - 1)
                up(piece, 0, ACC[0], 0).then_inc(used, 1)
                b_extras(0, h, True, prev)
                piece = Piece(B0 + 1, h, B_STEPS)
                pe.wait_ge(lo_ready, piece.after(0))
                if not prev:
                    pe.wait_ge(c_lo_ready, 2 * LT)
                pe.wait_ge(acc_read, g)
                up(piece, 0, ACC[1], 1)
                pe.wait_ge(acc_read, g + 1)
                up(piece, P, ACC[0], 1).then_inc(used, 1)
                b_extras(1, h, True, prev)

            def b_gate(h, prev):
                for s in range(2):
                    if s == 0:
                        pe.wait_ge(acc_read, h * 4 + (HEADS * 4 + 12))
                    project(Piece(B0 + 2 + s, h, B_STEPS), ACC[1], s, 2, h_hi, h_lo, 8 * s)
                    b_extras(2 + s, h, True, prev)

            b_up(0, False)
            b_gate(0, False)
            with pe.Fori(1, HEADS - 1) as h:
                b_up(h, True)
                b_gate(h, True)
            last_h = HEADS - 1
            b_up(last_h, True)

            def merge(i, tail):
                for s in range(M_STEPS):
                    b, k = s // 6, s % 6
                    piece = Piece(M0 + s, i, M_STEPS)
                    if tail:
                        if s == 0:
                            pe.wait_ge(acc_read, last_h * 4 + HEADS * 4 + 13)
                        if s == 4:
                            pe.wait_ge(g_lo_ready, HEADS)
                            pe.wait_ge(head_gated, 2 * HEADS)
                        if s == 5:
                            pe.wait_ge(g_lo_ready, 2 * HEADS)
                    else:
                        if k in (0, 2):
                            pe.wait_ge(sig_ready, i * 4 + (2 * b + k // 2 - 3))
                        if k == 4:
                            pe.wait_ge(part_a, i * 2 + (b - 1))
                        if k == 5:
                            pe.wait_ge(part_b, i * 2 + (b - 1))
                    if k < 4:
                        project(piece, bank[4 * b + k // 2], k % 2, 2, h_hi, h_lo, 8 * (k % 2))
                    elif k == 4:
                        project(piece, bank[4 * b + 2], 0, 1, ga_hi, ga_lo, 0)
                    else:
                        project(piece, bank[4 * b + 3], 0, 1, gb_hl[:, :, 0, :], gb_hl[:, :, 1, :], 0)
                    if tail and s < 2:
                        b_extras(s + 2, last_h, True, True)
                    elif tail and s < 5:
                        b_extras(s - 2, HEADS, False, True)

            merge(0, True)
            with pe.Fori(1, KT // 2) as i:
                merge(i, False)

            def out_chunk(c, first):
                for s in range(F_STEPS):
                    piece = Piece(FIN0 + s, c, F_STEPS)
                    pe.wait_ge(lo_ready, piece.after(0))
                    if first:
                        pe.wait_ge(mg_lo_ready, 2 * s + 2)
                        if s == 0:
                            pe.wait_ge(merged_ready, KT - 1)
                    for t in range(TOK):
                        if s == 0 and not first:
                            pe.wait_ge(x_added, c * TOK + (t - (TOK - 1)))
                        for k in range(2):
                            hi, lo = tile(piece, k * SEQ, SEQ)
                            kt = 2 * s + k
                            q = slice(t * P, (t + 1) * P)
                            last = three(bank[t][:, :], mg_hi[:, kt, q], mg_lo[:, kt, q], hi, lo,
                                         kt == 0, kt == KT - 1)
                        if s == F_STEPS - 1 and t < TOK - 1:
                            last.then_inc(chunk_done, 1)
                    last.then_inc(used, 1)
                return last

            out_chunk(0, True)
            with pe.Fori(1, N_CHUNK) as c:
                out_chunk(c, False)


_INS = ['x', 'positions', 'norm_g', 'w_in', 'lam_q1', 'lam_k1', 'lam_q2', 'lam_k2', 'a_subln_g', 'w_oa',
        'q_norm_g', 'w_uq', 'kv_norm_g', 'w_ukv', 'w_ob', 'w_out', 'final_g']


def kernel(**inputs):
    import numpy as _np
    import concourse.bacc as _bacc
    from concourse import mybir as _mybir
    from concourse.bass_utils import run_bass_kernel_spmd as _run

    consts = _np.zeros((P, 2 * P + 1), _np.float32)
    consts[:, 0:P] = _np.eye(P)
    half = B_ROPE // 2
    for m in range(P):
        low = m % B_ROPE < half
        consts[m + half if low else m - half, P + m] = -1.0 if low else 1.0
        consts[m, 2 * P] = 10000.0 ** (-(m % half) / half)

    nc = _bacc.Bacc("TRN2", target_bir_lowering=False, num_devices=1)
    arrays, args = {}, []
    for name, a in [(n, inputs[n]) for n in _INS] + [("consts", consts)]:
        a = _np.ascontiguousarray(a)
        arrays[f"in_{name}_dram"] = a
        args.append(nc.dram_tensor(f"in_{name}_dram", a.shape, _mybir.dt.from_np(a.dtype), kind="ExternalInput").ap())
    args.append(nc.dram_tensor("out_0_dram", (1, SEQ, D_MODEL), _mybir.dt.float32, kind="ExternalOutput").ap())
    hybrid_encoder(nc, *args)
    r = _run(nc, [arrays], core_ids=[0])
    return r.results[0]["out_0_dram"]
```

```python
import math
from contextlib import ExitStack

import concourse.bass as bass
from concourse import mybir

F32 = mybir.dt.float32
F32R = mybir.dt.float32r
I32 = mybir.dt.int32
ALU = mybir.AluOpType
ACT = mybir.ActivationFunctionType
AX_X = mybir.AxisListType.X

P = 128
SEQ, D_MODEL = 512, 2048
TOK = SEQ // P
KT = D_MODEL // P
HEADS = 8
A_DIM, B_NOPE, B_ROPE = 64, 128, 64
LORA = 512
LT = LORA // P
AQ, AK, AV, AG = 0, 1024, 2048, 3072
CQ, CKV, KR, BG, MG = 4096, 4608, 5120, 5184, 6208
A_SCALE = A_DIM ** -0.5
B_SCALE = (B_NOPE + B_ROPE) ** -0.5
LAM_INIT = 0.8 - 0.6 * math.exp(-0.3 * 0)
SLOPE0, SLOPE_RATIO = 2.0 ** (-8.0 / HEADS), 2.0 ** (-8.0 / HEADS)
NORM_EPS, SUBLN_EPS = 1e-6, 1e-5

SLOTS = 4
AHEAD = 2
A_STEPS, C_STEPS, B_STEPS, M_STEPS, F_STEPS = 8, 20, 4, 12, 8
C0 = HEADS * A_STEPS
B0 = C0 + C_STEPS
M0 = B0 + B_STEPS * HEADS - 2
FIN0 = M0 + M_STEPS * (KT // 2)
N_CHUNK = D_MODEL // SEQ
LAST_C = N_CHUNK - 1
EXTRAS = 4
EXTRA_PER_CHUNK = EXTRAS // (LAST_C - 1)
EXTRA_FIRST = 2
LAST_RING = F_STEPS - EXTRAS
LAST0 = FIN0 + F_STEPS * LAST_C
PIECES = LAST0 + LAST_RING

GATED_AT = [(0, 1, 2), (3, 4, 5), (6, 7, 8, 9), (12,), (10, 11, 13, 14, 15), ()] + [()] * (M_STEPS - 6)

TWO_PI_1 = 6.28125
TWO_PI_2 = 1.93500518798828125e-3
TWO_PI_3 = 2 * math.pi - TWO_PI_1 - TWO_PI_2
GATED_ORDER = [head for step in GATED_AT for head in step]
X_AHEAD = 3
EARLY_SPLIT = {4: AHEAD, 10: AHEAD + 1}
ROUND_1 = 1.5 * 2.0 ** 23
ROUND_2048 = 1.5 * 2.0 ** 34
PI_DOWN = 3.1415925

FINAL_A = 2 * SEQ
FINAL_STORES = [(1, 1, slice(3 * SEQ, 4 * SEQ)), (0, 1, slice(0, FINAL_A)), (1, 2, slice(FINAL_A, 3 * SEQ))]


EXTRA_AT = (1, 3)


class Piece:

    def __init__(self, first, loop=0, stride=0):
        self.first = first
        self.slot = first % SLOTS
        self.n = loop * stride + first
        self.turn = loop * (stride // SLOTS) + first // SLOTS

    def after(self, k):
        return self.n + (k + 1)


def hybrid_encoder(nc, x, positions, norm_g, w_in, lam_q1, lam_k1, lam_q2, lam_k2, a_subln_g, w_oa,
                   q_norm_g, w_uq, kv_norm_g, w_ukv, w_ob, w_out, final_g, consts, out):
    ctx = ExitStack()
    with ctx:
        base = (nc.sbuf_base + 63) // 64 * 64
        KB = 1024

        def at(name, kb, shape, dt=F32):
            return nc.alloc_sbuf_tensor_at(name, shape, dt, offset=base + int(kb * KB))

        def sem(name):
            return ctx.enter_context(nc.semaphore(name))

        h_hi = at("h_hi", 0, [P, KT, SEQ], F32R)
        h_lo = at("h_lo", 32, [P, KT, SEQ], F32R)
        mg_hi = at("mg_hi", 0, [P, KT, SEQ], F32R)
        mg_lo = at("mg_lo", 32, [P, KT, SEQ], F32R)
        w_raw = at("w_raw", 64, [P, SLOTS, 1024])
        w_lo = at("w_lo", 64, [P, SLOTS, 1024], F32R)
        w_hi = at("w_hi", 80, [P, SLOTS, 1024], F32R)
        gated = at("gated", 96, [P, 2 * HEADS * SEQ])
        merged = at("merged", 96, [P, KT * SEQ])
        e_lo = at("e_lo", 96, [P, EXTRAS, 1024], F32R)
        e_raw = at("e_raw", 96, [P, EXTRAS, 1024])
        e_hi = at("e_hi", 112, [P, EXTRAS, 1024], F32R)
        c_raw = at("c_raw", 112, [P, 2 * LT, SEQ])
        dist = at("dist", 120, [P, TOK, SEQ])
        x_tok = at("x_tok", 128, [P, TOK, D_MODEL])
        c_hi = at("c_hi", 128, [P, 2 * LT, SEQ], F32R)
        c_lo = at("c_lo", 144, [P, 2 * LT, SEQ], F32R)
        ga_hi = at("ga_hi", 128, [P, HEADS, SEQ], F32R)
        ga_lo = at("ga_lo", 144, [P, HEADS, SEQ], F32R)
        gb_hl = at("gb_hl", 160, [P, HEADS, 2, SEQ], F32R)
        square_junk = at("square_junk", 160, [P, D_MODEL])
        fg = at("fg", 160, [P, D_MODEL])
        q_hl = at("q_hl", 160, [P, 2, SEQ], F32R)
        c_sq = at("c_sq", 160, [P, SEQ])
        k_hl = at("k_hl", 164, [P, 2, SEQ], F32R)
        qa = at("qa", 160, [P, 2, SEQ], F32R)
        ka = at("ka", 164, [P, 2, SEQ], F32R)
        ka_lo = at("ka_lo", 198, [P, SEQ], F32R)
        vT = at("vT", 168, [P, SEQ])
        v_hl = at("v_hl", 170, [P, 2, TOK, P], F32R)
        e = at("e", 174, [P, 2, 2, SEQ])
        e_b = at("e_b", 174, [P, 2, SEQ])
        rope_in = at("rope_in", 178, [P, SEQ])
        rope_sw = at("rope_sw", 180, [P, SEQ])
        pt = at("pt", 182, [P, 2, TOK, 2 * P], F32R)
        oT = at("oT", 190, [P, SEQ])
        eg = at("eg", 192, [P, SEQ])
        cos_t = at("cos_t", 194, [P, SEQ])
        sin_t = at("sin_t", 196, [P, SEQ])
        kr_hi = at("kr_hi", 198, [P, SEQ], F32R)
        kr_lo = at("kr_lo", 200, [P, SEQ], F32R)
        qr_hl = at("qr_hl", 202, [P, SEQ], F32R)
        sig = at("sig", 192, [P, 2, 2, SEQ])
        part = at("part", 200, [P, 2, SEQ])
        cst = at("cst", 204, [P, P + 2])
        small = at("small", 205.25, [P, 160])
        pos_i = at("pos_i", 182, [P, SEQ], I32)
        pos_f = at("pos_f", 184, [P, SEQ])
        lam_in = at("lam_in", 186, [P, 6, A_DIM])
        assert base + 207 * KB <= nc.sbuf_usable_end

        ident = cst[:, 0:P]
        inv_freq, rope_sign = cst[:, P:P + 1], cst[:, P + 1:P + 2]
        g_in = small[:, 0:KT]
        g_q, g_kv = small[:, 16:20], small[:, 20:24]
        g_sub = small[:, 24:25]
        lam = small[:, 25:26]
        ones = small[:, 26:27]
        mhalf = small[:, 27:31]
        pos_q = small[:, 31:35]
        x_ss, x_var, x_rstd = small[:, 35:39], small[:, 39:43], small[:, 43:47]
        mx, nm = small[:, 47:55], small[:, 55:63]
        sums, rs = small[:, 63:71], small[:, 71:79]
        o_var, o_rstd = small[:, 79:83], small[:, 83:87]
        c_ss, c_var, c_rstd = small[:, 87:91], small[:, 91:95], small[:, 95:99]
        f_ss = small[:, 99:115]
        f_sum, f_var, f_rstd = small[:, 115:119], small[:, 119:123], small[:, 123:127]
        lam_s, lam_e = small[:, 127:129], small[:, 129:131]
        half_pi = small[:, 131:132]
        g_sub_raw = small[:, 132:133]
        rs_lam = small[:, 133:135]
        pos_qi = at("pos_qi", 187.75, [P, TOK], I32)

        bank = [ctx.enter_context(nc.psum_tensor(f"bank{i}", [P, SEQ], F32)) for i in range(8)]
        ACC = bank[0:2]
        SC = bank[2:6]
        TR = bank[6]
        OB = bank[7]

        landed = [sem(f"landed{i}") for i in range(SLOTS)]
        hi_ready = sem("hi_ready")
        lo_ready = sem("lo_ready")
        extra_in = [sem(f"extra_in{j}") for j in range(EXTRA_PER_CHUNK)]
        extra_hi, extra_lo = sem("extra_hi"), sem("extra_lo")
        used = sem("used")
        gains_in, lambdas_in = sem("gains_in"), sem("lambdas_in")
        x_in = [sem(f"x_in{t}") for t in range(TOK)]
        pos_in, cst_in = sem("pos_in"), sem("cst_in")
        ones_set = sem("ones_set")
        v_chain = sem("v_chain")
        a_chain = sem("a_chain")
        lam_sum, lam_exp = sem("lam_sum"), sem("lam_exp")
        angle_ready, trig_ready = sem("angle_ready"), sem("trig_ready")
        x_ss_ready, x_var_ready, x_rstd_ready, x_normed = (
            sem("x_ss_ready"), sem("x_var_ready"), sem("x_rstd_ready"), sem("x_normed"))
        x_turned, h_hi_ready, h_lo_ready = sem("x_turned"), sem("h_hi_ready"), sem("h_lo_ready")
        dist_ready, dist_halved = sem("dist_ready"), sem("dist_halved")
        proj_hi = sem("proj_hi")
        acc_read = sem("acc_read")
        gate_exp, silu_add, silu_inv, silu_done = sem("gate_exp"), sem("silu_add"), sem("silu_inv"), sem("silu_done")
        v_turned, v_hi_ready, v_lo_ready = sem("v_turned"), sem("v_hi_ready"), sem("v_lo_ready")
        scored = sem("scored")
        max_taken = sem("max_taken")
        bias_ready = sem("bias_ready")
        exp_done = sem("exp_done")
        inv_ready, inv_lam_ready, e2_scaled, p_ready = (
            sem("inv_ready"), sem("inv_lam_ready"), sem("e2_scaled"), sem("p_ready"))
        p_turned, pt_hi_ready, pt_lo_ready = sem("p_turned"), sem("pt_hi_ready"), sem("pt_lo_ready")
        pv_done = sem("pv_done")
        o_squared, o_copied, o_summed, o_var_ready, o_rstd_ready, o_spread, o_normed, head_gated = (
            sem("o_squared"), sem("o_copied"), sem("o_summed"), sem("o_var_ready"), sem("o_rstd_ready"),
            sem("o_spread"), sem("o_normed"), sem("head_gated"))
        c_squared, c_summed, c_ss_ready, c_var_ready, c_rstd_ready, c_spread, c_scaled, c_hi_ready, c_lo_ready = (
            sem("c_squared"), sem("c_summed"), sem("c_ss_ready"), sem("c_var_ready"), sem("c_rstd_ready"),
            sem("c_spread"), sem("c_scaled"), sem("c_hi_ready"), sem("c_lo_ready"))
        k_up = sem("k_up")
        rope_up = sem("rope_up")
        rope_shifted, rope_cos, rope_sin, rope_done, rope_hi, rope_lo = (
            sem("rope_shifted"), sem("rope_cos"), sem("rope_sin"), sem("rope_done"), sem("rope_hi"), sem("rope_lo"))
        g_hi_ready, g_lo_ready = sem("g_hi_ready"), sem("g_lo_ready")
        sig_ready, part_a, part_b, merged_ready = sem("sig_ready"), sem("part_a"), sem("part_b"), sem("merged_ready")
        mg_hi_ready, mg_lo_ready = sem("mg_hi_ready"), sem("mg_lo_ready")
        x_again, fg_in = sem("x_again"), sem("fg_in")
        chunk_done, x_added, f_squared, f_sum_ready, f_var_ready, f_rstd_ready, stored = (
            sem("chunk_done"), sem("x_added"), sem("f_squared"), sem("f_sum_ready"), sem("f_var_ready"),
            sem("f_rstd_ready"), sem("stored"))
        gained = sem("gained")
        scaled_a, scaled_v = sem("scaled_a"), sem("scaled_v")

        LOW, HIGH = slice(0, 64), slice(64, P)
        BH = HEADS
        ROPES = HEADS + 1

        def tile_no(head, t):
            return head * TOK + (t + 1)

        block = ctx.enter_context(nc.Block())

        @block.sync
        def _(sp):
            def load(piece, parts):
                if not isinstance(piece.n, int) or piece.n >= SLOTS:
                    sp.wait_ge(used, piece.n - (SLOTS - 1))
                    sp.nop(nofuse=True)
                for dst, src in parts:
                    sp.dma_start(dst, src).then_inc(landed[piece.slot], 16)

            def rows(w, r0, n, col, width):
                return w[0, r0 * P:(r0 + n) * P, bass.ds(col, width)].rearrange("(k p) c -> p k c", p=P)

            def block_piece(piece, w, r0, col):
                raw = w_raw[:, piece.slot, :].rearrange("p (k c) -> p k c", k=8)
                load(piece, [(raw[:, 4 * j:4 * j + 4, :], rows(w, r0 + 4 * j, 4, col, P)) for j in range(2)])

            def a_head(h, steps=range(A_STEPS)):
                for s in steps:
                    block_piece(Piece(s, h, A_STEPS), w_in, 8 * (s % 2), h * P + (AQ, AK, AV, AG)[s // 2])

            def up_pieces(h):
                piece = Piece(B0, h, B_STEPS)
                raw = w_raw[:, piece.slot, :].rearrange("p (k c) -> p k c", k=LT)
                width = B_NOPE + B_ROPE
                load(piece, [(raw[:, :, 0:width], rows(w_uq, 0, LT, h * width, width)),
                             (raw[:, :, width:2 * P], rows(w_uq, 0, LT, h * width + B_NOPE, B_ROPE))])
                piece = Piece(B0 + 1, h, B_STEPS)
                raw = w_raw[:, piece.slot, :].rearrange("p (k c) -> p k c", k=LT)
                load(piece, [(raw[:, 2 * j:2 * j + 2, :], rows(w_ukv, 2 * j, 2, h * (2 * P), 2 * P))
                             for j in range(2)])

            def merge_blocks(i):
                for b in range(2):
                    col = i * (2 * P) + b * P
                    for s in range(4):
                        block_piece(Piece(M0 + 6 * b + s, i, M_STEPS), w_in, 8 * (s % 2),
                                    col + (MG if s < 2 else MG + D_MODEL))
                    block_piece(Piece(M0 + 6 * b + 4, i, M_STEPS), w_oa, 0, col)
                    block_piece(Piece(M0 + 6 * b + 5, i, M_STEPS), w_ob, 0, col)

            def out_parts(dst, s, col):
                raw = dst.rearrange("p (k c) -> p k c", k=2)
                return [(raw[:, j:j + 1, :], rows(w_out, 2 * s + j, 1, col, SEQ)) for j in range(2)]

            def residual(c):
                sp.dma_start(x_tok[:, :, bass.ds(c * SEQ, SEQ)],
                             x[0, :, bass.ds(c * SEQ, SEQ)].rearrange("(t p) c -> p t c", p=P)
                             ).then_inc(x_again, 16)

            def out_chunk(c):
                for s in range(F_STEPS):
                    piece = Piece(FIN0 + s, c, F_STEPS)
                    load(piece, out_parts(w_raw[:, piece.slot, :], s, c * SEQ))
                    if isinstance(c, int) and s == 3:
                        sp.dma_start(fg[:, :], final_g.rearrange("(a d) -> a d", a=1).broadcast_to([P, D_MODEL])
                                     ).then_inc(fg_in, 16)
                    if s == 4:
                        residual(c)
                    if not isinstance(c, int) and s in EXTRA_AT:
                        j = EXTRA_AT.index(s)
                        if s == EXTRA_AT[0]:
                            sp.wait_ge(mg_lo_ready, KT)
                            sp.nop(nofuse=True)
                        n = c * EXTRA_PER_CHUNK + (j - EXTRA_PER_CHUNK)
                        for k in range(2):
                            sp.dma_start(e_raw[:, bass.ds(n, 1), k * SEQ:(k + 1) * SEQ],
                                         w_out[0, bass.ds(n * (2 * P) + (2 * EXTRA_FIRST + k) * P, P),
                                               LAST_C * SEQ:D_MODEL].rearrange("(k p) c -> p k c", p=P)
                                         ).then_inc(extra_in[j], 16)

            def last_chunk():
                for i in range(LAST_RING):
                    piece = Piece(LAST0 + i)
                    load(piece, out_parts(w_raw[:, piece.slot, :], i if i < EXTRA_FIRST else i + EXTRAS,
                                          LAST_C * SEQ))
                residual(LAST_C)

            for t in range(TOK):
                sp.dma_start(x_tok[:, t, :], x[0, t * P:(t + 1) * P, :]).then_inc(x_in[t], 16)
            sp.dma_start(cst[:, :], consts[:, :]).then_inc(cst_in, 16)
            with nc.allow_non_contiguous_dma("gains by partition"):
                for dst, src in ((g_in, norm_g), (g_q, q_norm_g), (g_kv, kv_norm_g), (g_sub_raw, a_subln_g)):
                    sp.dma_start(dst, src[0, :].rearrange("(t p) -> p t", p=P)).then_inc(gains_in, 16)
            a_head(0, range(SLOTS))
            sp.dma_start(pos_i[:, :], positions.broadcast_to([P, SEQ])).then_inc(pos_in, 16)
            with nc.allow_non_contiguous_dma("positions by partition"):
                sp.dma_start(pos_qi[:, :], positions[0, :].rearrange("(t p) -> p t", p=P)).then_inc(pos_in, 16)
            for i, src in enumerate((lam_q1, lam_k1, lam_q2, lam_k2)):
                sp.dma_start(lam_in[:, i, :], src.broadcast_to([P, A_DIM])).then_inc(lambdas_in, 16)
            a_head(0, range(SLOTS, A_STEPS))
            with sp.Fori(1, HEADS) as h:
                a_head(h)
            for b in range(2 * LT):
                for s in range(2):
                    block_piece(Piece(C0 + 2 * b + s), w_in, 8 * s, CQ + b * P)
            for s in range(2):
                piece = Piece(C0 + 4 * LT + s)
                raw = w_raw[:, piece.slot, :].rearrange("p (k c) -> p k c", k=8)
                load(piece, [(raw[:, :, j * B_ROPE:(j + 1) * B_ROPE], rows(w_in, 8 * s, 8, KR, B_ROPE))
                             for j in range(2)])
            for s in range(2):
                block_piece(Piece(C0 + 4 * LT + 2 + s), w_in, 8 * s, BG)
            up_pieces(0)
            with sp.Fori(1, HEADS) as h:
                for s in range(2):
                    block_piece(Piece(B0 - 2 + s, h, B_STEPS), w_in, 8 * s, h * P + BG)
                up_pieces(h)
            with sp.Fori(0, KT // 2) as i:
                merge_blocks(i)
            out_chunk(0)
            with sp.Fori(1, LAST_C) as c:
                out_chunk(c)
            last_chunk()
            for t in range(TOK):
                for ready, n, cols in FINAL_STORES:
                    sp.wait_ge((scaled_a, scaled_v)[ready], t * (1, 2)[ready] + n)
                    sp.dma_start(out[0, t * P:(t + 1) * P, cols], x_tok[:, t, cols]).then_inc(stored, 16)
            sp.wait_ge(stored, 16 * TOK * len(FINAL_STORES))

        @block.gpsimd
        def _(pool):
            pool.memset(ones, 1.0).then_inc(ones_set, 1)
            pool.memset(mhalf, -0.5).then_inc(ones_set, 1)
            pool.memset(half_pi, math.pi / 2).then_inc(ones_set, 1)
            pool.wait_ge(ones_set, 3)

            def rsqrt(dst, src, ready, n, done):
                pool.wait_ge(ready, n)
                pool.tensor_tensor(dst, src, mhalf[:, 0:src.shape[1]], ALU.pow).then_inc(done, 1)

            for t in range(TOK):
                rsqrt(x_rstd[:, t:t + 1], x_var[:, t:t + 1], x_var_ready, t + 1, x_rstd_ready)

            def halve(h, t):
                pool.wait_ge(max_taken, tile_no(h, t))
                pool.nop(nofuse=True)
                pool.tensor_scalar(dist[:, t, :], dist[:, t, :], SLOPE_RATIO, 1.0, ALU.mult, ALU.mult
                                   ).then_inc(dist_halved, 1)

            for t in range(3):
                halve(0, t)
            with pool.Fori(1, HEADS) as h:
                halve(h - 1, 3)
                rsqrt(o_rstd, o_var, o_var_ready, h, o_rstd_ready)
                for t in range(3):
                    halve(h, t)
            rsqrt(o_rstd, o_var, o_var_ready, HEADS, o_rstd_ready)
            for i in range(2):
                rsqrt(c_rstd, c_var, c_var_ready, i + 1, c_rstd_ready)
            for t in range(TOK):
                rsqrt(f_rstd[:, t:t + 1], f_var[:, t:t + 1], f_var_ready, t + 1, f_rstd_ready)

        @block.scalar
        def _(act):
            def split_hi(piece):
                act.wait_ge(landed[piece.slot], (piece.turn + 1) * 32)
                act.activation(w_hi[:, piece.slot, :], w_raw[:, piece.slot, :], ACT.Copy).then_inc(hi_ready, 1)

            def proj_split_hi(dst, src, piece_end, n_use, use_sem):
                act.wait_ge(used, piece_end)
                if use_sem is not None:
                    act.wait_ge(use_sem, n_use)
                act.activation(dst, src, ACT.Copy).then_inc(proj_hi, 1)

            def pt_hi(head, t, src):
                act.wait_ge(p_turned, tile_no(head, t))
                if t >= 2:
                    act.wait_ge(pv_done, head * 2 + 1)
                act.activation(pt[:, 0, :, (t % 2) * P:(t % 2 + 1) * P],
                               src[:, :].rearrange("p (k c) -> p k c", k=TOK), ACT.Copy).then_inc(pt_hi_ready, 1)

            def exp_a(head, t):
                act.wait_ge(bias_ready, tile_no(head, t))
                for m in range(2):
                    b = 2 * (t % 2) + m
                    last = act.activation(e[:, t % 2, m, :], e[:, t % 2, m, :], ACT.Exp, bias=nm[:, b:b + 1],
                                          scale=A_SCALE, accum_out=sums[:, b:b + 1])
                last.then_inc(exp_done, 1)

            def exp_b(head, t, first):
                act.wait_ge(bias_ready, tile_no(head, t))
                if not first or t >= 2:
                    act.wait_ge(p_turned, tile_no(head, t) - 2)
                act.activation(e_b[:, t % 2, :], SC[t][:, :], ACT.Exp, bias=nm[:, t:t + 1], scale=B_SCALE,
                               accum_out=sums[:, t:t + 1]).then_inc(exp_done, 1)

            def gate(head, piece_end, bank_, first):
                act.wait_ge(used, piece_end)
                if not first:
                    act.wait_ge(silu_done, head)
                act.activation(eg[:, :], bank_[:, :], ACT.Exp, scale=-1.0).then_inc(gate_exp, 1)

            def v_hi(head, src):
                act.wait_ge(v_turned, head + 1)
                act.activation(v_hl[:, 0, :, :], src[:, :].rearrange("p (t c) -> p t c", t=TOK), ACT.Copy
                               ).then_inc(v_hi_ready, 1)

            def rope_tables():
                act.wait_ge(angle_ready, 1)
                act.activation(sin_t[:, :], cos_t[:, :], ACT.Sin).then_inc(trig_ready, 1)
                act.activation(eg[:, :], cos_t[:, :], ACT.Abs).then_inc(a_chain, 1)
                act.wait_ge(a_chain, 1)
                act.activation(cos_t[:, :], eg[:, :], ACT.Sin, scale=-1.0, bias=half_pi).then_inc(trig_ready, 1)

            act.wait_ge(ones_set, 3)
            for t in range(TOK):
                act.wait_ge(x_in[t], 16)
                if t:
                    act.wait_ge(x_ss_ready, t)
                act.activation(square_junk[:, :], x_tok[:, t, :], ACT.Square, accum_out=x_ss[:, t:t + 1]
                               ).then_inc(x_ss_ready, 1)
            for n in range(AHEAD):
                split_hi(Piece(n))
            act.wait_ge(gains_in, 16 * 4)
            for k in range(KT):
                if k in EARLY_SPLIT:
                    split_hi(Piece(EARLY_SPLIT[k]))
                act.wait_ge(x_turned, k + 1)
                act.activation(h_hi[:, k, :], bank[2 + k % 6][:, :], ACT.Copy, scale=g_in[:, k:k + 1]
                               ).then_inc(h_hi_ready, 1)

            def a_step(s, h, cur, prev, first=False):
                if s == 0 and prev:
                    pt_hi(h - 1, 1, TR)
                    exp_a(h - 1, 3)
                    gate(h - 1, (h - 1) * A_STEPS + 8, ACC[1], first)
                if s == 1 and prev:
                    pt_hi(h - 1, 2, TR)
                if s == 2 and prev:
                    pt_hi(h - 1, 3, TR)
                if s == 2 and cur:
                    act.wait_ge(used, h * A_STEPS + 2)
                    if prev:
                        act.wait_ge(scored, tile_no(h, 0) - 1)
                    for m, own in enumerate((LOW, HIGH)):
                        last = act.activation(qa[own, m, :], ACC[0][own, :], ACT.Copy)
                    last.then_inc(proj_hi, 1)
                if s == 3 and prev:
                    act.wait_ge(pv_done, h * 2)
                    act.activation(vT[:, :], OB[:, :], ACT.Square).then_inc(o_squared, 1)
                if s == 4 and cur:
                    act.wait_ge(used, h * A_STEPS + 4)
                    if prev:
                        act.wait_ge(scored, tile_no(h, 0) - 1)
                    for m, own in enumerate((LOW, HIGH)):
                        for half in (LOW, HIGH):
                            last = act.activation(ka[half, m, :], ACC[1][own, :], ACT.Copy)
                    last.then_inc(proj_hi, 1)
                if s == 5 and cur:
                    exp_a(h, 0)
                if s == 6 and cur:
                    exp_a(h, 1)
                if s == 7 and cur:
                    pt_hi(h, 0, TR)
                    v_hi(h, OB)
                    exp_a(h, 2)

            for s in range(A_STEPS):
                if s >= AHEAD:
                    split_hi(Piece(s + AHEAD))
                if s == 0:
                    act.wait_ge(lam_sum, 2)
                    act.activation(lam_e, lam_s, ACT.Exp).then_inc(lam_exp, 1)
                a_step(s, 0, True, False)
            for s in range(A_STEPS):
                split_hi(Piece(A_STEPS + s + AHEAD))
                a_step(s, 1, True, True, True)
            with act.Fori(2, HEADS) as h:
                for s in range(A_STEPS):
                    split_hi(Piece(s + AHEAD, h, A_STEPS))
                    a_step(s, h, True, True)

            def c_hi_of(i):
                act.wait_ge(c_scaled, i + 1)
                act.activation(c_hi[:, i, :], c_raw[:, i, :], ACT.Copy).then_inc(c_hi_ready, 1)

            def rope_shift(i, src):
                if not isinstance(i, int) or i > 0:
                    act.wait_ge(rope_done, i)
                for q in range(4):
                    d = (q ^ 1) * 32
                    last = act.activation(rope_sw[d:d + 32, :], src[q * 32:q * 32 + 32, :], ACT.Copy)
                last.then_inc(rope_shifted, 1)

            def rope_his(i):
                act.wait_ge(rope_done, i + 1)
                if i == 0:
                    act.activation(kr_hi[:, :], rope_in[:, :], ACT.Copy).then_inc(rope_hi, 1)

            for s in range(C_STEPS):
                split_hi(Piece(C0 + s + AHEAD))
                if s < 6:
                    a_step(s, HEADS, False, True)
                if s == 9:
                    rope_tables()
                b = s // 2 - 1
                if s % 2 == 0 and 0 <= b < 2 * LT:
                    act.wait_ge(acc_read, HEADS * 4 + b + 1)
                    if b:
                        act.wait_ge(c_summed, b)
                    act.activation(c_sq[:, :], c_raw[:, b, :], ACT.Square).then_inc(c_squared, 1)
                if s in (10, 11):
                    for i in range(2):
                        c_hi_of(2 * (s - 10) + i)
                if s in (18, 19):
                    for i in range(2):
                        c_hi_of(LT + 2 * (s - 18) + i)
                if s == 18:
                    act.wait_ge(used, C0 + 18)
                    rope_shift(0, ACC[0])
                if s == 19:
                    rope_his(0)

            def b_step(s, h, cur, prev):
                H = h + BH
                if s == 0 and cur:
                    gate(H, h * B_STEPS + B0, ACC[1], False)
                if s == 0 and prev:
                    exp_b(H - 1, 2, False)
                    exp_b(H - 1, 3, False)
                    pt_hi(H - 1, 0, SC[0])
                    pt_hi(H - 1, 1, SC[1])
                if s == 1 and cur:
                    proj_split_hi(q_hl[:, 0, :], ACC[0][:, :], h * B_STEPS + (B0 + 1),
                                  tile_no(H, 0) - 1 if prev else 2 * LT, scored if prev else c_summed)
                if s == 1 and prev:
                    pt_hi(H - 1, 2, SC[2])
                    pt_hi(H - 1, 3, SC[3])
                if s == 1 and cur:
                    act.wait_ge(rope_up, h + 1)
                    rope_shift(h + 1, TR)
                    act.wait_ge(k_up, h + 1)
                    act.wait_ge(scored, tile_no(H, 0) - 1)
                    act.activation(k_hl[:, 0, :], ACC[1][:, :], ACT.Copy).then_inc(proj_hi, 1)
                if s == 2 and cur:
                    act.wait_ge(rope_done, h + 2)
                    if prev:
                        act.wait_ge(scored, tile_no(H, 0) - 1)
                    act.activation(kr_lo[64:P, :], rope_in[64:P, :], ACT.Copy).then_inc(rope_hi, 1)
                    act.activation(qr_hl[0:64, :], rope_in[0:64, :], ACT.Copy).then_inc(rope_hi, 1)
                if s == 3 and cur:
                    exp_b(H, 0, False)
                    exp_b(H, 1, False)
                    v_hi(H, TR)

            for s in range(B_STEPS):
                split_hi(Piece(B0 + s + AHEAD))
                b_step(s, 0, True, False)
            with act.Fori(1, HEADS - 1) as h:
                for s in range(B_STEPS):
                    split_hi(Piece(B0 + s + AHEAD, h, B_STEPS))
                    b_step(s, h, True, True)
            last = HEADS - 1
            for s in range(2):
                split_hi(Piece(B0 + B_STEPS * last + s + AHEAD))
                b_step(s, last, True, True)

            def sigmoid(i, b, branch):
                first = M0 + 6 * b + 2 * branch + 2
                act.wait_ge(used, i * M_STEPS + first)
                act.activation(sig[:, b, branch, :], bank[(0, 4)[b] + branch][:, :], ACT.Sigmoid
                               ).then_inc(sig_ready, 1)

            def merge_step(s, i):
                if s in (2, 4, 8, 10):
                    b = s // 6
                    if s % 6 == 2 and not isinstance(i, int):
                        act.wait_ge(merged_ready, i * 2 + (b - 1))
                    sigmoid(i, b, (s % 6) // 4)

            def gated_hi(head):
                act.wait_ge(head_gated, head + 1)
                dst = ga_hi[:, head, :] if head < HEADS else gb_hl[:, head - HEADS, 0, :]
                act.activation(dst, gated[:, head * SEQ:(head + 1) * SEQ], ACT.Copy).then_inc(g_hi_ready, 1)

            for s in range(M_STEPS):
                split_hi(Piece(M0 + s + AHEAD))
                if s < 2:
                    b_step(s + 2, last, True, True)
                elif s < 5:
                    b_step(s - 2, HEADS, False, True)
                if s == 0:
                    act.wait_ge(used, M0)
                if s == 2:
                    act.wait_ge(scored, tile_no(2 * HEADS - 1, 3))
                    act.wait_ge(silu_done, 2 * HEADS)
                if s == 3:
                    act.wait_ge(p_turned, tile_no(2 * HEADS - 1, 3))
                if s == 4:
                    act.wait_ge(pv_done, 4 * HEADS)
                for head in GATED_AT[s]:
                    gated_hi(head)
                merge_step(s, 0)
            with act.Fori(1, KT // 2) as i:
                for s in range(M_STEPS):
                    split_hi(Piece(M0 + s + AHEAD, i, M_STEPS))
                    merge_step(s, i)

            def extra_split_hi(c, s):
                j = EXTRA_AT.index(s - 2)
                act.wait_ge(extra_in[j], c * 32)
                n = c * EXTRA_PER_CHUNK + (j - EXTRA_PER_CHUNK)
                act.activation(e_hi[:, bass.ds(n, 1), :], e_raw[:, bass.ds(n, 1), :], ACT.Copy).then_inc(extra_hi, 1)

            def merged_hi(j):
                act.wait_ge(merged_ready, j + 1)
                if j == 0:
                    act.wait_ge(used, FIN0 - 2)
                act.activation(mg_hi[:, j, :], merged[:, j * SEQ:(j + 1) * SEQ], ACT.Copy).then_inc(mg_hi_ready, 1)

            def chunk_square(c, t):
                act.wait_ge(x_added, c * TOK + (t + 1))
                if not (isinstance(c, int) and c == 0 and t == 0):
                    act.wait_ge(f_squared, c * TOK + t)
                act.activation(eg[:, :], x_tok[:, t, bass.ds(c * SEQ, SEQ)], ACT.Square,
                               accum_out=f_ss[:, bass.ds(c * TOK + t, 1)]).then_inc(f_squared, 1)

            def chunk_squares(c):
                for t in range(TOK):
                    chunk_square(c, t)

            def scale_a(t):
                act.wait_ge(f_rstd_ready, t + 1)
                act.activation(x_tok[:, t, 0:FINAL_A], x_tok[:, t, 0:FINAL_A], ACT.Copy, scale=f_rstd[:, t:t + 1]
                               ).then_inc(scaled_a, 1)

            for j in range(4):
                merged_hi(j)
            for s in range(F_STEPS):
                split_hi(Piece(FIN0 + s + AHEAD))
                for j in (4 + 2 * s, 5 + 2 * s):
                    if j < KT:
                        merged_hi(j)
            chunk_squares(0)
            with act.Fori(1, LAST_C) as c:
                for s in range(F_STEPS):
                    split_hi(Piece(FIN0 + s + AHEAD, c, F_STEPS))
                    if s - 2 in EXTRA_AT:
                        extra_split_hi(c, s)
                chunk_squares(c)
            for i in range(AHEAD, LAST_RING):
                split_hi(Piece(LAST0 + i))
            for t in range(TOK):
                chunk_square(LAST_C, t)
                scale_a(t)

        @block.vector
        def _(dve):
            chain = [0]

            def link(ins):
                chain[0] += 1
                ins.then_inc(v_chain, 1)
                dve.wait_ge(v_chain, chain[0])

            def split_lo(piece):
                dve.wait_ge(hi_ready, piece.after(0))
                dve.tensor_tensor(w_lo[:, piece.slot, :], w_raw[:, piece.slot, :],
                                  w_hi[:, piece.slot, :].bitcast(F32), ALU.subtract).then_inc(lo_ready, 1)

            def proj_split_lo(dst, src, n):
                dve.wait_ge(proj_hi, n)
                dve.tensor_tensor(dst[:, 1, :], src[:, :], dst[:, 0, :].bitcast(F32), ALU.subtract
                                  ).then_inc(acc_read, 1)

            def pt_lo(head, t, src):
                dve.wait_ge(pt_hi_ready, tile_no(head, t))
                c = slice((t % 2) * P, (t % 2 + 1) * P)
                dve.tensor_tensor(pt[:, 1, :, c], src[:, :].rearrange("p (k c) -> p k c", k=TOK),
                                  pt[:, 0, :, c].bitcast(F32), ALU.subtract).then_inc(pt_lo_ready, 1)

            def max_a(head, t, first):
                n = tile_no(head, t)
                dve.wait_ge(scored, n)
                if not first:
                    dve.wait_ge(dist_halved, n - TOK)
                if not first or t >= 2:
                    dve.wait_ge(p_turned, n - 2)
                dve.nop(nofuse=True)
                for m in range(2):
                    b = 2 * (t % 2) + m
                    last = dve.tensor_tensor_reduce(out=e[:, t % 2, m, :], in0=SC[b][:, :], in1=dist[:, t, :],
                                                    scale=1.0, scalar=-3.0e38, op0=ALU.add, op1=ALU.max,
                                                    accum_out=mx[:, b:b + 1])
                last.then_inc(max_taken, 1)
                dve.wait_ge(max_taken, n)
                b = 2 * (t % 2)
                dve.tensor_scalar(nm[:, b:b + 2], mx[:, b:b + 2], -A_SCALE, None, ALU.mult).then_inc(bias_ready, 1)

            def norm_a(head, t):
                n = tile_no(head, t)
                b = 2 * (t % 2)
                dve.wait_ge(exp_done, n)
                dve.reciprocal(rs[:, b:b + 2], sums[:, b:b + 2]).then_inc(inv_ready, 1)
                dve.wait_ge(inv_ready, n)
                dve.tensor_scalar(rs_lam[:, t % 2:t % 2 + 1], rs[:, b + 1:b + 2], lam, None, ALU.mult
                                  ).then_inc(inv_lam_ready, 1)
                dve.wait_ge(inv_lam_ready, n)
                dve.tensor_scalar(e[:, t % 2, 1, :], e[:, t % 2, 1, :], rs_lam[:, t % 2:t % 2 + 1], None, ALU.mult
                                  ).then_inc(e2_scaled, 1)
                dve.wait_ge(e2_scaled, n)
                dve.scalar_tensor_tensor(e[:, t % 2, 0, :], e[:, t % 2, 0, :], rs[:, b:b + 1], e[:, t % 2, 1, :],
                                         ALU.mult, ALU.subtract).then_inc(p_ready, 1)

            def max_b(head, t):
                n = tile_no(head, t)
                dve.wait_ge(scored, n)
                dve.reduce_max(mx[:, t:t + 1], SC[t][:, :], AX_X).then_inc(max_taken, 1)
                dve.wait_ge(max_taken, n)
                dve.tensor_scalar(nm[:, t:t + 1], mx[:, t:t + 1], -B_SCALE, None, ALU.mult).then_inc(bias_ready, 1)

            def norm_b(head, t):
                n = tile_no(head, t)
                dve.wait_ge(exp_done, n)
                dve.reciprocal(rs[:, t:t + 1], sums[:, t:t + 1]).then_inc(inv_ready, 1)
                dve.wait_ge(inv_ready, n)
                dve.tensor_scalar(e_b[:, t % 2, :], e_b[:, t % 2, :], rs[:, t:t + 1], None, ALU.mult
                                  ).then_inc(p_ready, 1)

            def gate_of(head):
                return gated[:, bass.ds(head * SEQ, SEQ)]

            def gate_copy(head, src):
                dve.wait_ge(gate_exp, head + 1)
                dve.tensor_copy(gate_of(head), src[:, :]).then_inc(acc_read, 1)

            def silu_half(head, half):
                if half == 0:
                    dve.wait_ge(gate_exp, head + 1)
                    dve.tensor_scalar(eg[:, :], eg[:, :], 1.0, None, ALU.add).then_inc(silu_add, 1)
                    dve.wait_ge(silu_add, head + 1)
                c = slice(half * (SEQ // 2), (half + 1) * (SEQ // 2))
                dve.reciprocal(eg[:, c], eg[:, c]).then_inc(silu_inv, 1)

            def silu_mult(head, n_copy):
                dve.wait_ge(silu_inv, head * 2 + 2)
                dve.wait_ge(acc_read, n_copy)
                dve.tensor_tensor(gate_of(head), gate_of(head), eg[:, :], ALU.mult).then_inc(silu_done, 1)

            def v_lo(head, src):
                dve.wait_ge(v_hi_ready, head + 1)
                dve.tensor_tensor(v_hl[:, 1, :, :], src[:, :].rearrange("p (t c) -> p t c", t=TOK),
                                  v_hl[:, 0, :, :].bitcast(F32), ALU.subtract).then_inc(v_lo_ready, 1)

            def rope_angles():
                r, n1, n0 = cos_t, sin_t, eg
                link(dve.tensor_scalar(n0[:, :], r[:, :], 1.0 / (2.0 * math.pi), ROUND_1, ALU.mult, ALU.add))
                link(dve.tensor_scalar(n0[:, :], n0[:, :], -ROUND_1, None, ALU.add))
                link(dve.tensor_scalar(n1[:, :], n0[:, :], ROUND_2048, -ROUND_2048, ALU.add, ALU.add))
                link(dve.tensor_tensor(n0[:, :], n0[:, :], n1[:, :], ALU.subtract))
                for part_2pi in (TWO_PI_1, TWO_PI_2, TWO_PI_3):
                    for n in (n1, n0):
                        link(dve.scalar_tensor_tensor(r[:, :], n[:, :], -part_2pi, r[:, :], ALU.mult, ALU.add))
                dve.tensor_scalar(r[:, :], r[:, :], PI_DOWN, -PI_DOWN, ALU.min, ALU.max).then_inc(angle_ready, 1)

            for t in range(TOK):
                dve.wait_ge(x_ss_ready, t + 1)
                dve.tensor_scalar(x_var[:, t:t + 1], x_ss[:, t:t + 1], 1.0 / D_MODEL, NORM_EPS, ALU.mult, ALU.add
                                  ).then_inc(x_var_ready, 1)
                dve.wait_ge(x_rstd_ready, t + 1)
                dve.tensor_scalar(x_tok[:, t, :], x_tok[:, t, :], x_rstd[:, t:t + 1], None, ALU.mult
                                  ).then_inc(x_normed, 1)
            for n in range(AHEAD):
                split_lo(Piece(n))
            dve.wait_ge(gains_in, 16 * 4)
            for k in range(KT):
                if k in EARLY_SPLIT:
                    split_lo(Piece(EARLY_SPLIT[k]))
                dve.wait_ge(h_hi_ready, k + 1)
                dve.scalar_tensor_tensor(h_lo[:, k, :], bank[2 + k % 6][:, :], g_in[:, k:k + 1],
                                         h_hi[:, k, :].bitcast(F32), ALU.mult, ALU.subtract
                                         ).then_inc(h_lo_ready, 1)
            dve.wait_ge(pos_in, 32)
            dve.wait_ge(cst_in, 16)
            dve.wait_ge(lambdas_in, 16 * 4)
            link(dve.tensor_copy(pos_f[:, :], pos_i[:, :]))
            link(dve.tensor_copy(pos_q, pos_qi[:, :]))
            link(dve.tensor_scalar(cos_t[:, :], pos_f[:, :], inv_freq, None, ALU.mult))
            for i in range(2):
                dve.tensor_tensor_reduce(out=lam_in[:, 4 + i, :], in0=lam_in[:, 2 * i, :],
                                              in1=lam_in[:, 2 * i + 1, :], scale=1.0, scalar=0.0,
                                              op0=ALU.mult, op1=ALU.add, accum_out=lam_s[:, i:i + 1]).then_inc(lam_sum, 1)
            link(dve.tensor_scalar(g_sub, g_sub_raw, 1.0 - LAM_INIT, None, ALU.mult))
            for t in range(TOK):
                link(dve.tensor_scalar(dist[:, t, :], pos_f[:, :], pos_q[:, t:t + 1], SLOPE0 / A_SCALE,
                                       ALU.subtract, ALU.mult))
                link(dve.scalar_tensor_tensor(dist[:, t, :], dist[:, t, :], -1.0, dist[:, t, :], ALU.mult, ALU.min))
            dve.wait_ge(lam_exp, 1)
            link(dve.tensor_scalar(lam, lam_e[:, 0:1], lam_e[:, 1:2], LAM_INIT, ALU.subtract, ALU.add))

            def a_step(s, h, cur, prev, first=False):
                if s == 0 and prev:
                    pt_lo(h - 1, 1, TR)
                    norm_a(h - 1, 2)
                    max_a(h - 1, 3, first)
                    gate_copy(h - 1, ACC[1])
                if s == 1 and prev:
                    pt_lo(h - 1, 2, TR)
                    norm_a(h - 1, 3)
                    silu_half(h - 1, 0)
                if s == 2 and prev:
                    pt_lo(h - 1, 3, TR)
                if s == 2 and cur:
                    dve.wait_ge(proj_hi, h * 2 + 1)
                    for m, (own, other) in enumerate(((LOW, HIGH), (HIGH, LOW))):
                        last = dve.tensor_tensor(qa[other, m, :], ACC[0][own, :], qa[own, m, :].bitcast(F32),
                                                 ALU.subtract)
                    last.then_inc(acc_read, 1)
                if s == 2 and prev:
                    silu_half(h - 1, 1)
                if s == 3 and prev:
                    dve.wait_ge(o_squared, h)
                    if not first:
                        dve.wait_ge(head_gated, h - 1)
                    dve.tensor_copy(oT[:, :], OB[:, :]).then_inc(o_copied, 1)
                    silu_mult(h - 1, h * 4)
                if s == 4 and cur:
                    dve.wait_ge(proj_hi, h * 2 + 2)
                    for m, own in enumerate((LOW, HIGH)):
                        last = dve.tensor_tensor(ka_lo[own, :], ACC[1][own, :], ka[own, m, :].bitcast(F32),
                                                 ALU.subtract)
                    last.then_inc(acc_read, 1)
                if s == 4 and prev:
                    dve.wait_ge(o_summed, h)
                    dve.tensor_scalar(o_var, TR[:, 0:TOK], 1.0 / P, SUBLN_EPS, ALU.mult, ALU.add
                                      ).then_inc(o_var_ready, 1)
                if s == 5 and cur:
                    max_a(h, 0, not prev)
                if s == 5 and prev:
                    dve.wait_ge(o_spread, h)
                    dve.wait_ge(o_copied, h)
                    dve.scalar_tensor_tensor(oT[:, :], TR[:, :], g_sub, oT[:, :], ALU.mult, ALU.mult
                                             ).then_inc(o_normed, 1)
                    dve.wait_ge(o_normed, h)
                    dve.wait_ge(silu_done, h)
                    dve.tensor_tensor(gate_of(h - 1), gate_of(h - 1), oT[:, :], ALU.mult).then_inc(head_gated, 1)
                if s == 6 and cur:
                    dve.wait_ge(used, h * A_STEPS + 6)
                    if prev:
                        dve.wait_ge(o_summed, h)
                    dve.tensor_copy(vT[:, :], ACC[0][:, :]).then_inc(acc_read, 1)
                    norm_a(h, 0)
                    max_a(h, 1, not prev)
                if s == 7 and cur:
                    pt_lo(h, 0, TR)
                    norm_a(h, 1)
                    max_a(h, 2, not prev)
                    v_lo(h, OB)

            for s in range(A_STEPS):
                if s >= AHEAD:
                    split_lo(Piece(s + AHEAD))
                a_step(s, 0, True, False)
            for s in range(A_STEPS):
                split_lo(Piece(A_STEPS + s + AHEAD))
                a_step(s, 1, True, True, True)
            with dve.Fori(2, HEADS) as h:
                for s in range(A_STEPS):
                    split_lo(Piece(s + AHEAD, h, A_STEPS))
                    a_step(s, h, True, True)

            def c_norm(i):
                j = i // LT
                dve.wait_ge(c_spread, j + 1)
                dve.wait_ge(acc_read, HEADS * 4 + i + 1)
                g = (g_q, g_kv)[j][:, i % LT:i % LT + 1]
                dve.scalar_tensor_tensor(c_raw[:, i, :], c_raw[:, i, :], g, SC[2 * j + 1][:, :],
                                         ALU.mult, ALU.mult).then_inc(c_scaled, 1)

            def c_lo_of(i):
                dve.wait_ge(c_hi_ready, i + 1)
                dve.tensor_tensor(c_lo[:, i, :], c_raw[:, i, :], c_hi[:, i, :].bitcast(F32), ALU.subtract
                                  ).then_inc(c_lo_ready, 1)

            def rotate(i, src, read=None):
                dve.wait_ge(rope_shifted, i + 1)
                if not isinstance(i, int) or i > 0:
                    dve.wait_ge(rope_lo, i)
                dve.tensor_tensor(rope_in[:, :], src[:, :], cos_t[:, :], ALU.mult).then_inc(read or rope_cos, 1)
                dve.tensor_tensor(rope_sw[:, :], rope_sw[:, :], sin_t[:, :], ALU.mult).then_inc(rope_sin, 1)
                dve.wait_ge(rope_sin, i + 1)
                if read is None:
                    dve.wait_ge(rope_cos, i)
                dve.tensor_tensor(rope_in[:, :], rope_in[:, :], rope_sw[:, :], ALU.add).then_inc(rope_done, 1)

            for s in range(C_STEPS):
                split_lo(Piece(C0 + s + AHEAD))
                if s < 6:
                    a_step(s, HEADS, False, True)
                if s == 7:
                    rope_angles()
                if s == 12:
                    dve.wait_ge(trig_ready, 2)
                    link(dve.tensor_scalar(sin_t[:, :], sin_t[:, :], rope_sign, None, ALU.mult))
                b = s // 2 - 1
                if s % 2 == 0 and 0 <= b < 2 * LT:
                    dve.wait_ge(used, C0 + s)
                    if b == LT:
                        dve.wait_ge(dist_halved, HEADS * TOK - 1)
                    dve.tensor_copy(c_raw[:, b, :], ACC[b % 2][:, :]).then_inc(acc_read, 1)
                if s in (9, 17):
                    j = s // 16
                    dve.wait_ge(c_summed, LT * (j + 1))
                    dve.tensor_reduce(c_ss, SC[2 * j][:, 0:LT * TOK].rearrange("p (b t) -> p t b", b=LT),
                                      axis=AX_X, op=ALU.add).then_inc(c_ss_ready, 1)
                    dve.wait_ge(c_ss_ready, j + 1)
                    dve.tensor_scalar(c_var, c_ss, 1.0 / LORA, NORM_EPS, ALU.mult, ALU.add).then_inc(c_var_ready, 1)
                if s in (10, 11, 18, 19):
                    i = (LT * (s // 16)) + 2 * (s % 2)
                    c_norm(i)
                    c_norm(i + 1)
                    c_lo_of(i)
                    c_lo_of(i + 1)
                if s == 18:
                    rotate(0, ACC[0], acc_read)
                if s == 19:
                    dve.wait_ge(rope_hi, 1)
                    dve.tensor_tensor(kr_lo[0:64, :], rope_in[0:64, :], kr_hi[0:64, :].bitcast(F32), ALU.subtract
                                      ).then_inc(rope_lo, 1)

            G0 = HEADS * 4 + 10

            def b_step(s, h, cur, prev):
                H = h + BH
                if s == 0 and cur:
                    gate_copy(H, ACC[1])
                if s == 0 and prev:
                    max_b(H - 1, 2)
                    max_b(H - 1, 3)
                    pt_lo(H - 1, 0, SC[0])
                    pt_lo(H - 1, 1, SC[1])
                    norm_b(H - 1, 2)
                    norm_b(H - 1, 3)
                if s == 1 and cur:
                    proj_split_lo(q_hl, ACC[0], H * 2 + 1)
                if s == 1 and prev:
                    pt_lo(H - 1, 2, SC[2])
                    pt_lo(H - 1, 3, SC[3])
                if s == 1 and cur:
                    rotate(h + 1, TR)
                    proj_split_lo(k_hl, ACC[1], H * 2 + 2)
                if s == 2 and cur:
                    dve.wait_ge(used, h * B_STEPS + (B0 + 2))
                    if prev:
                        dve.wait_ge(v_turned, H)
                    dve.tensor_copy(vT[:, :], ACC[0][:, :]).then_inc(acc_read, 1)
                    dve.wait_ge(rope_hi, h * 2 + 3)
                    dve.tensor_tensor(qr_hl[64:P, :], rope_in[64:P, :], kr_lo[64:P, :].bitcast(F32), ALU.subtract
                                      ).then_inc(rope_lo, 1)
                    silu_half(H, 0)
                if s == 2 and prev:
                    dve.wait_ge(pv_done, H * 2)
                    dve.wait_ge(silu_done, H)
                    dve.tensor_tensor(gate_of(H - 1), OB[:, :], gate_of(H - 1), ALU.mult).then_inc(head_gated, 1)
                if s == 3 and cur:
                    max_b(H, 0)
                    max_b(H, 1)
                    v_lo(H, TR)
                    norm_b(H, 0)
                    norm_b(H, 1)
                    silu_half(H, 1)
                    silu_mult(H, h * 4 + G0)

            for s in range(B_STEPS):
                split_lo(Piece(B0 + s + AHEAD))
                b_step(s, 0, True, False)
            with dve.Fori(1, HEADS - 1) as h:
                for s in range(B_STEPS):
                    split_lo(Piece(B0 + s + AHEAD, h, B_STEPS))
                    b_step(s, h, True, True)
            last = HEADS - 1
            for s in range(2):
                split_lo(Piece(B0 + B_STEPS * last + s + AHEAD))
                b_step(s, last, True, True)

            def gated_lo(head):
                dve.wait_ge(g_hi_ready, GATED_ORDER.index(head) + 1)
                hi, lo = ((ga_hi[:, head, :], ga_lo[:, head, :]) if head < HEADS else
                          (gb_hl[:, head - HEADS, 0, :], gb_hl[:, head - HEADS, 1, :]))
                dve.tensor_tensor(lo, gated[:, head * SEQ:(head + 1) * SEQ], hi.bitcast(F32), ALU.subtract
                                  ).then_inc(g_lo_ready, 1)

            def branch_a(i, b):
                dve.wait_ge(used, i * M_STEPS + (M0 + 6 * b + 5))
                dve.wait_ge(sig_ready, i * 4 + (2 * b + 1))
                dve.tensor_tensor(part[:, 0, :], bank[4 * b + 2][:, :], sig[:, b, 0, :], ALU.mult).then_inc(part_a, 1)

            def branch_b(i, b):
                n = i * 2 + (b + 1)
                dve.wait_ge(used, i * M_STEPS + (M0 + 6 * b + 6))
                dve.wait_ge(sig_ready, i * 4 + (2 * b + 2))
                dve.tensor_tensor(part[:, 1, :], bank[4 * b + 3][:, :], sig[:, b, 1, :], ALU.mult).then_inc(part_b, 1)
                dve.wait_ge(part_a, n)
                dve.wait_ge(part_b, n)
                dve.tensor_tensor(merged[:, bass.ds(i * (2 * SEQ) + b * SEQ, SEQ)], part[:, 0, :], part[:, 1, :],
                                  ALU.add).then_inc(merged_ready, 1)

            def merge_step(s, i, prev):
                if s == 0 and prev:
                    branch_b(i - 1, 1)
                if s == 5:
                    if prev:
                        dve.wait_ge(merged_ready, i * 2)
                    branch_a(i, 0)
                if s == 6:
                    branch_b(i, 0)
                if s == 11:
                    dve.wait_ge(merged_ready, i * 2 + 1)
                    branch_a(i, 1)

            for s in range(M_STEPS):
                split_lo(Piece(M0 + s + AHEAD))
                if s < 2:
                    b_step(s + 2, last, True, True)
                elif s < 5:
                    b_step(s - 2, HEADS, False, True)
                for head in GATED_AT[s]:
                    gated_lo(head)
                merge_step(s, 0, False)
            with dve.Fori(1, KT // 2) as i:
                for s in range(M_STEPS):
                    split_lo(Piece(M0 + s + AHEAD, i, M_STEPS))
                    merge_step(s, i, True)

            def extra_split_lo(c, s):
                n = c * EXTRA_PER_CHUNK + (EXTRA_AT.index(s - 2) - EXTRA_PER_CHUNK)
                dve.wait_ge(extra_hi, n + 1)
                dve.tensor_tensor(e_lo[:, bass.ds(n, 1), :], e_raw[:, bass.ds(n, 1), :],
                                  e_hi[:, bass.ds(n, 1), :].bitcast(F32), ALU.subtract).then_inc(extra_lo, 1)

            def merged_lo(j):
                dve.wait_ge(mg_hi_ready, j + 1)
                dve.tensor_tensor(mg_lo[:, j, :], merged[:, j * SEQ:(j + 1) * SEQ], mg_hi[:, j, :].bitcast(F32),
                                  ALU.subtract).then_inc(mg_lo_ready, 1)

            def add_x(c, t):
                if t < TOK - 1 or (isinstance(c, int) and c == LAST_C):
                    dve.wait_ge(chunk_done, c * (TOK - 1) + (t + 1))
                else:
                    dve.wait_ge(used, c * F_STEPS + (FIN0 + F_STEPS))
                dve.wait_ge(x_again, c * 16 + 16)
                xt = x_tok[:, t, bass.ds(c * SEQ, SEQ)]
                dve.tensor_tensor(xt, bank[t][:, :], xt, ALU.add).then_inc(x_added, 1)

            def add_chunk(c):
                for t in range(TOK):
                    add_x(c, t)
                for t in range(TOK):
                    dve.wait_ge(f_squared, c * TOK + (t + 1))
                    xt = x_tok[:, t, bass.ds(c * SEQ, SEQ)]
                    dve.tensor_tensor(xt, xt, fg[:, bass.ds(c * SEQ, SEQ)], ALU.mult).then_inc(gained, 1)

            for j in range(4):
                merged_lo(j)
            branch_b(KT // 2 - 1, 1)
            for s in range(F_STEPS):
                split_lo(Piece(FIN0 + s + AHEAD))
                for j in (4 + 2 * s, 5 + 2 * s):
                    if j < KT:
                        merged_lo(j)
            dve.wait_ge(fg_in, 16)
            add_chunk(0)
            with dve.Fori(1, LAST_C) as c:
                for s in range(F_STEPS):
                    split_lo(Piece(FIN0 + s + AHEAD, c, F_STEPS))
                    if s - 2 in EXTRA_AT:
                        extra_split_lo(c, s)
                add_chunk(c)
            for i in range(AHEAD, LAST_RING):
                split_lo(Piece(LAST0 + i))
            last_c = slice(LAST_C * SEQ, D_MODEL)

            def variance(t):
                dve.wait_ge(f_squared, LAST_C * TOK + t + 1)
                dve.tensor_reduce(f_sum[:, t:t + 1], f_ss.rearrange("p (c t) -> p t c", t=TOK)[:, t:t + 1, :],
                                  axis=AX_X, op=ALU.add).then_inc(f_sum_ready, 1)
                dve.wait_ge(f_sum_ready, t + 1)
                dve.tensor_scalar(f_var[:, t:t + 1], f_sum[:, t:t + 1], 1.0 / D_MODEL, NORM_EPS, ALU.mult, ALU.add
                                  ).then_inc(f_var_ready, 1)

            def scale_v(t):
                dve.wait_ge(gained, TOK * LAST_C)
                dve.wait_ge(f_rstd_ready, t + 1)
                dve.scalar_tensor_tensor(x_tok[:, t, last_c], x_tok[:, t, last_c], f_rstd[:, t:t + 1],
                                         fg[:, last_c], ALU.mult, ALU.mult).then_inc(scaled_v, 1)
                dve.tensor_scalar(x_tok[:, t, FINAL_A:LAST_C * SEQ], x_tok[:, t, FINAL_A:LAST_C * SEQ],
                                  f_rstd[:, t:t + 1], None, ALU.mult).then_inc(scaled_v, 1)

            for t in range(TOK):
                add_x(LAST_C, t)
                variance(t)
                scale_v(t)

        @block.tensor
        def _(pe):
            def three(dst, lhs_hi, lhs_lo, rhs_hi, rhs_lo, start, stop):
                pe.matmul(dst, lhs_hi, rhs_hi, start=start, stop=False)
                pe.matmul(dst, lhs_hi, rhs_lo, start=False, stop=False)
                return pe.matmul(dst, lhs_lo, rhs_hi, start=False, stop=stop)

            def tile(piece, c0, width=P):
                return w_hi[:, piece.slot, c0:c0 + width], w_lo[:, piece.slot, c0:c0 + width]

            def project(piece, dst, half, halves, rhs_hi, rhs_lo, k0, h_waits=False):
                pe.wait_ge(lo_ready, piece.after(0))
                for k in range(8):
                    if h_waits:
                        if k0 + k + X_AHEAD < KT:
                            turn_x(k0 + k + X_AHEAD)
                        pe.wait_ge(h_lo_ready, k0 + k + 1)
                    hi, lo = tile(piece, k * P)
                    last = three(dst[:, :], hi, lo, rhs_hi[:, k0 + k, :], rhs_lo[:, k0 + k, :],
                                 half == 0 and k == 0, half == halves - 1 and k == 7)
                last.then_inc(used, 1)

            def scores_a(head, t, first):
                if t == 0:
                    pe.wait_ge(acc_read, head * 4 + 2)
                if not first or t >= 2:
                    pe.wait_ge(max_taken, tile_no(head, t) - 2)
                a, b = SC[2 * (t % 2)], SC[2 * (t % 2) + 1]
                q = slice(t * P, (t + 1) * P)
                for m, dst in enumerate((a, b)):
                    pe.matmul(dst[:, :], qa[:, m, q], ka[:, m, :], start=True, stop=False)
                for m, (dst, own) in enumerate(((a, LOW), (b, HIGH))):
                    last = pe.matmul(dst[:, :], qa[own, m, q], ka_lo[own, :], start=False, stop=True)
                last.then_inc(scored, 1)

            def scores_b(h, t, prev):
                H = h + BH
                if t == 0:
                    pe.wait_ge(acc_read, h * 4 + (HEADS * 4 + 12))
                    pe.wait_ge(rope_lo, h + 2)
                if prev:
                    pe.wait_ge(pt_lo_ready, tile_no(H, t) - TOK)
                elif t == 0:
                    pe.wait_ge(c_lo_ready, 2 * LT)
                q = slice(t * P, (t + 1) * P)
                dst = SC[t][:, :]
                pe.matmul(dst, q_hl[:, 0, q], k_hl[:, 0, :], start=True, stop=False)
                pe.matmul(dst, q_hl[:, 0, q], k_hl[:, 1, :], start=False, stop=False)
                pe.matmul(dst, q_hl[:, 1, q], k_hl[:, 0, :], start=False, stop=False)
                pe.matmul(dst, qr_hl[:, q], kr_hi[:, :], start=False, stop=False)
                pe.matmul(dst, qr_hl[0:64, q], kr_lo[0:64, :], start=False, stop=True).then_inc(scored, 1)

            def turn(src, dst, done):
                for k in range(TOK):
                    last = pe.transpose(dst[:, k * P:(k + 1) * P], src[:, k * P:(k + 1) * P], ident)
                last.then_inc(done, 1)

            def turn_p_a(head, t, first):
                pe.wait_ge(p_ready, tile_no(head, t))
                if t:
                    pe.wait_ge(pt_lo_ready, tile_no(head, t) - 1)
                elif not first:
                    pe.wait_ge(o_normed, head)
                turn(e[:, t % 2, 0, :], TR, p_turned)

            def turn_p_b(head, t):
                pe.wait_ge(p_ready, tile_no(head, t))
                turn(e_b[:, t % 2, :], SC[t], p_turned)

            def pv(head, pair):
                pe.wait_ge(pt_lo_ready, tile_no(head, 2 * pair + 1))
                pe.wait_ge(v_lo_ready, head + 1)
                for k in range(TOK):
                    last = three(OB[:, pair * 2 * P:(pair + 1) * 2 * P], v_hl[:, 0, k, :], v_hl[:, 1, k, :],
                                 pt[:, 0, k, :], pt[:, 1, k, :], k == 0, k == TOK - 1)
                last.then_inc(pv_done, 1)

            def column_sums(sq, dst, c0, done):
                for t in range(TOK):
                    last = pe.matmul(dst[:, c0 + t:c0 + t + 1], sq[:, t * P:(t + 1) * P], ones, start=True, stop=True)
                last.then_inc(done, 1)

            def spread(col, dst, done):
                for t in range(TOK):
                    last = pe.matmul(dst[:, t * P:(t + 1) * P], col[:, t:t + 1].broadcast_to([P, P]), ident,
                                     start=True, stop=True)
                last.then_inc(done, 1)

            pe.wait_ge(cst_in, 16)
            pe.wait_ge(ones_set, 3)
            pe.wait_ge(x_normed, TOK)
            def turn_x(k):
                if k >= 6:
                    pe.wait_ge(h_lo_ready, k - 5)
                for t in range(TOK):
                    last = pe.transpose(bank[2 + k % 6][:, t * P:(t + 1) * P], x_tok[:, t, k * P:(k + 1) * P], ident)
                last.then_inc(x_turned, 1)

            for k in range(X_AHEAD):
                turn_x(k)

            def a_extras(s, h, cur, prev, first=False):
                if s == 0 and prev:
                    turn_p_a(h - 1, 2, first)
                    pv(h - 1, 0)
                if s == 1 and prev:
                    turn_p_a(h - 1, 3, first)
                if s == 2 and prev:
                    pv(h - 1, 1)
                if s == 3 and prev:
                    pe.wait_ge(o_squared, h)
                    pe.wait_ge(pt_lo_ready, h * TOK)
                    column_sums(vT, TR, 0, o_summed)
                if s == 4 and cur:
                    scores_a(h, 0, not prev)
                if s == 4 and prev:
                    pe.wait_ge(o_rstd_ready, h)
                    spread(o_rstd, TR, o_spread)
                if s == 5 and cur:
                    scores_a(h, 1, not prev)
                if s == 6 and cur:
                    pe.wait_ge(acc_read, h * 4 + 3)
                    if prev:
                        pe.wait_ge(o_copied, h)
                    turn(vT, OB, v_turned)
                    turn_p_a(h, 0, not prev)
                    scores_a(h, 2, not prev)
                if s == 7 and cur:
                    turn_p_a(h, 1, not prev)
                    scores_a(h, 3, not prev)

            def a_head(h, prev, first=False):
                for s in range(A_STEPS):
                    g = s // 2
                    if s % 2 == 0 and (prev or g >= 2):
                        pe.wait_ge(acc_read, h * 4 + (g - 1))
                    project(Piece(s, h, A_STEPS), ACC[g % 2], s % 2, 2, h_hi, h_lo, 8 * (s % 2),
                            h_waits=not prev and s < 2)
                    a_extras(s, h, True, prev, first)

            a_head(0, False)
            with pe.Fori(1, HEADS) as h:
                a_head(h, True)

            for s in range(C_STEPS):
                b = s // 2
                if s % 2 == 0:
                    pe.wait_ge(acc_read, HEADS * 4 + b - 1)
                project(Piece(C0 + s), ACC[b % 2], s % 2, 2, h_hi, h_lo, 8 * (s % 2))
                if s < 6:
                    a_extras(s, HEADS, False, True)
                b -= 1
                if s % 2 == 0 and 0 <= b < 2 * LT:
                    if b == 0:
                        pe.wait_ge(max_taken, HEADS * TOK)
                    pe.wait_ge(c_squared, b + 1)
                    column_sums(c_sq, SC[2 * (b // LT)], TOK * (b % LT), c_summed)
                if s in (9, 17):
                    j = s // 16
                    pe.wait_ge(c_rstd_ready, j + 1)
                    spread(c_rstd, SC[2 * j + 1], c_spread)

            def up(piece, c0, dst, which):
                for k in range(LT):
                    hi, lo = tile(piece, k * 2 * P + c0)
                    last = three(dst[:, :], hi, lo, c_hi[:, which * LT + k, :], c_lo[:, which * LT + k, :],
                                 k == 0, k == LT - 1)
                return last

            def b_extras(s, h, cur, prev):
                H = h + BH
                if s == 0 and prev:
                    pe.wait_ge(head_gated, H - 1)
                    pv(H - 1, 0)
                    turn_p_b(H - 1, 2)
                    turn_p_b(H - 1, 3)
                if s == 1 and prev:
                    pv(H - 1, 1)
                if s == 2 and cur:
                    scores_b(h, 0, prev)
                    scores_b(h, 1, prev)
                    pe.wait_ge(acc_read, h * 4 + (HEADS * 4 + 13))
                    pe.wait_ge(rope_cos, h + 1)
                    turn(vT, TR, v_turned)
                if s == 3 and cur:
                    scores_b(h, 2, prev)
                    scores_b(h, 3, prev)
                    turn_p_b(H, 0)
                    turn_p_b(H, 1)

            def b_up(h, prev):
                g = h * 4 + (HEADS * 4 + 10)
                H = h + BH
                piece = Piece(B0, h, B_STEPS)
                pe.wait_ge(lo_ready, piece.after(0))
                if prev:
                    pe.wait_ge(v_lo_ready, H)
                else:
                    pe.wait_ge(o_normed, HEADS)
                    pe.wait_ge(c_lo_ready, LT)
                up(piece, P, TR, 0).then_inc(rope_up, 1)
                pe.wait_ge(acc_read, g - 1)
                up(piece, 0, ACC[0], 0).then_inc(used, 1)
                b_extras(0, h, True, prev)
                piece = Piece(B0 + 1, h, B_STEPS)
                pe.wait_ge(lo_ready, piece.after(0))
                if not prev:
                    pe.wait_ge(c_lo_ready, 2 * LT)
                pe.wait_ge(acc_read, g)
                up(piece, 0, ACC[1], 1).then_inc(k_up, 1)
                pe.wait_ge(acc_read, g + 1)
                up(piece, P, ACC[0], 1).then_inc(used, 1)
                b_extras(1, h, True, prev)

            def b_gate(h, prev):
                for s in range(2):
                    if s == 0:
                        pe.wait_ge(acc_read, h * 4 + (HEADS * 4 + 12))
                    project(Piece(B0 + 2 + s, h, B_STEPS), ACC[1], s, 2, h_hi, h_lo, 8 * s)
                    b_extras(2 + s, h, True, prev)

            b_up(0, False)
            b_gate(0, False)
            with pe.Fori(1, HEADS - 1) as h:
                b_up(h, True)
                b_gate(h, True)
            last_h = HEADS - 1
            b_up(last_h, True)

            def merge(i, tail):
                for s in range(M_STEPS):
                    b, k = s // 6, s % 6
                    piece = Piece(M0 + s, i, M_STEPS)
                    if tail:
                        if s == 0:
                            pe.wait_ge(acc_read, last_h * 4 + HEADS * 4 + 13)
                        if s == 4:
                            pe.wait_ge(g_lo_ready, HEADS)
                            pe.wait_ge(head_gated, 2 * HEADS)
                        if s == 5:
                            pe.wait_ge(g_lo_ready, 2 * HEADS)
                    else:
                        if k in (0, 2):
                            pe.wait_ge(sig_ready, i * 4 + (2 * b + k // 2 - 3))
                        if k == 4:
                            pe.wait_ge(part_a, i * 2 + (b - 1))
                        if k == 5:
                            pe.wait_ge(part_b, i * 2 + (b - 1))
                    if k < 4:
                        project(piece, bank[4 * b + k // 2], k % 2, 2, h_hi, h_lo, 8 * (k % 2))
                    elif k == 4:
                        project(piece, bank[4 * b + 2], 0, 1, ga_hi, ga_lo, 0)
                    else:
                        project(piece, bank[4 * b + 3], 0, 1, gb_hl[:, :, 0, :], gb_hl[:, :, 1, :], 0)
                    if tail and s < 2:
                        b_extras(s + 2, last_h, True, True)
                    elif tail and s < 5:
                        b_extras(s - 2, HEADS, False, True)

            merge(0, True)
            with pe.Fori(1, KT // 2) as i:
                merge(i, False)

            def out_chunk(c, first):
                for s in range(F_STEPS):
                    piece = Piece(FIN0 + s, c, F_STEPS)
                    pe.wait_ge(lo_ready, piece.after(0))
                    if first:
                        pe.wait_ge(mg_lo_ready, 2 * s + 2)
                        if s == 0:
                            pe.wait_ge(merged_ready, KT - 1)
                    for t in range(TOK):
                        if s == 0 and not first:
                            pe.wait_ge(x_added, c * TOK + (t - (TOK - 1)))
                        for k in range(2):
                            hi, lo = tile(piece, k * SEQ, SEQ)
                            kt = 2 * s + k
                            q = slice(t * P, (t + 1) * P)
                            last = three(bank[t][:, :], mg_hi[:, kt, q], mg_lo[:, kt, q], hi, lo,
                                         kt == 0, kt == KT - 1)
                        if s == F_STEPS - 1 and t < TOK - 1:
                            last.then_inc(chunk_done, 1)
                    last.then_inc(used, 1)
                return last

            out_chunk(0, True)
            with pe.Fori(1, LAST_C) as c:
                out_chunk(c, False)

            for t in range(TOK):
                q = slice(t * P, (t + 1) * P)
                pe.wait_ge(x_added, LAST_C * TOK + t - (TOK - 1))
                for s in range(F_STEPS):
                    extra = s - EXTRA_FIRST
                    if 0 <= extra < EXTRAS:
                        hi, lo = e_hi[:, extra, :], e_lo[:, extra, :]
                        if t == 0:
                            pe.wait_ge(extra_lo, extra + 1)
                    else:
                        piece = Piece(LAST0 + (s if extra < 0 else s - EXTRAS))
                        hi, lo = tile(piece, 0, 2 * SEQ)
                        if t == 0:
                            pe.wait_ge(lo_ready, piece.after(0))
                    for k in range(2):
                        kt, w = 2 * s + k, slice(k * SEQ, (k + 1) * SEQ)
                        last = three(bank[t][:, :], mg_hi[:, kt, q], mg_lo[:, kt, q], hi[:, w], lo[:, w],
                                     kt == 0, kt == KT - 1)
                last.then_inc(chunk_done, 1)


_INS = ['x', 'positions', 'norm_g', 'w_in', 'lam_q1', 'lam_k1', 'lam_q2', 'lam_k2', 'a_subln_g', 'w_oa',
        'q_norm_g', 'w_uq', 'kv_norm_g', 'w_ukv', 'w_ob', 'w_out', 'final_g']


def kernel(**inputs):
    import numpy as _np
    import concourse.bacc as _bacc
    from concourse import mybir as _mybir
    from concourse.bass_utils import run_bass_kernel_spmd as _run

    consts = _np.zeros((P, P + 2), _np.float32)
    consts[:, 0:P] = _np.eye(P)
    half = B_ROPE // 2
    for m in range(P):
        consts[m, P] = 10000.0 ** (-(m % half) / half)
        consts[m, P + 1] = -1.0 if m % B_ROPE < half else 1.0

    nc = _bacc.Bacc("TRN2", target_bir_lowering=False, num_devices=1)
    arrays, args = {}, []
    for name, a in [(n, inputs[n]) for n in _INS] + [("consts", consts)]:
        a = _np.ascontiguousarray(a)
        arrays[f"in_{name}_dram"] = a
        args.append(nc.dram_tensor(f"in_{name}_dram", a.shape, _mybir.dt.from_np(a.dtype), kind="ExternalInput").ap())
    args.append(nc.dram_tensor("out_0_dram", (1, SEQ, D_MODEL), _mybir.dt.float32, kind="ExternalOutput").ap())
    hybrid_encoder(nc, *args)
    r = _run(nc, [arrays], core_ids=[0])
    return r.results[0]["out_0_dram"]
```

```python
import math
from contextlib import ExitStack

import concourse.bass as bass
from concourse import mybir

F32 = mybir.dt.float32
F32R = mybir.dt.float32r
I32 = mybir.dt.int32
ALU = mybir.AluOpType
ACT = mybir.ActivationFunctionType
AX_X = mybir.AxisListType.X

P = 128
SEQ, D_MODEL = 512, 2048
TOK = SEQ // P
KT = D_MODEL // P
HEADS = 8
A_DIM, B_NOPE, B_ROPE = 64, 128, 64
LORA = 512
LT = LORA // P
AQ, AK, AV, AG = 0, 1024, 2048, 3072
CQ, CKV, KR, BG, MG = 4096, 4608, 5120, 5184, 6208
A_SCALE = A_DIM ** -0.5
B_SCALE = (B_NOPE + B_ROPE) ** -0.5
LAM_INIT = 0.8 - 0.6 * math.exp(-0.3 * 0)
SLOPE0, SLOPE_RATIO = 2.0 ** (-8.0 / HEADS), 2.0 ** (-8.0 / HEADS)
NORM_EPS, SUBLN_EPS = 1e-6, 1e-5

SLOTS = 4
AHEAD = 2
A_STEPS, C_STEPS, B_STEPS, M_STEPS, F_STEPS = 8, 20, 4, 12, 8
C0 = HEADS * A_STEPS
B0 = C0 + C_STEPS
M0 = B0 + B_STEPS * HEADS - 2
FIN0 = M0 + M_STEPS * (KT // 2)
N_CHUNK = D_MODEL // SEQ
LAST_C = N_CHUNK - 1
EXTRAS = 4
EXTRA_PER_CHUNK = EXTRAS // (LAST_C - 1)
EXTRA_FIRST = 2
LAST_RING = F_STEPS - EXTRAS
LAST0 = FIN0 + F_STEPS * LAST_C
HALF_PIECE = SEQ

GATED_AT = [(0, 1, 2), (3, 4, 5), (6, 7, 8, 9), (12,), (10, 11, 13, 14, 15), ()] + [()] * (M_STEPS - 6)

TWO_PI_1 = 6.28125
TWO_PI_2 = 1.93500518798828125e-3
TWO_PI_3 = 2 * math.pi - TWO_PI_1 - TWO_PI_2
GATED_ORDER = [head for step in GATED_AT for head in step]
X_AHEAD = 6
C_SUMS_AT = (9, 16)
C_NORM_AT = (11, 12, 18, 19)
WARM_UP = {1: 3, 2: 1, 3: 6}
EARLY_SPLIT = {3: 1, 7: 2, 12: 3}
ROUND_1 = 1.5 * 2.0 ** 23
ROUND_2048 = 1.5 * 2.0 ** 34
PI_DOWN = 3.1415925

FINAL_A = 2 * SEQ
FINAL_STORES = [(1, 1, slice(LAST_C * SEQ, D_MODEL)), (0, 1, slice(0, FINAL_A)), (1, 2, slice(FINAL_A, LAST_C * SEQ))]

EXTRA_AT = (1, 3)

X_PARTS = [(t, slice(0, D_MODEL)) for t in range(TOK - 1)] + [
    (TOK - 1, slice(0, D_MODEL // 2)), (TOK - 1, slice(D_MODEL // 2, D_MODEL))]


class Piece:

    def __init__(self, first, loop=0, stride=0):
        self.first = first
        self.slot = first % SLOTS
        self.n = loop * stride + first
        self.turn = loop * (stride // SLOTS) + first // SLOTS

    def after(self, k):
        return self.n + (k + 1)


def hybrid_encoder(nc, x, positions, norm_g, w_in, lam_q1, lam_k1, lam_q2, lam_k2, a_subln_g, w_oa,
                   q_norm_g, w_uq, kv_norm_g, w_ukv, w_ob, w_out, final_g, consts, out):
    ctx = ExitStack()
    with ctx:
        base = (nc.sbuf_base + 63) // 64 * 64
        KB = 1024

        def at(name, kb, shape, dt=F32):
            return nc.alloc_sbuf_tensor_at(name, shape, dt, offset=base + int(kb * KB))

        def sem(name):
            return ctx.enter_context(nc.semaphore(name))

        h_hi = at("h_hi", 0, [P, KT, SEQ], F32R)
        h_lo = at("h_lo", 32, [P, KT, SEQ], F32R)
        mg_hi = at("mg_hi", 0, [P, KT, SEQ], F32R)
        mg_lo = at("mg_lo", 32, [P, KT, SEQ], F32R)
        w_raw = at("w_raw", 64, [P, SLOTS, 1024])
        w_lo = at("w_lo", 64, [P, SLOTS, 1024], F32R)
        w_hi = at("w_hi", 80, [P, SLOTS, 1024], F32R)
        gated = at("gated", 96, [P, 2 * HEADS * SEQ])
        merged = at("merged", 96, [P, KT * SEQ])
        e_lo = at("e_lo", 96, [P, EXTRAS, 1024], F32R)
        e_raw = at("e_raw", 96, [P, EXTRAS, 1024])
        e_hi = at("e_hi", 112, [P, EXTRAS, 1024], F32R)
        c_raw = at("c_raw", 112, [P, 2 * LT, SEQ])
        dist = at("dist", 120, [P, TOK, SEQ])
        x_tok = at("x_tok", 128, [P, TOK, D_MODEL])
        c_hi = at("c_hi", 128, [P, 2 * LT, SEQ], F32R)
        c_lo = at("c_lo", 144, [P, 2 * LT, SEQ], F32R)
        ga_hi = at("ga_hi", 128, [P, HEADS, SEQ], F32R)
        ga_lo = at("ga_lo", 144, [P, HEADS, SEQ], F32R)
        gb_hl = at("gb_hl", 160, [P, HEADS, 2, SEQ], F32R)
        square_junk = at("square_junk", 160, [P, D_MODEL])
        fg = at("fg", 160, [P, D_MODEL])
        q_hl = at("q_hl", 160, [P, 2, SEQ], F32R)
        c_sq = at("c_sq", 160, [P, SEQ])
        c_sq_tile = at("c_sq_tile", 162, [P, SEQ])
        k_hl = at("k_hl", 164, [P, 2, SEQ], F32R)
        qa = at("qa", 160, [P, 2, SEQ], F32R)
        ka = at("ka", 164, [P, 2, SEQ], F32R)
        ka_lo = at("ka_lo", 198, [P, SEQ], F32R)
        vT = at("vT", 168, [P, SEQ])
        v_hl = at("v_hl", 170, [P, 2, TOK, P], F32R)
        e = at("e", 174, [P, 2, 2, SEQ])
        e_b = at("e_b", 174, [P, 2, SEQ])
        rope_in = at("rope_in", 178, [P, SEQ])
        rope_sw = at("rope_sw", 180, [P, SEQ])
        pt = at("pt", 182, [P, 2, TOK, 2 * P], F32R)
        oT = at("oT", 190, [P, SEQ])
        eg = at("eg", 192, [P, SEQ])
        cos_t = at("cos_t", 194, [P, SEQ])
        sin_t = at("sin_t", 196, [P, SEQ])
        kr_hi = at("kr_hi", 198, [P, SEQ], F32R)
        kr_lo = at("kr_lo", 200, [P, SEQ], F32R)
        qr_hl = at("qr_hl", 202, [P, SEQ], F32R)
        sig = at("sig", 192, [P, 2, 2, SEQ])
        part = at("part", 200, [P, 2, SEQ])
        cst = at("cst", 204, [P, P + 2])
        small = at("small", 205.25, [P, 160])
        pos_i = at("pos_i", 182, [P, SEQ], I32)
        pos_f = at("pos_f", 184, [P, SEQ])
        lam_in = at("lam_in", 186, [P, 6, A_DIM])
        assert base + 207 * KB <= nc.sbuf_usable_end

        ident = cst[:, 0:P]
        inv_freq, rope_sign = cst[:, P:P + 1], cst[:, P + 1:P + 2]
        g_in = small[:, 0:KT]
        g_q, g_kv = small[:, 16:20], small[:, 20:24]
        g_sub = small[:, 24:25]
        lam = small[:, 25:26]
        ones = small[:, 26:27]
        mhalf = small[:, 27:31]
        pos_q = small[:, 31:35]
        x_ss, x_var, x_rstd = small[:, 35:39], small[:, 39:43], small[:, 43:47]
        mx, nm = small[:, 47:55], small[:, 55:63]
        sums, rs = small[:, 63:71], small[:, 71:79]
        o_var, o_rstd = small[:, 79:83], small[:, 83:87]
        c_var, c_rstd = small[:, 91:95], small[:, 95:99]
        f_ss = small[:, 99:115]
        f_sum, f_var, f_rstd = small[:, 115:119], small[:, 119:123], small[:, 123:127]
        lam_s, lam_e = small[:, 127:129], small[:, 129:131]
        half_pi = small[:, 131:132]
        g_sub_raw = small[:, 132:133]
        rs_lam = small[:, 133:135]
        x_half_ss, x_half_var = small[:, 135:136], small[:, 136:137]
        pos_qi = at("pos_qi", 187.75, [P, TOK], I32)

        bank = [ctx.enter_context(nc.psum_tensor(f"bank{i}", [P, SEQ], F32)) for i in range(8)]
        ACC = bank[0:2]
        SC = bank[2:6]
        TR = bank[6]
        OB = bank[7]

        landed = [sem(f"landed{i}") for i in range(SLOTS)]
        hi_ready = sem("hi_ready")
        lo_ready = sem("lo_ready")
        extra_in = [sem(f"extra_in{j}") for j in range(EXTRA_PER_CHUNK)]
        extra_hi, extra_lo = sem("extra_hi"), sem("extra_lo")
        used = sem("used")
        g_in_in, gains_in, lambdas_in = sem("g_in_in"), sem("gains_in"), sem("lambdas_in")
        x_in = [sem(f"x_in{i}") for i in range(TOK + 1)]
        pos_in, cst_in = sem("pos_in"), sem("cst_in")
        ones_set = sem("ones_set")
        v_chain = sem("v_chain")
        a_chain = sem("a_chain")
        lam_sum, lam_exp = sem("lam_sum"), sem("lam_exp")
        angle_ready, trig_ready = sem("angle_ready"), sem("trig_ready")
        x_ss_ready, x_var_ready, x_rstd_ready, x_normed = (
            sem("x_ss_ready"), sem("x_var_ready"), sem("x_rstd_ready"), sem("x_normed"))
        x_turned, h_hi_ready, h_lo_ready = sem("x_turned"), sem("h_hi_ready"), sem("h_lo_ready")
        dist_ready, dist_halved = sem("dist_ready"), sem("dist_halved")
        proj_hi = sem("proj_hi")
        acc_read = sem("acc_read")
        gate_exp, silu_add, silu_inv, silu_done = sem("gate_exp"), sem("silu_add"), sem("silu_inv"), sem("silu_done")
        v_turned, v_hi_ready, v_lo_ready = sem("v_turned"), sem("v_hi_ready"), sem("v_lo_ready")
        scored = sem("scored")
        max_taken = sem("max_taken")
        bias_ready = sem("bias_ready")
        exp_done = sem("exp_done")
        inv_ready, inv_lam_ready, e2_scaled, p_ready = (
            sem("inv_ready"), sem("inv_lam_ready"), sem("e2_scaled"), sem("p_ready"))
        p_turned, pt_hi_ready, pt_lo_ready = sem("p_turned"), sem("pt_hi_ready"), sem("pt_lo_ready")
        pv_done = sem("pv_done")
        o_squared, o_copied, o_summed, o_var_ready, o_rstd_ready, o_spread, o_normed, head_gated = (
            sem("o_squared"), sem("o_copied"), sem("o_summed"), sem("o_var_ready"), sem("o_rstd_ready"),
            sem("o_spread"), sem("o_normed"), sem("head_gated"))
        c_squared, c_added, c_summed, c_var_ready, c_rstd_ready, c_spread, c_scaled, c_hi_ready, c_lo_ready = (
            sem("c_squared"), sem("c_added"), sem("c_summed"), sem("c_var_ready"), sem("c_rstd_ready"),
            sem("c_spread"), sem("c_scaled"), sem("c_hi_ready"), sem("c_lo_ready"))
        k_up = sem("k_up")
        rope_up = sem("rope_up")
        rope_shifted, rope_cos, rope_sin, rope_done, rope_hi, rope_lo = (
            sem("rope_shifted"), sem("rope_cos"), sem("rope_sin"), sem("rope_done"), sem("rope_hi"), sem("rope_lo"))
        g_hi_ready, g_lo_ready = sem("g_hi_ready"), sem("g_lo_ready")
        sig_ready, part_a, part_b, merged_ready = sem("sig_ready"), sem("part_a"), sem("part_b"), sem("merged_ready")
        mg_hi_ready, mg_lo_ready = sem("mg_hi_ready"), sem("mg_lo_ready")
        x_again, fg_in = sem("x_again"), sem("fg_in")
        chunk_done, x_added, f_squared, f_sum_ready, f_var_ready, f_rstd_ready, stored = (
            sem("chunk_done"), sem("x_added"), sem("f_squared"), sem("f_sum_ready"), sem("f_var_ready"),
            sem("f_rstd_ready"), sem("stored"))
        gained = sem("gained")
        scaled_a, scaled_v = sem("scaled_a"), sem("scaled_v")

        LOW, HIGH = slice(0, 64), slice(64, P)
        BH = HEADS

        LAST_PAIR = (HEADS // 2 - 1, HIGH)

        def tile_no(head, t):
            return head * TOK + (t + 1)

        block = ctx.enter_context(nc.Block())

        @block.sync
        def _(sp):
            def load(piece, parts):
                if not isinstance(piece.n, int) or piece.n >= SLOTS:
                    sp.wait_ge(used, piece.n - (SLOTS - 1))
                    sp.nop(nofuse=True)
                for dst, src in parts:
                    sp.dma_start(dst, src).then_inc(landed[piece.slot], 16)

            def rows(w, r0, n, col, width):
                return w[0, r0 * P:(r0 + n) * P, bass.ds(col, width)].rearrange("(k p) c -> p k c", p=P)

            def block_piece(piece, w, r0, col):
                raw = w_raw[:, piece.slot, :].rearrange("p (k c) -> p k c", k=8)
                load(piece, [(raw[:, 4 * j:4 * j + 4, :], rows(w, r0 + 4 * j, 4, col, P)) for j in range(2)])

            def a_head(h, steps=range(A_STEPS)):
                for s in steps:
                    block_piece(Piece(s, h, A_STEPS), w_in, 8 * (s % 2), h * P + (AQ, AK, AV, AG)[s // 2])

            def up_pieces(h, odd):
                piece = Piece(B0, h, B_STEPS)
                width = B_NOPE + B_ROPE
                if odd:
                    raw = w_raw[:, piece.slot, 0:HALF_PIECE].rearrange("p (k c) -> p k c", k=LT)
                    load(piece, [(raw[:, 2 * j:2 * j + 2, :], rows(w_uq, 2 * j, 2, h * width, B_NOPE))
                                 for j in range(2)])
                else:
                    raw = w_raw[:, piece.slot, :].rearrange("p (k c) -> p k c", k=LT)
                    load(piece, [(raw[:, :, 0:width], rows(w_uq, 0, LT, h * width, width)),
                                 (raw[:, :, width:2 * P], rows(w_uq, 0, LT, h * width + (width + B_NOPE), B_ROPE))])
                piece = Piece(B0 + 1, h, B_STEPS)
                raw = w_raw[:, piece.slot, :].rearrange("p (k c) -> p k c", k=LT)
                load(piece, [(raw[:, 2 * j:2 * j + 2, :], rows(w_ukv, 2 * j, 2, h * (2 * P), 2 * P))
                             for j in range(2)])

            def merge_blocks(i):
                for b in range(2):
                    col = i * (2 * P) + b * P
                    for s in range(4):
                        block_piece(Piece(M0 + 6 * b + s, i, M_STEPS), w_in, 8 * (s % 2),
                                    col + (MG if s < 2 else MG + D_MODEL))
                    block_piece(Piece(M0 + 6 * b + 4, i, M_STEPS), w_oa, 0, col)
                    block_piece(Piece(M0 + 6 * b + 5, i, M_STEPS), w_ob, 0, col)

            def out_parts(dst, s, col):
                raw = dst.rearrange("p (k c) -> p k c", k=2)
                return [(raw[:, j:j + 1, :], rows(w_out, 2 * s + j, 1, col, SEQ)) for j in range(2)]

            def residual(c):
                sp.dma_start(x_tok[:, :, bass.ds(c * SEQ, SEQ)],
                             x[0, :, bass.ds(c * SEQ, SEQ)].rearrange("(t p) c -> p t c", p=P)
                             ).then_inc(x_again, 16)

            def out_chunk(c):
                for s in range(F_STEPS):
                    piece = Piece(FIN0 + s, c, F_STEPS)
                    load(piece, out_parts(w_raw[:, piece.slot, :], s, c * SEQ))
                    if isinstance(c, int) and s == 3:
                        sp.dma_start(fg[:, :], final_g.rearrange("(a d) -> a d", a=1).broadcast_to([P, D_MODEL])
                                     ).then_inc(fg_in, 16)
                    if s == 4:
                        residual(c)
                    if not isinstance(c, int) and s in EXTRA_AT:
                        j = EXTRA_AT.index(s)
                        if s == EXTRA_AT[0]:
                            sp.wait_ge(mg_lo_ready, KT)
                            sp.nop(nofuse=True)
                        n = c * EXTRA_PER_CHUNK + (j - EXTRA_PER_CHUNK)
                        for k in range(2):
                            sp.dma_start(e_raw[:, bass.ds(n, 1), k * SEQ:(k + 1) * SEQ],
                                         w_out[0, bass.ds(n * (2 * P) + (2 * EXTRA_FIRST + k) * P, P),
                                               LAST_C * SEQ:D_MODEL].rearrange("(k p) c -> p k c", p=P)
                                         ).then_inc(extra_in[j], 16)

            def last_chunk():
                for i in range(LAST_RING):
                    piece = Piece(LAST0 + i)
                    load(piece, out_parts(w_raw[:, piece.slot, :], i if i < EXTRA_FIRST else i + EXTRAS,
                                          LAST_C * SEQ))
                residual(LAST_C)

            for i, (t, cols) in enumerate(X_PARTS):
                if i == TOK - 1:
                    sp.dma_start(cst[:, :], consts[:, :]).then_inc(cst_in, 16)
                sp.dma_start(x_tok[:, t, cols], x[0, t * P:(t + 1) * P, cols]).then_inc(x_in[i], 16)
            a_head(0, range(1))
            with nc.allow_non_contiguous_dma("gains by partition"):
                sp.dma_start(g_in, norm_g[0, :].rearrange("(t p) -> p t", p=P)).then_inc(g_in_in, 16)
            a_head(0, range(1, 2))
            with nc.allow_non_contiguous_dma("gains by partition"):
                for dst, src in ((g_q, q_norm_g), (g_kv, kv_norm_g), (g_sub_raw, a_subln_g)):
                    sp.dma_start(dst, src[0, :].rearrange("(t p) -> p t", p=P)).then_inc(gains_in, 16)
            a_head(0, range(2, SLOTS))
            sp.dma_start(pos_i[:, :], positions.broadcast_to([P, SEQ])).then_inc(pos_in, 16)
            with nc.allow_non_contiguous_dma("positions by partition"):
                sp.dma_start(pos_qi[:, :], positions[0, :].rearrange("(t p) -> p t", p=P)).then_inc(pos_in, 16)
            for i, src in enumerate((lam_q1, lam_k1, lam_q2, lam_k2)):
                sp.dma_start(lam_in[:, i, :], src.broadcast_to([P, A_DIM])).then_inc(lambdas_in, 16)
            a_head(0, range(SLOTS, A_STEPS))
            with sp.Fori(1, HEADS) as h:
                a_head(h)
            for b in range(2 * LT):
                for s in range(2):
                    block_piece(Piece(C0 + 2 * b + s), w_in, 8 * s, CQ + b * P)
            for s in range(2):
                piece = Piece(C0 + 4 * LT + s)
                raw = w_raw[:, piece.slot, :].rearrange("p (k c) -> p k c", k=8)
                load(piece, [(raw[:, :, j * B_ROPE:(j + 1) * B_ROPE], rows(w_in, 8 * s, 8, KR, B_ROPE))
                             for j in range(2)])
            for s in range(2):
                block_piece(Piece(C0 + 4 * LT + 2 + s), w_in, 8 * s, BG)
            def b_head(h, odd):
                for s in range(2):
                    block_piece(Piece(B0 - 2 + s, h, B_STEPS), w_in, 8 * s, h * P + BG)
                up_pieces(h, odd)

            up_pieces(0, False)
            with sp.Fori(0, HEADS // 2 - 1) as i:
                b_head(i * 2 + 1, True)
                b_head(i * 2 + 2, False)
            b_head(HEADS - 1, True)
            with sp.Fori(0, KT // 2) as i:
                merge_blocks(i)
            out_chunk(0)
            with sp.Fori(1, LAST_C) as c:
                out_chunk(c)
            last_chunk()
            for t in range(TOK):
                for ready, n, cols in FINAL_STORES:
                    sp.wait_ge((scaled_a, scaled_v)[ready], t * (1, 2)[ready] + n)
                    sp.dma_start(out[0, t * P:(t + 1) * P, cols], x_tok[:, t, cols]).then_inc(stored, 16)
            sp.wait_ge(stored, 16 * TOK * len(FINAL_STORES))

        @block.gpsimd
        def _(pool):
            pool.memset(ones, 1.0).then_inc(ones_set, 1)
            pool.memset(mhalf, -0.5).then_inc(ones_set, 1)
            pool.memset(half_pi, math.pi / 2).then_inc(ones_set, 1)
            pool.wait_ge(ones_set, 3)

            def rsqrt(dst, src, ready, n, done):
                pool.wait_ge(ready, n)
                pool.tensor_tensor(dst, src, mhalf[:, 0:src.shape[1]], ALU.pow).then_inc(done, 1)

            for t in range(TOK):
                rsqrt(x_rstd[:, t:t + 1], x_var[:, t:t + 1], x_var_ready, t + 1, x_rstd_ready)

            def halve(h, t):
                pool.wait_ge(max_taken, tile_no(h, t))
                pool.nop(nofuse=True)
                pool.tensor_scalar(dist[:, t, :], dist[:, t, :], SLOPE_RATIO, 1.0, ALU.mult, ALU.mult
                                   ).then_inc(dist_halved, 1)

            for t in range(3):
                halve(0, t)
            with pool.Fori(1, HEADS) as h:
                halve(h - 1, 3)
                rsqrt(o_rstd, o_var, o_var_ready, h, o_rstd_ready)
                for t in range(3):
                    halve(h, t)
            rsqrt(o_rstd, o_var, o_var_ready, HEADS, o_rstd_ready)
            for i in range(2):
                rsqrt(c_rstd, c_var, c_var_ready, i + 1, c_rstd_ready)
            for t in range(TOK):
                rsqrt(f_rstd[:, t:t + 1], f_var[:, t:t + 1], f_var_ready, t + 1, f_rstd_ready)

        @block.scalar
        def _(act):
            def split_hi(piece, cols=2 * HALF_PIECE):
                act.wait_ge(landed[piece.slot], (piece.turn + 1) * 32)
                act.activation(w_hi[:, piece.slot, 0:cols], w_raw[:, piece.slot, 0:cols], ACT.Copy
                               ).then_inc(hi_ready, 1)

            def proj_split_hi(dst, src, piece_end, n_use, use_sem):
                act.wait_ge(used, piece_end)
                if use_sem is not None:
                    act.wait_ge(use_sem, n_use)
                act.activation(dst, src, ACT.Copy).then_inc(proj_hi, 1)

            def pt_hi(head, t, src):
                act.wait_ge(p_turned, tile_no(head, t))
                if t >= 2:
                    act.wait_ge(pv_done, head * 2 + 1)
                act.activation(pt[:, 0, :, (t % 2) * P:(t % 2 + 1) * P],
                               src[:, :].rearrange("p (k c) -> p k c", k=TOK), ACT.Copy).then_inc(pt_hi_ready, 1)

            def exp_a(head, t):
                act.wait_ge(bias_ready, tile_no(head, t))
                for m in range(2):
                    b = 2 * (t % 2) + m
                    last = act.activation(e[:, t % 2, m, :], e[:, t % 2, m, :], ACT.Exp, bias=nm[:, b:b + 1],
                                          scale=A_SCALE, accum_out=sums[:, b:b + 1])
                last.then_inc(exp_done, 1)

            def exp_b(head, t, first):
                act.wait_ge(bias_ready, tile_no(head, t))
                if not first or t >= 2:
                    act.wait_ge(p_turned, tile_no(head, t) - 2)
                act.activation(e_b[:, t % 2, :], SC[t][:, :], ACT.Exp, bias=nm[:, t:t + 1], scale=B_SCALE,
                               accum_out=sums[:, t:t + 1]).then_inc(exp_done, 1)

            def gate(head, piece_end, bank_, first):
                act.wait_ge(used, piece_end)
                if not first:
                    act.wait_ge(silu_done, head)
                act.activation(eg[:, :], bank_[:, :], ACT.Exp, scale=-1.0).then_inc(gate_exp, 1)

            def v_hi(head, src):
                act.wait_ge(v_turned, head + 1)
                act.activation(v_hl[:, 0, :, :], src[:, :].rearrange("p (t c) -> p t c", t=TOK), ACT.Copy
                               ).then_inc(v_hi_ready, 1)

            def rope_tables():
                act.wait_ge(angle_ready, 1)
                act.activation(sin_t[:, :], cos_t[:, :], ACT.Sin).then_inc(trig_ready, 1)
                act.activation(eg[:, :], cos_t[:, :], ACT.Abs).then_inc(a_chain, 1)
                act.wait_ge(a_chain, 1)
                act.activation(cos_t[:, :], eg[:, :], ACT.Sin, scale=-1.0, bias=half_pi).then_inc(trig_ready, 1)

            act.wait_ge(ones_set, 3)
            for i, (t, cols) in enumerate(X_PARTS):
                act.wait_ge(x_in[i], 16)
                if i:
                    act.wait_ge(x_ss_ready, i)
                act.activation(square_junk[:, cols], x_tok[:, t, cols], ACT.Square,
                               accum_out=x_half_ss if i == TOK - 1 else x_ss[:, t:t + 1]).then_inc(x_ss_ready, 1)
            split_hi(Piece(0))
            act.wait_ge(g_in_in, 16)
            for k in range(KT):
                if k in EARLY_SPLIT:
                    split_hi(Piece(EARLY_SPLIT[k]))
                act.wait_ge(x_turned, k + 1)
                act.activation(h_hi[:, k, :], bank[2 + k % X_AHEAD][:, :], ACT.Copy, scale=g_in[:, k:k + 1]
                               ).then_inc(h_hi_ready, 1)
            act.wait_ge(gains_in, 16 * 3)

            def a_step(s, h, cur, prev, first=False):
                if s == 0 and prev:
                    pt_hi(h - 1, 1, TR)
                    exp_a(h - 1, 3)
                    gate(h - 1, (h - 1) * A_STEPS + 8, ACC[1], first)
                if s == 1 and prev:
                    pt_hi(h - 1, 2, TR)
                if s == 2 and prev:
                    pt_hi(h - 1, 3, TR)
                if s == 2 and cur:
                    act.wait_ge(used, h * A_STEPS + 2)
                    if prev:
                        act.wait_ge(scored, tile_no(h, 0) - 1)
                    for m, own in enumerate((LOW, HIGH)):
                        last = act.activation(qa[own, m, :], ACC[0][own, :], ACT.Copy)
                    last.then_inc(proj_hi, 1)
                if s == 3 and prev:
                    act.wait_ge(pv_done, h * 2)
                    act.activation(vT[:, :], OB[:, :], ACT.Square).then_inc(o_squared, 1)
                if s == 4 and cur:
                    act.wait_ge(used, h * A_STEPS + 4)
                    if prev:
                        act.wait_ge(scored, tile_no(h, 0) - 1)
                    for m, own in enumerate((LOW, HIGH)):
                        for half in (LOW, HIGH):
                            last = act.activation(ka[half, m, :], ACC[1][own, :], ACT.Copy)
                    last.then_inc(proj_hi, 1)
                if s == 5 and cur:
                    exp_a(h, 0)
                if s == 6 and cur:
                    exp_a(h, 1)
                if s == 7 and cur:
                    pt_hi(h, 0, TR)
                    v_hi(h, OB)
                    exp_a(h, 2)

            for s in range(A_STEPS):
                if s >= AHEAD:
                    split_hi(Piece(s + AHEAD))
                if s == 0:
                    act.wait_ge(lam_sum, 2)
                    act.activation(lam_e, lam_s, ACT.Exp).then_inc(lam_exp, 1)
                a_step(s, 0, True, False)
            for s in range(A_STEPS):
                split_hi(Piece(A_STEPS + s + AHEAD))
                a_step(s, 1, True, True, True)
            with act.Fori(2, HEADS) as h:
                for s in range(A_STEPS):
                    split_hi(Piece(s + AHEAD, h, A_STEPS))
                    a_step(s, h, True, True)

            def c_hi_of(i):
                act.wait_ge(c_scaled, i + 1)
                act.activation(c_hi[:, i, :], c_raw[:, i, :], ACT.Copy).then_inc(c_hi_ready, 1)

            def rope_shift(i, src):
                if not isinstance(i, int) or i > 0:
                    act.wait_ge(rope_done, i)
                for q in range(4):
                    d = (q ^ 1) * 32
                    last = act.activation(rope_sw[d:d + 32, :], src[q * 32:q * 32 + 32, :], ACT.Copy)
                last.then_inc(rope_shifted, 1)

            for s in range(C_STEPS):
                split_hi(Piece(C0 + s + AHEAD))
                if s < 6:
                    a_step(s, HEADS, False, True)
                if s == 9:
                    rope_tables()
                b = s // 2 - 1
                if s % 2 == 0 and 0 <= b < 2 * LT:
                    act.wait_ge(acc_read, HEADS * 4 + b + 1)
                    j, k = b // LT, b % LT
                    if k == 0 and j:
                        act.wait_ge(c_summed, j)
                    if k > 1:
                        act.wait_ge(c_added, j * (LT - 1) + k - 1)
                    act.activation((c_sq_tile if k else c_sq)[:, :], c_raw[:, b, :], ACT.Square
                                   ).then_inc(c_squared, 1)
                if s in C_NORM_AT:
                    for i in range(2):
                        c_hi_of(2 * C_NORM_AT.index(s) + i)
                if s == 18:
                    act.wait_ge(used, C0 + 18)
                    rope_shift(0, ACC[0])
                if s == 19:
                    act.wait_ge(rope_done, 1)
                    act.activation(kr_hi[:, :], rope_in[:, :], ACT.Copy).then_inc(rope_hi, 1)

            def b_step(s, h, pair, cur, prev):
                H = h + BH
                if s == 0 and cur:
                    gate(H, h * B_STEPS + B0, ACC[1], False)
                if s == 0 and prev:
                    pt_hi(H - 1, 0, SC[0])
                    pt_hi(H - 1, 1, SC[1])
                    exp_b(H - 1, 2, False)
                    exp_b(H - 1, 3, False)
                if s == 1 and cur:
                    proj_split_hi(q_hl[:, 0, :], ACC[0][:, :], h * B_STEPS + (B0 + 1),
                                  tile_no(H, 0) - 1 if prev else 2, scored if prev else c_summed)
                if s == 1 and prev:
                    pt_hi(H - 1, 2, SC[2])
                    pt_hi(H - 1, 3, SC[3])
                if s == 1 and cur:
                    if pair[1] == LOW:
                        act.wait_ge(rope_up, pair[0] + 1)
                        rope_shift(pair[0] + 1, TR)
                    act.wait_ge(k_up, h + 1)
                    act.wait_ge(scored, tile_no(H, 0) - 1)
                    act.activation(k_hl[:, 0, :], ACC[1][:, :], ACT.Copy).then_inc(proj_hi, 1)
                if s == 2 and cur:
                    act.wait_ge(rope_done, pair[0] + 2)
                    if prev:
                        act.wait_ge(scored, tile_no(H, 0) - 1)
                    act.activation(qr_hl[pair[1], :], rope_in[pair[1], :], ACT.Copy).then_inc(rope_hi, 1)
                if s == 3 and cur:
                    exp_b(H, 0, False)
                    exp_b(H, 1, False)
                    v_hi(H, TR)

            def b_head(h, pair, prev):
                for s in range(B_STEPS):
                    half = s + AHEAD == B_STEPS and pair[1] == LOW
                    split_hi(Piece(B0 + s + AHEAD, h, B_STEPS), HALF_PIECE if half else 2 * HALF_PIECE)
                    b_step(s, h, pair, True, prev)

            b_head(0, (0, LOW), False)
            with act.Fori(0, HEADS // 2 - 1) as i:
                b_head(i * 2 + 1, (i, HIGH), True)
                b_head(i * 2 + 2, (i + 1, LOW), True)
            last = HEADS - 1
            for s in range(2):
                split_hi(Piece(B0 + B_STEPS * last + s + AHEAD))
                b_step(s, last, LAST_PAIR, True, True)

            def sigmoid(i, b, branch):
                first = M0 + 6 * b + 2 * branch + 2
                act.wait_ge(used, i * M_STEPS + first)
                act.activation(sig[:, b, branch, :], bank[(0, 4)[b] + branch][:, :], ACT.Sigmoid
                               ).then_inc(sig_ready, 1)

            def merge_step(s, i):
                if s in (2, 4, 8, 10):
                    b = s // 6
                    if s % 6 == 2 and not isinstance(i, int):
                        act.wait_ge(merged_ready, i * 2 + (b - 1))
                    sigmoid(i, b, (s % 6) // 4)

            def gated_hi(head):
                act.wait_ge(head_gated, head + 1)
                dst = ga_hi[:, head, :] if head < HEADS else gb_hl[:, head - HEADS, 0, :]
                act.activation(dst, gated[:, head * SEQ:(head + 1) * SEQ], ACT.Copy).then_inc(g_hi_ready, 1)

            for s in range(M_STEPS):
                split_hi(Piece(M0 + s + AHEAD))
                if s < 2:
                    b_step(s + 2, last, LAST_PAIR, True, True)
                elif s < 5:
                    b_step(s - 2, HEADS, None, False, True)
                if s == 0:
                    act.wait_ge(used, M0)
                if s == 2:
                    act.wait_ge(scored, tile_no(2 * HEADS - 1, 3))
                    act.wait_ge(silu_done, 2 * HEADS)
                if s == 3:
                    act.wait_ge(p_turned, tile_no(2 * HEADS - 1, 3))
                if s == 4:
                    act.wait_ge(pv_done, 4 * HEADS)
                for head in GATED_AT[s]:
                    gated_hi(head)
                merge_step(s, 0)
            with act.Fori(1, KT // 2) as i:
                for s in range(M_STEPS):
                    split_hi(Piece(M0 + s + AHEAD, i, M_STEPS))
                    merge_step(s, i)

            def extra_split_hi(c, s):
                j = EXTRA_AT.index(s - 2)
                act.wait_ge(extra_in[j], c * 32)
                n = c * EXTRA_PER_CHUNK + (j - EXTRA_PER_CHUNK)
                act.activation(e_hi[:, bass.ds(n, 1), :], e_raw[:, bass.ds(n, 1), :], ACT.Copy).then_inc(extra_hi, 1)

            def merged_hi(j):
                act.wait_ge(merged_ready, j + 1)
                if j == 0:
                    act.wait_ge(used, FIN0 - 2)
                act.activation(mg_hi[:, j, :], merged[:, j * SEQ:(j + 1) * SEQ], ACT.Copy).then_inc(mg_hi_ready, 1)

            def chunk_square(c, t):
                act.wait_ge(x_added, c * TOK + (t + 1))
                if not (isinstance(c, int) and c == 0 and t == 0):
                    act.wait_ge(f_squared, c * TOK + t)
                act.activation(eg[:, :], x_tok[:, t, bass.ds(c * SEQ, SEQ)], ACT.Square,
                               accum_out=f_ss[:, bass.ds(c * TOK + t, 1)]).then_inc(f_squared, 1)

            def chunk_squares(c):
                for t in range(TOK):
                    chunk_square(c, t)

            def scale_a(t):
                act.wait_ge(f_rstd_ready, t + 1)
                act.activation(x_tok[:, t, 0:FINAL_A], x_tok[:, t, 0:FINAL_A], ACT.Copy, scale=f_rstd[:, t:t + 1]
                               ).then_inc(scaled_a, 1)

            for j in range(4):
                merged_hi(j)
            for s in range(F_STEPS):
                split_hi(Piece(FIN0 + s + AHEAD))
                for j in (4 + 2 * s, 5 + 2 * s):
                    if j < KT:
                        merged_hi(j)
            chunk_squares(0)
            with act.Fori(1, LAST_C) as c:
                for s in range(F_STEPS):
                    split_hi(Piece(FIN0 + s + AHEAD, c, F_STEPS))
                    if s - 2 in EXTRA_AT:
                        extra_split_hi(c, s)
                chunk_squares(c)
            for i in range(AHEAD, LAST_RING):
                split_hi(Piece(LAST0 + i))
            for t in range(TOK):
                chunk_square(LAST_C, t)
                scale_a(t)

        @block.vector
        def _(dve):
            chain = [0]

            def link(ins):
                chain[0] += 1
                ins.then_inc(v_chain, 1)
                dve.wait_ge(v_chain, chain[0])

            def split_lo(piece, cols=2 * HALF_PIECE):
                dve.wait_ge(hi_ready, piece.after(0))
                dve.tensor_tensor(w_lo[:, piece.slot, 0:cols], w_raw[:, piece.slot, 0:cols],
                                  w_hi[:, piece.slot, 0:cols].bitcast(F32), ALU.subtract).then_inc(lo_ready, 1)

            def proj_split_lo(dst, src, n):
                dve.wait_ge(proj_hi, n)
                dve.tensor_tensor(dst[:, 1, :], src[:, :], dst[:, 0, :].bitcast(F32), ALU.subtract
                                  ).then_inc(acc_read, 1)

            def pt_lo(head, t, src):
                dve.wait_ge(pt_hi_ready, tile_no(head, t))
                c = slice((t % 2) * P, (t % 2 + 1) * P)
                dve.tensor_tensor(pt[:, 1, :, c], src[:, :].rearrange("p (k c) -> p k c", k=TOK),
                                  pt[:, 0, :, c].bitcast(F32), ALU.subtract).then_inc(pt_lo_ready, 1)

            def max_a(head, t, first):
                n = tile_no(head, t)
                dve.wait_ge(scored, n)
                if not first:
                    dve.wait_ge(dist_halved, n - TOK)
                if not first or t >= 2:
                    dve.wait_ge(p_turned, n - 2)
                dve.nop(nofuse=True)
                for m in range(2):
                    b = 2 * (t % 2) + m
                    last = dve.tensor_tensor_reduce(out=e[:, t % 2, m, :], in0=SC[b][:, :], in1=dist[:, t, :],
                                                    scale=1.0, scalar=-3.0e38, op0=ALU.add, op1=ALU.max,
                                                    accum_out=mx[:, b:b + 1])
                last.then_inc(max_taken, 1)
                dve.wait_ge(max_taken, n)
                b = 2 * (t % 2)
                dve.tensor_scalar(nm[:, b:b + 2], mx[:, b:b + 2], -A_SCALE, None, ALU.mult).then_inc(bias_ready, 1)

            def norm_a(head, t):
                n = tile_no(head, t)
                b = 2 * (t % 2)
                dve.wait_ge(exp_done, n)
                dve.reciprocal(rs[:, b:b + 2], sums[:, b:b + 2]).then_inc(inv_ready, 1)
                dve.wait_ge(inv_ready, n)
                dve.tensor_scalar(rs_lam[:, t % 2:t % 2 + 1], rs[:, b + 1:b + 2], lam, None, ALU.mult
                                  ).then_inc(inv_lam_ready, 1)
                dve.wait_ge(inv_lam_ready, n)
                dve.tensor_scalar(e[:, t % 2, 1, :], e[:, t % 2, 1, :], rs_lam[:, t % 2:t % 2 + 1], None, ALU.mult
                                  ).then_inc(e2_scaled, 1)
                dve.wait_ge(e2_scaled, n)
                dve.scalar_tensor_tensor(e[:, t % 2, 0, :], e[:, t % 2, 0, :], rs[:, b:b + 1], e[:, t % 2, 1, :],
                                         ALU.mult, ALU.subtract).then_inc(p_ready, 1)

            def max_b(head, t):
                n = tile_no(head, t)
                dve.wait_ge(scored, n)
                dve.reduce_max(mx[:, t:t + 1], SC[t][:, :], AX_X).then_inc(max_taken, 1)
                dve.wait_ge(max_taken, n)
                dve.tensor_scalar(nm[:, t:t + 1], mx[:, t:t + 1], -B_SCALE, None, ALU.mult).then_inc(bias_ready, 1)

            def norm_b(head, t):
                n = tile_no(head, t)
                dve.wait_ge(exp_done, n)
                dve.reciprocal(rs[:, t:t + 1], sums[:, t:t + 1]).then_inc(inv_ready, 1)
                dve.wait_ge(inv_ready, n)
                dve.tensor_scalar(e_b[:, t % 2, :], e_b[:, t % 2, :], rs[:, t:t + 1], None, ALU.mult
                                  ).then_inc(p_ready, 1)

            def gate_of(head):
                return gated[:, bass.ds(head * SEQ, SEQ)]

            def gate_copy(head, src):
                dve.wait_ge(gate_exp, head + 1)
                dve.tensor_copy(gate_of(head), src[:, :]).then_inc(acc_read, 1)

            def silu_half(head, half):
                if half == 0:
                    dve.wait_ge(gate_exp, head + 1)
                    dve.tensor_scalar(eg[:, :], eg[:, :], 1.0, None, ALU.add).then_inc(silu_add, 1)
                    dve.wait_ge(silu_add, head + 1)
                c = slice(half * (SEQ // 2), (half + 1) * (SEQ // 2))
                dve.reciprocal(eg[:, c], eg[:, c]).then_inc(silu_inv, 1)

            def silu_mult(head, n_copy):
                dve.wait_ge(silu_inv, head * 2 + 2)
                dve.wait_ge(acc_read, n_copy)
                dve.tensor_tensor(gate_of(head), gate_of(head), eg[:, :], ALU.mult).then_inc(silu_done, 1)

            def v_lo(head, src):
                dve.wait_ge(v_hi_ready, head + 1)
                dve.tensor_tensor(v_hl[:, 1, :, :], src[:, :].rearrange("p (t c) -> p t c", t=TOK),
                                  v_hl[:, 0, :, :].bitcast(F32), ALU.subtract).then_inc(v_lo_ready, 1)

            def rope_angles():
                r, n1, n0 = cos_t, sin_t, eg
                link(dve.tensor_scalar(n0[:, :], r[:, :], 1.0 / (2.0 * math.pi), ROUND_1, ALU.mult, ALU.add))
                link(dve.tensor_scalar(n0[:, :], n0[:, :], -ROUND_1, None, ALU.add))
                link(dve.tensor_scalar(n1[:, :], n0[:, :], ROUND_2048, -ROUND_2048, ALU.add, ALU.add))
                link(dve.tensor_tensor(n0[:, :], n0[:, :], n1[:, :], ALU.subtract))
                for part_2pi in (TWO_PI_1, TWO_PI_2, TWO_PI_3):
                    for n in (n1, n0):
                        link(dve.scalar_tensor_tensor(r[:, :], n[:, :], -part_2pi, r[:, :], ALU.mult, ALU.add))
                dve.tensor_scalar(r[:, :], r[:, :], PI_DOWN, -PI_DOWN, ALU.min, ALU.max).then_inc(angle_ready, 1)

            def norm_x(t, cols):
                dve.tensor_scalar(x_tok[:, t, cols], x_tok[:, t, cols], x_rstd[:, t:t + 1], None, ALU.mult
                                  ).then_inc(x_normed, 1)

            for t in range(TOK):
                dve.wait_ge(x_ss_ready, t + 1)
                if t < TOK - 1:
                    dve.tensor_scalar(x_var[:, t:t + 1], x_ss[:, t:t + 1], 1.0 / D_MODEL, NORM_EPS, ALU.mult, ALU.add
                                      ).then_inc(x_var_ready, 1)
                else:
                    link(dve.tensor_scalar(x_half_var, x_half_ss, 1.0 / D_MODEL, NORM_EPS, ALU.mult, ALU.add))
                    dve.wait_ge(x_ss_ready, t + 2)
                    dve.scalar_tensor_tensor(x_var[:, t:t + 1], x_ss[:, t:t + 1], 1.0 / D_MODEL, x_half_var,
                                             ALU.mult, ALU.add).then_inc(x_var_ready, 1)
                dve.wait_ge(x_rstd_ready, t + 1)
                norm_x(t, slice(0, D_MODEL if t < TOK - 1 else X_AHEAD * P))
            split_lo(Piece(0))
            dve.wait_ge(g_in_in, 16)
            for k in range(KT):
                if k in EARLY_SPLIT:
                    split_lo(Piece(EARLY_SPLIT[k]))
                if k == 1:
                    norm_x(TOK - 1, slice(X_AHEAD * P, D_MODEL))
                dve.wait_ge(h_hi_ready, k + 1)
                dve.scalar_tensor_tensor(h_lo[:, k, :], bank[2 + k % X_AHEAD][:, :], g_in[:, k:k + 1],
                                         h_hi[:, k, :].bitcast(F32), ALU.mult, ALU.subtract
                                         ).then_inc(h_lo_ready, 1)
            dve.wait_ge(gains_in, 16 * 3)
            dve.wait_ge(pos_in, 32)
            dve.wait_ge(cst_in, 16)
            dve.wait_ge(lambdas_in, 16 * 4)
            link(dve.tensor_copy(pos_f[:, :], pos_i[:, :]))
            link(dve.tensor_copy(pos_q, pos_qi[:, :]))
            link(dve.tensor_scalar(cos_t[:, :], pos_f[:, :], inv_freq, None, ALU.mult))
            for i in range(2):
                dve.tensor_tensor_reduce(out=lam_in[:, 4 + i, :], in0=lam_in[:, 2 * i, :],
                                              in1=lam_in[:, 2 * i + 1, :], scale=1.0, scalar=0.0,
                                              op0=ALU.mult, op1=ALU.add, accum_out=lam_s[:, i:i + 1]).then_inc(lam_sum, 1)
            link(dve.tensor_scalar(g_sub, g_sub_raw, 1.0 - LAM_INIT, None, ALU.mult))
            for t in range(TOK):
                link(dve.tensor_scalar(dist[:, t, :], pos_f[:, :], pos_q[:, t:t + 1], SLOPE0 / A_SCALE,
                                       ALU.subtract, ALU.mult))
                link(dve.scalar_tensor_tensor(dist[:, t, :], dist[:, t, :], -1.0, dist[:, t, :], ALU.mult, ALU.min))
            dve.wait_ge(lam_exp, 1)
            link(dve.tensor_scalar(lam, lam_e[:, 0:1], lam_e[:, 1:2], LAM_INIT, ALU.subtract, ALU.add))

            def a_step(s, h, cur, prev, first=False):
                if s == 0 and prev:
                    pt_lo(h - 1, 1, TR)
                    norm_a(h - 1, 2)
                    max_a(h - 1, 3, first)
                    gate_copy(h - 1, ACC[1])
                if s == 1 and prev:
                    pt_lo(h - 1, 2, TR)
                    norm_a(h - 1, 3)
                    silu_half(h - 1, 0)
                if s == 2 and prev:
                    pt_lo(h - 1, 3, TR)
                if s == 2 and cur:
                    dve.wait_ge(proj_hi, h * 2 + 1)
                    for m, (own, other) in enumerate(((LOW, HIGH), (HIGH, LOW))):
                        last = dve.tensor_tensor(qa[other, m, :], ACC[0][own, :], qa[own, m, :].bitcast(F32),
                                                 ALU.subtract)
                    last.then_inc(acc_read, 1)
                if s == 2 and prev:
                    silu_half(h - 1, 1)
                if s == 3 and prev:
                    dve.wait_ge(o_squared, h)
                    if not first:
                        dve.wait_ge(head_gated, h - 1)
                    dve.tensor_copy(oT[:, :], OB[:, :]).then_inc(o_copied, 1)
                    silu_mult(h - 1, h * 4)
                if s == 4 and cur:
                    dve.wait_ge(proj_hi, h * 2 + 2)
                    for m, own in enumerate((LOW, HIGH)):
                        last = dve.tensor_tensor(ka_lo[own, :], ACC[1][own, :], ka[own, m, :].bitcast(F32),
                                                 ALU.subtract)
                    last.then_inc(acc_read, 1)
                if s == 4 and prev:
                    dve.wait_ge(o_summed, h)
                    dve.tensor_scalar(o_var, TR[:, 0:TOK], 1.0 / P, SUBLN_EPS, ALU.mult, ALU.add
                                      ).then_inc(o_var_ready, 1)
                if s == 5 and cur:
                    max_a(h, 0, not prev)
                if s == 5 and prev:
                    dve.wait_ge(o_spread, h)
                    dve.wait_ge(o_copied, h)
                    dve.scalar_tensor_tensor(oT[:, :], TR[:, :], g_sub, oT[:, :], ALU.mult, ALU.mult
                                             ).then_inc(o_normed, 1)
                    dve.wait_ge(o_normed, h)
                    dve.wait_ge(silu_done, h)
                    dve.tensor_tensor(gate_of(h - 1), gate_of(h - 1), oT[:, :], ALU.mult).then_inc(head_gated, 1)
                if s == 6 and cur:
                    dve.wait_ge(used, h * A_STEPS + 6)
                    if prev:
                        dve.wait_ge(o_summed, h)
                    dve.tensor_copy(vT[:, :], ACC[0][:, :]).then_inc(acc_read, 1)
                    norm_a(h, 0)
                    max_a(h, 1, not prev)
                if s == 7 and cur:
                    pt_lo(h, 0, TR)
                    norm_a(h, 1)
                    max_a(h, 2, not prev)
                    v_lo(h, OB)

            for s in range(A_STEPS):
                if s >= AHEAD:
                    split_lo(Piece(s + AHEAD))
                a_step(s, 0, True, False)
            for s in range(A_STEPS):
                split_lo(Piece(A_STEPS + s + AHEAD))
                a_step(s, 1, True, True, True)
            with dve.Fori(2, HEADS) as h:
                for s in range(A_STEPS):
                    split_lo(Piece(s + AHEAD, h, A_STEPS))
                    a_step(s, h, True, True)

            def c_norm(i):
                j = i // LT
                dve.wait_ge(c_spread, j + 1)
                dve.wait_ge(acc_read, HEADS * 4 + i + 1)
                g = (g_q, g_kv)[j][:, i % LT:i % LT + 1]
                dve.scalar_tensor_tensor(c_raw[:, i, :], c_raw[:, i, :], g, SC[2 * j + 1][:, :],
                                         ALU.mult, ALU.mult).then_inc(c_scaled, 1)

            def c_lo_of(i):
                dve.wait_ge(c_hi_ready, i + 1)
                dve.tensor_tensor(c_lo[:, i, :], c_raw[:, i, :], c_hi[:, i, :].bitcast(F32), ALU.subtract
                                  ).then_inc(c_lo_ready, 1)

            def rotate(i, src, read=None):
                dve.wait_ge(rope_shifted, i + 1)
                if not isinstance(i, int) or i > 0:
                    dve.wait_ge(rope_lo, i * 2 - 1)
                dve.tensor_tensor(rope_in[:, :], src[:, :], cos_t[:, :], ALU.mult).then_inc(read or rope_cos, 1)
                dve.tensor_tensor(rope_sw[:, :], rope_sw[:, :], sin_t[:, :], ALU.mult).then_inc(rope_sin, 1)
                dve.wait_ge(rope_sin, i + 1)
                if read is None:
                    dve.wait_ge(rope_cos, i)
                dve.tensor_tensor(rope_in[:, :], rope_in[:, :], rope_sw[:, :], ALU.add).then_inc(rope_done, 1)

            for s in range(C_STEPS):
                split_lo(Piece(C0 + s + AHEAD))
                if s < 6:
                    a_step(s, HEADS, False, True)
                if s == 7:
                    rope_angles()
                if s == 12:
                    dve.wait_ge(trig_ready, 2)
                    link(dve.tensor_scalar(sin_t[:, :], sin_t[:, :], rope_sign, None, ALU.mult))
                b = s // 2 - 1
                if s % 2 == 0 and 0 <= b < 2 * LT:
                    dve.wait_ge(used, C0 + s)
                    if b == LT:
                        dve.wait_ge(dist_halved, HEADS * TOK - 1)
                    dve.tensor_copy(c_raw[:, b, :], ACC[b % 2][:, :]).then_inc(acc_read, 1)
                    j, k = b // LT, b % LT
                    if k:
                        dve.wait_ge(c_squared, b + 1)
                        if k > 1:
                            dve.wait_ge(c_added, j * (LT - 1) + k - 1)
                        dve.tensor_tensor(c_sq[:, :], c_sq[:, :], c_sq_tile[:, :], ALU.add).then_inc(c_added, 1)
                if s - 1 in C_SUMS_AT:
                    j = C_SUMS_AT.index(s - 1)
                    dve.wait_ge(c_summed, j + 1)
                    dve.tensor_scalar(c_var, SC[2 * j][:, 0:TOK], 1.0 / LORA, NORM_EPS, ALU.mult, ALU.add
                                      ).then_inc(c_var_ready, 1)
                if s in C_NORM_AT:
                    i = 2 * C_NORM_AT.index(s)
                    c_norm(i)
                    c_norm(i + 1)
                    c_lo_of(i)
                    c_lo_of(i + 1)
                if s == 18:
                    rotate(0, ACC[0], acc_read)
                if s == 19:
                    dve.wait_ge(rope_hi, 1)
                    dve.tensor_tensor(kr_lo[:, :], rope_in[:, :], kr_hi[:, :].bitcast(F32), ALU.subtract
                                      ).then_inc(rope_lo, 1)

            G0 = HEADS * 4 + 10

            def b_step(s, h, pair, cur, prev):
                H = h + BH
                if s == 0 and cur:
                    gate_copy(H, ACC[1])
                if s == 0 and prev:
                    max_b(H - 1, 2)
                    pt_lo(H - 1, 0, SC[0])
                    pt_lo(H - 1, 1, SC[1])
                    max_b(H - 1, 3)
                    norm_b(H - 1, 2)
                    norm_b(H - 1, 3)
                if s == 1 and cur:
                    proj_split_lo(q_hl, ACC[0], H * 2 + 1)
                if s == 1 and prev:
                    pt_lo(H - 1, 2, SC[2])
                    pt_lo(H - 1, 3, SC[3])
                if s == 1 and cur:
                    if pair[1] == LOW:
                        rotate(pair[0] + 1, TR)
                    proj_split_lo(k_hl, ACC[1], H * 2 + 2)
                if s == 2 and cur:
                    dve.wait_ge(used, h * B_STEPS + (B0 + 2))
                    if prev:
                        dve.wait_ge(v_turned, H)
                    dve.tensor_copy(vT[:, :], ACC[0][:, :]).then_inc(acc_read, 1)
                    dve.wait_ge(rope_hi, h + 2)
                    own, other = pair[1], HIGH if pair[1] == LOW else LOW
                    dve.tensor_tensor(qr_hl[other, :], rope_in[own, :], qr_hl[own, :].bitcast(F32), ALU.subtract
                                      ).then_inc(rope_lo, 1)
                    silu_half(H, 0)
                if s == 2 and prev:
                    dve.wait_ge(pv_done, H * 2)
                    dve.wait_ge(silu_done, H)
                    dve.tensor_tensor(gate_of(H - 1), OB[:, :], gate_of(H - 1), ALU.mult).then_inc(head_gated, 1)
                if s == 3 and cur:
                    max_b(H, 0)
                    max_b(H, 1)
                    v_lo(H, TR)
                    norm_b(H, 0)
                    norm_b(H, 1)
                    silu_half(H, 1)
                    silu_mult(H, h * 4 + G0)

            def b_head(h, pair, prev):
                for s in range(B_STEPS):
                    half = s + AHEAD == B_STEPS and pair[1] == LOW
                    split_lo(Piece(B0 + s + AHEAD, h, B_STEPS), HALF_PIECE if half else 2 * HALF_PIECE)
                    b_step(s, h, pair, True, prev)

            b_head(0, (0, LOW), False)
            with dve.Fori(0, HEADS // 2 - 1) as i:
                b_head(i * 2 + 1, (i, HIGH), True)
                b_head(i * 2 + 2, (i + 1, LOW), True)
            last = HEADS - 1
            for s in range(2):
                split_lo(Piece(B0 + B_STEPS * last + s + AHEAD))
                b_step(s, last, LAST_PAIR, True, True)

            def gated_lo(head):
                dve.wait_ge(g_hi_ready, GATED_ORDER.index(head) + 1)
                hi, lo = ((ga_hi[:, head, :], ga_lo[:, head, :]) if head < HEADS else
                          (gb_hl[:, head - HEADS, 0, :], gb_hl[:, head - HEADS, 1, :]))
                dve.tensor_tensor(lo, gated[:, head * SEQ:(head + 1) * SEQ], hi.bitcast(F32), ALU.subtract
                                  ).then_inc(g_lo_ready, 1)

            def branch_a(i, b):
                dve.wait_ge(used, i * M_STEPS + (M0 + 6 * b + 5))
                dve.wait_ge(sig_ready, i * 4 + (2 * b + 1))
                dve.tensor_tensor(part[:, 0, :], bank[4 * b + 2][:, :], sig[:, b, 0, :], ALU.mult).then_inc(part_a, 1)

            def branch_b(i, b):
                n = i * 2 + (b + 1)
                dve.wait_ge(used, i * M_STEPS + (M0 + 6 * b + 6))
                dve.wait_ge(sig_ready, i * 4 + (2 * b + 2))
                dve.tensor_tensor(part[:, 1, :], bank[4 * b + 3][:, :], sig[:, b, 1, :], ALU.mult).then_inc(part_b, 1)
                dve.wait_ge(part_a, n)
                dve.wait_ge(part_b, n)
                dve.tensor_tensor(merged[:, bass.ds(i * (2 * SEQ) + b * SEQ, SEQ)], part[:, 0, :], part[:, 1, :],
                                  ALU.add).then_inc(merged_ready, 1)

            def merge_step(s, i, prev):
                if s == 0 and prev:
                    branch_b(i - 1, 1)
                if s == 5:
                    if prev:
                        dve.wait_ge(merged_ready, i * 2)
                    branch_a(i, 0)
                if s == 6:
                    branch_b(i, 0)
                if s == 11:
                    dve.wait_ge(merged_ready, i * 2 + 1)
                    branch_a(i, 1)

            for s in range(M_STEPS):
                split_lo(Piece(M0 + s + AHEAD))
                if s < 2:
                    b_step(s + 2, last, LAST_PAIR, True, True)
                elif s < 5:
                    b_step(s - 2, HEADS, None, False, True)
                for head in GATED_AT[s]:
                    gated_lo(head)
                merge_step(s, 0, False)
            with dve.Fori(1, KT // 2) as i:
                for s in range(M_STEPS):
                    split_lo(Piece(M0 + s + AHEAD, i, M_STEPS))
                    merge_step(s, i, True)

            def extra_split_lo(c, s):
                n = c * EXTRA_PER_CHUNK + (EXTRA_AT.index(s - 2) - EXTRA_PER_CHUNK)
                dve.wait_ge(extra_hi, n + 1)
                dve.tensor_tensor(e_lo[:, bass.ds(n, 1), :], e_raw[:, bass.ds(n, 1), :],
                                  e_hi[:, bass.ds(n, 1), :].bitcast(F32), ALU.subtract).then_inc(extra_lo, 1)

            def merged_lo(j):
                dve.wait_ge(mg_hi_ready, j + 1)
                dve.tensor_tensor(mg_lo[:, j, :], merged[:, j * SEQ:(j + 1) * SEQ], mg_hi[:, j, :].bitcast(F32),
                                  ALU.subtract).then_inc(mg_lo_ready, 1)

            def add_x(c, t):
                if t < TOK - 1 or (isinstance(c, int) and c == LAST_C):
                    dve.wait_ge(chunk_done, c * (TOK - 1) + (t + 1))
                else:
                    dve.wait_ge(used, c * F_STEPS + (FIN0 + F_STEPS))
                dve.wait_ge(x_again, c * 16 + 16)
                xt = x_tok[:, t, bass.ds(c * SEQ, SEQ)]
                dve.tensor_tensor(xt, bank[t][:, :], xt, ALU.add).then_inc(x_added, 1)

            def add_chunk(c):
                for t in range(TOK):
                    add_x(c, t)
                for t in range(TOK):
                    dve.wait_ge(f_squared, c * TOK + (t + 1))
                    xt = x_tok[:, t, bass.ds(c * SEQ, SEQ)]
                    dve.tensor_tensor(xt, xt, fg[:, bass.ds(c * SEQ, SEQ)], ALU.mult).then_inc(gained, 1)

            for j in range(4):
                merged_lo(j)
            branch_b(KT // 2 - 1, 1)
            for s in range(F_STEPS):
                split_lo(Piece(FIN0 + s + AHEAD))
                for j in (4 + 2 * s, 5 + 2 * s):
                    if j < KT:
                        merged_lo(j)
            dve.wait_ge(fg_in, 16)
            add_chunk(0)
            with dve.Fori(1, LAST_C) as c:
                for s in range(F_STEPS):
                    split_lo(Piece(FIN0 + s + AHEAD, c, F_STEPS))
                    if s - 2 in EXTRA_AT:
                        extra_split_lo(c, s)
                add_chunk(c)
            for i in range(AHEAD, LAST_RING):
                split_lo(Piece(LAST0 + i))
            last_c = slice(LAST_C * SEQ, D_MODEL)

            def variance(t):
                dve.wait_ge(f_squared, LAST_C * TOK + t + 1)
                dve.tensor_reduce(f_sum[:, t:t + 1], f_ss.rearrange("p (c t) -> p t c", t=TOK)[:, t:t + 1, :],
                                  axis=AX_X, op=ALU.add).then_inc(f_sum_ready, 1)
                dve.wait_ge(f_sum_ready, t + 1)
                dve.tensor_scalar(f_var[:, t:t + 1], f_sum[:, t:t + 1], 1.0 / D_MODEL, NORM_EPS, ALU.mult, ALU.add
                                  ).then_inc(f_var_ready, 1)

            def scale_v(t):
                dve.wait_ge(gained, TOK * LAST_C)
                dve.wait_ge(f_rstd_ready, t + 1)
                dve.scalar_tensor_tensor(x_tok[:, t, last_c], x_tok[:, t, last_c], f_rstd[:, t:t + 1],
                                         fg[:, last_c], ALU.mult, ALU.mult).then_inc(scaled_v, 1)
                dve.tensor_scalar(x_tok[:, t, FINAL_A:LAST_C * SEQ], x_tok[:, t, FINAL_A:LAST_C * SEQ],
                                  f_rstd[:, t:t + 1], None, ALU.mult).then_inc(scaled_v, 1)

            for t in range(TOK):
                add_x(LAST_C, t)
                variance(t)
                scale_v(t)

        @block.tensor
        def _(pe):
            def three(dst, lhs_hi, lhs_lo, rhs_hi, rhs_lo, start, stop):
                pe.matmul(dst, lhs_hi, rhs_hi, start=start, stop=False)
                pe.matmul(dst, lhs_hi, rhs_lo, start=False, stop=False)
                return pe.matmul(dst, lhs_lo, rhs_hi, start=False, stop=stop)

            def tile(piece, c0, width=P):
                return w_hi[:, piece.slot, c0:c0 + width], w_lo[:, piece.slot, c0:c0 + width]

            def project(piece, dst, half, halves, rhs_hi, rhs_lo, k0, h_waits=False):
                pe.wait_ge(lo_ready, piece.after(0))
                for k in range(8):
                    if h_waits:
                        pe.wait_ge(h_lo_ready, k0 + k + 1)
                    hi, lo = tile(piece, k * P)
                    last = three(dst[:, :], hi, lo, rhs_hi[:, k0 + k, :], rhs_lo[:, k0 + k, :],
                                 half == 0 and k == 0, half == halves - 1 and k == 7)
                    if h_waits and k0 + k + X_AHEAD < KT:
                        turn_x(k0 + k + X_AHEAD)
                last.then_inc(used, 1)

            def scores_a(head, t, first):
                if t == 0:
                    pe.wait_ge(acc_read, head * 4 + 2)
                if not first or t >= 2:
                    pe.wait_ge(max_taken, tile_no(head, t) - 2)
                a, b = SC[2 * (t % 2)], SC[2 * (t % 2) + 1]
                q = slice(t * P, (t + 1) * P)
                for m, dst in enumerate((a, b)):
                    pe.matmul(dst[:, :], qa[:, m, q], ka[:, m, :], start=True, stop=False)
                for m, (dst, own) in enumerate(((a, LOW), (b, HIGH))):
                    last = pe.matmul(dst[:, :], qa[own, m, q], ka_lo[own, :], start=False, stop=True)
                last.then_inc(scored, 1)

            def scores_b(h, t, own, prev):
                H = h + BH
                if t == 0:
                    pe.wait_ge(acc_read, h * 4 + (HEADS * 4 + 12))
                    pe.wait_ge(rope_lo, h + 2)
                if prev:
                    pe.wait_ge(pt_lo_ready, tile_no(H, t) - TOK)
                elif t == 0:
                    pe.wait_ge(c_lo_ready, 2 * LT)
                q = slice(t * P, (t + 1) * P)
                dst = SC[t][:, :]
                pe.matmul(dst, q_hl[:, 0, q], k_hl[:, 0, :], start=True, stop=False)
                pe.matmul(dst, q_hl[:, 0, q], k_hl[:, 1, :], start=False, stop=False)
                pe.matmul(dst, q_hl[:, 1, q], k_hl[:, 0, :], start=False, stop=False)
                pe.matmul(dst, qr_hl[:, q], kr_hi[:, :], start=False, stop=False)
                pe.matmul(dst, qr_hl[own, q], kr_lo[own, :], start=False, stop=True).then_inc(scored, 1)

            def turn(src, dst, done):
                for k in range(TOK):
                    last = pe.transpose(dst[:, k * P:(k + 1) * P], src[:, k * P:(k + 1) * P], ident)
                last.then_inc(done, 1)

            def turn_p_a(head, t, first):
                pe.wait_ge(p_ready, tile_no(head, t))
                if t:
                    pe.wait_ge(pt_lo_ready, tile_no(head, t) - 1)
                elif not first:
                    pe.wait_ge(o_normed, head)
                turn(e[:, t % 2, 0, :], TR, p_turned)

            def turn_p_b(head, t):
                pe.wait_ge(p_ready, tile_no(head, t))
                turn(e_b[:, t % 2, :], SC[t], p_turned)

            def pv(head, pair):
                pe.wait_ge(pt_lo_ready, tile_no(head, 2 * pair + 1))
                pe.wait_ge(v_lo_ready, head + 1)
                for k in range(TOK):
                    last = three(OB[:, pair * 2 * P:(pair + 1) * 2 * P], v_hl[:, 0, k, :], v_hl[:, 1, k, :],
                                 pt[:, 0, k, :], pt[:, 1, k, :], k == 0, k == TOK - 1)
                last.then_inc(pv_done, 1)

            def column_sums(sq, dst, done):
                for t in range(TOK):
                    last = pe.matmul(dst[:, t:t + 1], sq[:, t * P:(t + 1) * P], ones, start=True, stop=True)
                last.then_inc(done, 1)

            def spread(col, dst, done):
                for t in range(TOK):
                    last = pe.matmul(dst[:, t * P:(t + 1) * P], col[:, t:t + 1].broadcast_to([P, P]), ident,
                                     start=True, stop=True)
                last.then_inc(done, 1)

            pe.wait_ge(cst_in, 16)
            pe.wait_ge(ones_set, 3)
            for t in range(TOK):
                pe.wait_ge(x_normed, t + 1)
                for k in range(X_AHEAD):
                    last = pe.transpose(bank[2 + k][:, t * P:(t + 1) * P], x_tok[:, t, k * P:(k + 1) * P], ident)
                    if t == TOK - 1:
                        last.then_inc(x_turned, 1)
                for _ in range(WARM_UP.get(t, 0)):
                    pe.matmul(bank[0][:, 0:P], ident, ident, start=True, stop=True)

            def turn_x(k):
                if k == X_AHEAD:
                    pe.wait_ge(x_normed, TOK + 1)
                for t in range(TOK):
                    last = pe.transpose(bank[2 + k % X_AHEAD][:, t * P:(t + 1) * P], x_tok[:, t, k * P:(k + 1) * P],
                                        ident)
                last.then_inc(x_turned, 1)

            def a_extras(s, h, cur, prev, first=False):
                if s == 0 and prev:
                    turn_p_a(h - 1, 2, first)
                    pv(h - 1, 0)
                if s == 1 and prev:
                    turn_p_a(h - 1, 3, first)
                if s == 2 and prev:
                    pv(h - 1, 1)
                if s == 3 and prev:
                    pe.wait_ge(o_squared, h)
                    pe.wait_ge(pt_lo_ready, h * TOK)
                    column_sums(vT, TR, o_summed)
                if s == 4 and cur:
                    scores_a(h, 0, not prev)
                if s == 4 and prev:
                    pe.wait_ge(o_rstd_ready, h)
                    spread(o_rstd, TR, o_spread)
                if s == 5 and cur:
                    scores_a(h, 1, not prev)
                if s == 6 and cur:
                    pe.wait_ge(acc_read, h * 4 + 3)
                    if prev:
                        pe.wait_ge(o_copied, h)
                    turn(vT, OB, v_turned)
                    turn_p_a(h, 0, not prev)
                    scores_a(h, 2, not prev)
                if s == 7 and cur:
                    turn_p_a(h, 1, not prev)
                    scores_a(h, 3, not prev)

            def a_head(h, prev, first=False):
                for s in range(A_STEPS):
                    g = s // 2
                    if s % 2 == 0 and (prev or g >= 2):
                        pe.wait_ge(acc_read, h * 4 + (g - 1))
                    project(Piece(s, h, A_STEPS), ACC[g % 2], s % 2, 2, h_hi, h_lo, 8 * (s % 2),
                            h_waits=not prev and s < 2)
                    a_extras(s, h, True, prev, first)

            a_head(0, False)
            with pe.Fori(1, HEADS) as h:
                a_head(h, True)

            for s in range(C_STEPS):
                b = s // 2
                if s % 2 == 0:
                    pe.wait_ge(acc_read, HEADS * 4 + b - 1)
                project(Piece(C0 + s), ACC[b % 2], s % 2, 2, h_hi, h_lo, 8 * (s % 2))
                if s < 6:
                    a_extras(s, HEADS, False, True)
                if s in C_SUMS_AT:
                    j = C_SUMS_AT.index(s)
                    pe.wait_ge(max_taken, HEADS * TOK)
                    pe.wait_ge(c_added, (LT - 1) * (j + 1))
                    column_sums(c_sq, SC[2 * j], c_summed)
                if s - 1 in C_SUMS_AT:
                    j = C_SUMS_AT.index(s - 1)
                    pe.wait_ge(c_rstd_ready, j + 1)
                    spread(c_rstd, SC[2 * j + 1], c_spread)

            def up(piece, c0, dst, which, stride=2 * P):
                for k in range(LT):
                    hi, lo = tile(piece, k * stride + c0)
                    last = three(dst[:, :], hi, lo, c_hi[:, which * LT + k, :], c_lo[:, which * LT + k, :],
                                 k == 0, k == LT - 1)
                return last

            def b_extras(s, h, pair, cur, prev):
                H = h + BH
                if s == 0 and prev:
                    pe.wait_ge(head_gated, H - 1)
                    pv(H - 1, 0)
                    turn_p_b(H - 1, 2)
                    turn_p_b(H - 1, 3)
                if s == 1 and prev:
                    pv(H - 1, 1)
                if s == 2 and cur:
                    scores_b(h, 0, pair[1], prev)
                    scores_b(h, 1, pair[1], prev)
                    pe.wait_ge(acc_read, h * 4 + (HEADS * 4 + 13))
                    if pair[1] == LOW:
                        pe.wait_ge(rope_cos, pair[0] + 1)
                    else:
                        pe.wait_ge(v_lo_ready, H)
                    turn(vT, TR, v_turned)
                if s == 3 and cur:
                    scores_b(h, 2, pair[1], prev)
                    scores_b(h, 3, pair[1], prev)
                    turn_p_b(H, 0)
                    turn_p_b(H, 1)

            def b_up(h, pair, prev):
                g = h * 4 + (HEADS * 4 + 10)
                H = h + BH
                piece = Piece(B0, h, B_STEPS)
                pe.wait_ge(lo_ready, piece.after(0))
                if pair[1] == LOW:
                    if prev:
                        pe.wait_ge(v_lo_ready, H)
                    else:
                        pe.wait_ge(o_normed, HEADS)
                        pe.wait_ge(c_lo_ready, LT)
                    up(piece, P, TR, 0).then_inc(rope_up, 1)
                pe.wait_ge(acc_read, g - 1)
                up(piece, 0, ACC[0], 0, 2 * P if pair[1] == LOW else P).then_inc(used, 1)
                b_extras(0, h, pair, True, prev)
                piece = Piece(B0 + 1, h, B_STEPS)
                pe.wait_ge(lo_ready, piece.after(0))
                if not prev:
                    pe.wait_ge(c_lo_ready, 2 * LT)
                pe.wait_ge(acc_read, g)
                up(piece, 0, ACC[1], 1).then_inc(k_up, 1)
                pe.wait_ge(acc_read, g + 1)
                up(piece, P, ACC[0], 1).then_inc(used, 1)
                b_extras(1, h, pair, True, prev)

            def b_gate(h, pair, prev):
                for s in range(2):
                    if s == 0:
                        pe.wait_ge(acc_read, h * 4 + (HEADS * 4 + 12))
                    project(Piece(B0 + 2 + s, h, B_STEPS), ACC[1], s, 2, h_hi, h_lo, 8 * s)
                    b_extras(2 + s, h, pair, True, prev)

            b_up(0, (0, LOW), False)
            b_gate(0, (0, LOW), False)
            with pe.Fori(0, HEADS // 2 - 1) as i:
                b_up(i * 2 + 1, (i, HIGH), True)
                b_gate(i * 2 + 1, (i, HIGH), True)
                b_up(i * 2 + 2, (i + 1, LOW), True)
                b_gate(i * 2 + 2, (i + 1, LOW), True)
            last_h = HEADS - 1
            b_up(last_h, LAST_PAIR, True)

            def merge(i, tail):
                for s in range(M_STEPS):
                    b, k = s // 6, s % 6
                    piece = Piece(M0 + s, i, M_STEPS)
                    if tail:
                        if s == 0:
                            pe.wait_ge(acc_read, last_h * 4 + HEADS * 4 + 13)
                        if s == 4:
                            pe.wait_ge(g_lo_ready, HEADS)
                            pe.wait_ge(pt_lo_ready, tile_no(2 * HEADS - 1, TOK - 1))
                        if s == 5:
                            pe.wait_ge(g_lo_ready, 2 * HEADS)
                    else:
                        if k in (0, 2):
                            pe.wait_ge(sig_ready, i * 4 + (2 * b + k // 2 - 3))
                        if k == 4:
                            pe.wait_ge(part_a, i * 2 + (b - 1))
                        if k == 5:
                            pe.wait_ge(part_b, i * 2 + (b - 1))
                    if k < 4:
                        project(piece, bank[4 * b + k // 2], k % 2, 2, h_hi, h_lo, 8 * (k % 2))
                    elif k == 4:
                        project(piece, bank[4 * b + 2], 0, 1, ga_hi, ga_lo, 0)
                    else:
                        project(piece, bank[4 * b + 3], 0, 1, gb_hl[:, :, 0, :], gb_hl[:, :, 1, :], 0)
                    if tail and s < 2:
                        b_extras(s + 2, last_h, LAST_PAIR, True, True)
                    elif tail and s < 5:
                        b_extras(s - 2, HEADS, None, False, True)

            merge(0, True)
            with pe.Fori(1, KT // 2) as i:
                merge(i, False)

            def out_chunk(c, first):
                for s in range(F_STEPS):
                    piece = Piece(FIN0 + s, c, F_STEPS)
                    pe.wait_ge(lo_ready, piece.after(0))
                    if first:
                        pe.wait_ge(mg_lo_ready, 2 * s + 2)
                        if s == 0:
                            pe.wait_ge(merged_ready, KT - 1)
                    for t in range(TOK):
                        if s == 0 and not first:
                            pe.wait_ge(x_added, c * TOK + (t - (TOK - 1)))
                        for k in range(2):
                            hi, lo = tile(piece, k * SEQ, SEQ)
                            kt = 2 * s + k
                            q = slice(t * P, (t + 1) * P)
                            last = three(bank[t][:, :], mg_hi[:, kt, q], mg_lo[:, kt, q], hi, lo,
                                         kt == 0, kt == KT - 1)
                        if s == F_STEPS - 1 and t < TOK - 1:
                            last.then_inc(chunk_done, 1)
                    last.then_inc(used, 1)
                return last

            out_chunk(0, True)
            with pe.Fori(1, LAST_C) as c:
                out_chunk(c, False)

            for t in range(TOK):
                q = slice(t * P, (t + 1) * P)
                pe.wait_ge(x_added, LAST_C * TOK + t - (TOK - 1))
                for s in range(F_STEPS):
                    extra = s - EXTRA_FIRST
                    if 0 <= extra < EXTRAS:
                        hi, lo = e_hi[:, extra, :], e_lo[:, extra, :]
                        if t == 0:
                            pe.wait_ge(extra_lo, extra + 1)
                    else:
                        piece = Piece(LAST0 + (s if extra < 0 else s - EXTRAS))
                        hi, lo = tile(piece, 0, 2 * SEQ)
                        if t == 0:
                            pe.wait_ge(lo_ready, piece.after(0))
                    for k in range(2):
                        kt, w = 2 * s + k, slice(k * SEQ, (k + 1) * SEQ)
                        last = three(bank[t][:, :], mg_hi[:, kt, q], mg_lo[:, kt, q], hi[:, w], lo[:, w],
                                     kt == 0, kt == KT - 1)
                last.then_inc(chunk_done, 1)


_INS = ['x', 'positions', 'norm_g', 'w_in', 'lam_q1', 'lam_k1', 'lam_q2', 'lam_k2', 'a_subln_g', 'w_oa',
        'q_norm_g', 'w_uq', 'kv_norm_g', 'w_ukv', 'w_ob', 'w_out', 'final_g']


def kernel(**inputs):
    import numpy as _np
    import concourse.bacc as _bacc
    from concourse import mybir as _mybir
    from concourse.bass_utils import run_bass_kernel_spmd as _run

    consts = _np.zeros((P, P + 2), _np.float32)
    consts[:, 0:P] = _np.eye(P)
    half = B_ROPE // 2
    for m in range(P):
        consts[m, P] = 10000.0 ** (-(m % half) / half)
        consts[m, P + 1] = -1.0 if m % B_ROPE < half else 1.0

    nc = _bacc.Bacc("TRN2", target_bir_lowering=False, num_devices=1)
    arrays, args = {}, []
    for name, a in [(n, inputs[n]) for n in _INS] + [("consts", consts)]:
        a = _np.ascontiguousarray(a)
        arrays[f"in_{name}_dram"] = a
        args.append(nc.dram_tensor(f"in_{name}_dram", a.shape, _mybir.dt.from_np(a.dtype), kind="ExternalInput").ap())
    args.append(nc.dram_tensor("out_0_dram", (1, SEQ, D_MODEL), _mybir.dt.float32, kind="ExternalOutput").ap())
    hybrid_encoder(nc, *args)
    r = _run(nc, [arrays], core_ids=[0])
    return r.results[0]["out_0_dram"]
```
